# Optimizing a Trainium2 kernel written in Bass

```python
import jax
import jax.numpy as jnp
from jax import lax
import numpy as np

D_MODEL = 1024
BATCH = 1
SEQ = 128
DEPTH = 2
DEC_BATCH = 1
DEC_SEQ = 256
PAST_LEN = 128

GRID_W = 64
N_EVEN = (DEPTH + 1) // 2
N_ODD = DEPTH // 2
ALPHA = (2.0 * DEPTH) ** 0.25
BETA = (8.0 * DEPTH) ** -0.25
LN_EPS = 1e-5
RMS_EPS = 1e-6
ROPE_BASE = 10000.0
Q_BLOCK = 128
NEG_INF = -1e30
MLA_HEADS = 8
MLA_NOPE_DIM = 64
MLA_ROPE_DIM = 32
MLA_V_DIM = 64
MLA_Q_RANK = 256
MLA_KV_RANK = 128
RET_HEADS = 8
RET_HEAD_DIM = 64
RET_CHUNK = 128
RET_WIDTH = RET_HEADS * RET_HEAD_DIM
MLA_IN_DIM = MLA_Q_RANK + MLA_KV_RANK + MLA_ROPE_DIM
EVEN_IN_DIM = MLA_IN_DIM + 4 * RET_WIDTH
EVEN_SPLITS = (MLA_Q_RANK, MLA_Q_RANK + MLA_KV_RANK, MLA_IN_DIM, MLA_IN_DIM + RET_WIDTH,
               MLA_IN_DIM + 2 * RET_WIDTH, MLA_IN_DIM + 3 * RET_WIDTH)
EVEN_MIX_DIM = MLA_HEADS * MLA_V_DIM + RET_WIDTH
SWA_HEADS = 16
SWA_KV_HEADS = 4
SWA_GROUP = SWA_HEADS // SWA_KV_HEADS
SWA_HEAD_DIM = 64
WINDOW = 128
SWA_Q_DIM = SWA_HEADS * SWA_HEAD_DIM
SWA_KV_DIM = SWA_KV_HEADS * SWA_HEAD_DIM
SWA_IN_DIM = SWA_Q_DIM + 2 * SWA_KV_DIM
N_EXPERTS = 64
TOP_K = 8
N_GROUPS = 8
TOPK_GROUPS = 4
EXPERT_DIM = 256
SHARED_DIM = 256
ROUTED_SCALE = 2.5
EXPERT_BLOCK = 128

kernel_name = 'hybrid_mla_retention_swa_moe_diffusion_step'

def _layernorm(x, g, b):
    xf = x.astype(jnp.float32)
    mu = xf.mean(-1, keepdims=True)
    var = jnp.square(xf - mu).mean(-1, keepdims=True)
    y = (xf - mu) * lax.rsqrt(var + LN_EPS) * g.astype(jnp.float32) + b.astype(jnp.float32)
    return y.astype(x.dtype)

def _rmsnorm(x, g):
    xf = x.astype(jnp.float32)
    y = xf * lax.rsqrt(jnp.mean(xf * xf, -1, keepdims=True) + RMS_EPS) * g.astype(jnp.float32)
    return y.astype(x.dtype)

def _head_norm(x):
    xf = x.astype(jnp.float32)
    mu = xf.mean(-1, keepdims=True)
    var = jnp.square(xf - mu).mean(-1, keepdims=True)
    return ((xf - mu) * lax.rsqrt(var + LN_EPS)).astype(x.dtype)

def _modulation(cond, w, b):
    m = jax.nn.silu(cond) @ w + b
    return jnp.split(m[:, None, :], 6, axis=-1)

def _modulate(x, shift, scale):
    return x * (1.0 + scale) + shift

def _axial_rope(rows, rot_dim):
    nf = rot_dim // 4
    t = jnp.arange(rows * GRID_W)
    r = (t // GRID_W).astype(jnp.float32)
    col = (t % GRID_W).astype(jnp.float32)
    freqs = ROPE_BASE ** (-jnp.arange(nf, dtype=jnp.float32) / nf)
    ang = jnp.concatenate([r[:, None] * freqs, col[:, None] * freqs], axis=-1)
    return jnp.cos(ang), jnp.sin(ang)

def _rope_2d(x, cos, sin):
    t, r = x.shape[1], x.shape[-1]
    nf = r // 4
    xs = x.reshape(x.shape[:-1] + (2, 2, nf))
    x1, x2 = xs[..., 0, :], xs[..., 1, :]
    bshape = (1, t) + (1,) * (x.ndim - 3) + (2, nf)
    c = cos.reshape(bshape).astype(x.dtype)
    s = sin.reshape(bshape).astype(x.dtype)
    return jnp.stack([x1 * c - x2 * s, x2 * c + x1 * s], axis=-2).reshape(x.shape)

def _softmax_with_sink(s, sink):
    if sink is None:
        return jax.nn.softmax(s, axis=-1)
    col = jnp.broadcast_to(sink.astype(jnp.float32).reshape(1, s.shape[1], s.shape[2], 1, 1), s.shape[:-1] + (1,))
    return jax.nn.softmax(jnp.concatenate([s, col], axis=-1), axis=-1)[..., :-1]

def _block_attention(q, k, v, sink):
    b, t, hk, g, dq = q.shape
    nb = t // Q_BLOCK
    scale = dq ** -0.5
    qb = jnp.moveaxis(q.reshape(b, nb, Q_BLOCK, hk, g, dq), 1, 0)

    def one(qi):
        s = jnp.einsum('bqhgd,bshd->bhgqs', qi, k).astype(jnp.float32) * scale
        p = _softmax_with_sink(s, sink).astype(v.dtype)
        return jnp.einsum('bhgqs,bshd->bqhgd', p, v)

    o = lax.map(one, qb)
    return jnp.moveaxis(o, 0, 1).reshape(b, t, hk, g, v.shape[-1])

def _window_attention(q, k, v, k_ctx, v_ctx, sink):
    b, t, hk, g, dh = q.shape
    nb = t // Q_BLOCK
    band = Q_BLOCK + 2 * WINDOW
    scale = dh ** -0.5
    pad = ((0, 0), (WINDOW, WINDOW), (0, 0), (0, 0))
    kp = jnp.pad(k, pad)
    vp = jnp.pad(v, pad)

    def one(i):
        start = i * Q_BLOCK
        qi = lax.dynamic_slice_in_dim(q, start, Q_BLOCK, axis=1)
        ki = lax.dynamic_slice_in_dim(kp, start, band, axis=1)
        vi = lax.dynamic_slice_in_dim(vp, start, band, axis=1)
        qpos = start + jnp.arange(Q_BLOCK)
        kpos = start - WINDOW + jnp.arange(band)
        valid = (jnp.abs(qpos[:, None] - kpos[None, :]) <= WINDOW) & (kpos >= 0)[None, :] & (kpos < t)[None, :]
        s_band = jnp.einsum('bqhgd,bshd->bhgqs', qi, ki).astype(jnp.float32) * scale
        s_band = jnp.where(valid, s_band, NEG_INF)
        s_ctx = jnp.einsum('bqhgd,bshd->bhgqs', qi, k_ctx).astype(jnp.float32) * scale
        p = _softmax_with_sink(jnp.concatenate([s_band, s_ctx], axis=-1), sink).astype(v.dtype)
        return (jnp.einsum('bhgqs,bshd->bqhgd', p[..., :band], vi)
                + jnp.einsum('bhgqs,bshd->bqhgd', p[..., band:], v_ctx))

    o = lax.map(one, jnp.arange(nb))
    return jnp.moveaxis(o, 0, 1).reshape(b, t, hk, g, dh)

def _retention_scan(q, k, v, log_gamma, s0):
    b, t, h, _ = q.shape
    dv = v.shape[-1]
    n = t // RET_CHUNK

    def to_chunks(a):
        return a.astype(jnp.float32).reshape(b, n, RET_CHUNK, h, a.shape[-1]).transpose(1, 0, 3, 2, 4)

    idx = jnp.arange(RET_CHUNK, dtype=jnp.float32)
    diff = idx[:, None] - idx[None, :]
    inner_decay = jnp.where(diff >= 0, jnp.exp(log_gamma[:, None, None] * jnp.maximum(diff, 0.0)), 0.0)
    q_decay = jnp.exp(log_gamma[:, None] * (idx + 1.0))
    k_decay = jnp.exp(log_gamma[:, None] * (RET_CHUNK - 1.0 - idx))
    chunk_decay = jnp.exp(log_gamma * RET_CHUNK)

    def step(state, xs_):
        qi, ki, vi = xs_
        attn = jnp.einsum('bhnd,bhmd->bhnm', qi, ki) * inner_decay
        o = (jnp.einsum('bhnm,bhme->bhne', attn, vi)
             + jnp.einsum('bhnd,bhde->bhne', qi, state) * q_decay[:, :, None])
        state = state * chunk_decay[:, None, None] + jnp.einsum('bhmd,bhme->bhde', ki * k_decay[:, :, None], vi)
        return state, o

    s_fin, o = lax.scan(step, s0.astype(jnp.float32), (to_chunks(q), to_chunks(k), to_chunks(v)))
    o = o.transpose(1, 0, 3, 2, 4).reshape(b, t, h, dv)
    return o.astype(q.dtype), s_fin.astype(q.dtype)

def _even_mixer(h, w_in, q_norm, w_uq, kv_norm, w_uk, w_uv, decay_f, decay_b, gn_g, w_out, rope, ctx):
    b, t, _ = h.shape
    q_lat, kv_lat, k_pe, r_q, r_k, r_v, r_g = jnp.split(h @ w_in, EVEN_SPLITS, axis=-1)
    q = (_rmsnorm(q_lat, q_norm) @ w_uq).reshape(b, t, MLA_HEADS, MLA_NOPE_DIM + MLA_ROPE_DIM)
    q_nope, q_pe = q[..., :MLA_NOPE_DIM], q[..., MLA_NOPE_DIM:]
    ckv = _rmsnorm(kv_lat, kv_norm)
    k_pe = k_pe[:, :, None, :]
    if ctx is None:
        ckv_all, kpe_all = ckv, k_pe
        s0_f = jnp.zeros((b, RET_HEADS, RET_HEAD_DIM, RET_HEAD_DIM), jnp.float32)
        s0_b = s0_f
    else:
        ctx_ckv, ctx_kpe, s0_f, s0_b = ctx
        q_pe = _rope_2d(q_pe, *rope)
        k_pe = _rope_2d(k_pe, *rope)
        ckv_all = jnp.concatenate([ckv, ctx_ckv], axis=1)
        kpe_all = jnp.concatenate([k_pe, ctx_kpe[:, :, None, :]], axis=1)
    s = ckv_all.shape[1]
    k_nope = (ckv_all @ w_uk).reshape(b, s, MLA_HEADS, MLA_NOPE_DIM)
    v = (ckv_all @ w_uv).reshape(b, s, MLA_HEADS, MLA_V_DIM)
    k = jnp.concatenate([k_nope, jnp.broadcast_to(kpe_all, (b, s, MLA_HEADS, MLA_ROPE_DIM))], axis=-1)
    qf = jnp.concatenate([q_nope, q_pe], axis=-1)[:, :, :, None, :]
    o_mla = _block_attention(qf, k, v, None).reshape(b, t, MLA_HEADS * MLA_V_DIM)
    rq = r_q.reshape(b, t, RET_HEADS, RET_HEAD_DIM)
    rk = r_k.reshape(b, t, RET_HEADS, RET_HEAD_DIM) * (RET_HEAD_DIM ** -0.5)
    rv = r_v.reshape(b, t, RET_HEADS, RET_HEAD_DIM)
    o_f, s_f = _retention_scan(rq, rk, rv, jax.nn.log_sigmoid(decay_f.astype(jnp.float32)), s0_f)
    o_b, s_b = _retention_scan(rq[:, ::-1], rk[:, ::-1], rv[:, ::-1],
                               jax.nn.log_sigmoid(decay_b.astype(jnp.float32)), s0_b)
    o_ret = (_head_norm(o_f) + _head_norm(o_b[:, ::-1])).reshape(b, t, RET_WIDTH) * gn_g * jax.nn.silu(r_g)
    out = jnp.concatenate([o_mla, o_ret], axis=-1) @ w_out
    return out, (ckv, k_pe[:, :, 0, :], s_f, s_b)

def _odd_mixer(h, w_in, sink, w_out, rope, ctx):
    b, t, _ = h.shape
    q, k, v = jnp.split(h @ w_in, (SWA_Q_DIM, SWA_Q_DIM + SWA_KV_DIM), axis=-1)
    q = q.reshape(b, t, SWA_KV_HEADS, SWA_GROUP, SWA_HEAD_DIM)
    k = k.reshape(b, t, SWA_KV_HEADS, SWA_HEAD_DIM)
    v = v.reshape(b, t, SWA_KV_HEADS, SWA_HEAD_DIM)
    if ctx is None:
        o = _block_attention(q, k, v, sink)
    else:
        ctx_k, ctx_v = ctx
        o = _window_attention(_rope_2d(q, *rope), _rope_2d(k, *rope), v, ctx_k, ctx_v, sink)
    return o.reshape(b, t, SWA_Q_DIM) @ w_out, (k, v)

def _swiglu(x, wg, wu, wd):
    return (jax.nn.silu(x @ wg) * (x @ wu)) @ wd

def _grouped_experts(xt, idx, w, wg, wu, wd):
    n, kk = idx.shape
    d = xt.shape[-1]
    n_assign = n * kk
    n_blocks = -(-n_assign // EXPERT_BLOCK) + N_EXPERTS
    flat_e = idx.reshape(-1)
    order = jnp.argsort(flat_e)
    e_sorted = flat_e[order]
    tok = order // kk
    counts = jnp.bincount(flat_e, length=N_EXPERTS)
    padded = (counts + EXPERT_BLOCK - 1) // EXPERT_BLOCK * EXPERT_BLOCK
    pad_end = jnp.cumsum(padded)
    start = jnp.cumsum(counts) - counts
    dest = (pad_end - padded)[e_sorted] + jnp.arange(n_assign) - start[e_sorted]
    buf = jnp.zeros((n_blocks * EXPERT_BLOCK, d), xt.dtype).at[dest].set(xt[tok])
    block_e = jnp.minimum(jnp.searchsorted(pad_end, jnp.arange(n_blocks) * EXPERT_BLOCK, side='right'),
                          N_EXPERTS - 1)

    def expert_block(args):
        xb, e = args
        return _swiglu(xb, wg[e], wu[e], wd[e])

    out = lax.map(expert_block, (buf.reshape(n_blocks, EXPERT_BLOCK, d), block_e)).reshape(-1, d)
    y = out[dest] * w.reshape(-1)[order][:, None].astype(xt.dtype)
    return jax.ops.segment_sum(y, tok, num_segments=n)

def _moe(h, router, router_bias, wg, wu, wd, sg, su, sd):
    b, t, d = h.shape
    xt = h.reshape(b * t, d)
    n = xt.shape[0]
    scores = jax.nn.sigmoid((xt @ router).astype(jnp.float32))
    sel = scores + router_bias.astype(jnp.float32)
    grp = lax.top_k(sel.reshape(n, N_GROUPS, N_EXPERTS // N_GROUPS), 2)[0].sum(-1)
    _, top_g = lax.top_k(grp, TOPK_GROUPS)
    gmask = jax.nn.one_hot(top_g, N_GROUPS, dtype=jnp.float32).sum(1) > 0
    emask = jnp.repeat(gmask, N_EXPERTS // N_GROUPS, axis=1)
    _, idx = lax.top_k(jnp.where(emask, sel, NEG_INF), TOP_K)
    w = jnp.take_along_axis(scores, idx, axis=1)
    w = w / w.sum(-1, keepdims=True) * ROUTED_SCALE
    routed = _grouped_experts(xt, idx, w, wg, wu, wd)
    return (routed + _swiglu(xt, sg, su, sd)).reshape(b, t, d)

def setup_inputs(seed: int = 0) -> dict:
    key = jax.random.key(seed)
    ks = iter(jax.random.split(key, 40))

    def nrm(shape, scale):
        return jax.random.normal(next(ks), shape, jnp.float32) * scale

    base = 1.0 - 2.0 ** (-5.0 - jnp.arange(RET_HEADS, dtype=jnp.float32))
    base_logit = jnp.log(base) - jnp.log1p(-base)
    d = D_MODEL
    return {
        'x_prompt': nrm((BATCH, SEQ, d), 1.0),
        'x_sample': nrm((DEC_BATCH, DEC_SEQ, d), 1.0),
        'cache_mla_ckv': nrm((DEC_BATCH, N_EVEN, PAST_LEN, MLA_KV_RANK), 1.0),
        'cache_mla_kpe': nrm((DEC_BATCH, N_EVEN, PAST_LEN, MLA_ROPE_DIM), 1.0),
        'state_ret_fwd': nrm((DEC_BATCH, N_EVEN, RET_HEADS, RET_HEAD_DIM, RET_HEAD_DIM), 1.0),
        'state_ret_bwd': nrm((DEC_BATCH, N_EVEN, RET_HEADS, RET_HEAD_DIM, RET_HEAD_DIM), 1.0),
        'cache_swa_k': nrm((DEC_BATCH, N_ODD, PAST_LEN, SWA_KV_HEADS, SWA_HEAD_DIM), 1.0),
        'cache_swa_v': nrm((DEC_BATCH, N_ODD, PAST_LEN, SWA_KV_HEADS, SWA_HEAD_DIM), 1.0),
        'c': nrm((DEC_BATCH, d), 1.0),
        'c_ctx': nrm((d,), 1.0),
        'w_mod': nrm((DEPTH, d, 6 * d), 0.5 * d ** -0.5),
        'b_mod': nrm((DEPTH, 6 * d), 0.02),
        'ln1_g': 1.0 + nrm((DEPTH, d), 0.02),
        'ln1_b': nrm((DEPTH, d), 0.02),
        'ln2_g': 1.0 + nrm((DEPTH, d), 0.02),
        'ln2_b': nrm((DEPTH, d), 0.02),
        'mla_ret_w_in': nrm((N_EVEN, d, EVEN_IN_DIM), d ** -0.5),
        'mla_q_norm': 1.0 + nrm((N_EVEN, MLA_Q_RANK), 0.02),
        'mla_w_uq': nrm((N_EVEN, MLA_Q_RANK, MLA_HEADS * (MLA_NOPE_DIM + MLA_ROPE_DIM)), MLA_Q_RANK ** -0.5),
        'mla_kv_norm': 1.0 + nrm((N_EVEN, MLA_KV_RANK), 0.02),
        'mla_w_uk': nrm((N_EVEN, MLA_KV_RANK, MLA_HEADS * MLA_NOPE_DIM), MLA_KV_RANK ** -0.5),
        'mla_w_uv': nrm((N_EVEN, MLA_KV_RANK, MLA_HEADS * MLA_V_DIM), MLA_KV_RANK ** -0.5),
        'ret_decay_fwd': base_logit + nrm((N_EVEN, RET_HEADS), 0.1),
        'ret_decay_bwd': base_logit + nrm((N_EVEN, RET_HEADS), 0.1),
        'ret_gn_g': 1.0 + nrm((N_EVEN, RET_WIDTH), 0.02),
        'even_w_out': nrm((N_EVEN, EVEN_MIX_DIM, d), EVEN_MIX_DIM ** -0.5 * BETA),
        'swa_w_in': nrm((N_ODD, d, SWA_IN_DIM), d ** -0.5),
        'swa_sink': nrm((N_ODD, SWA_HEADS), 0.5),
        'swa_w_out': nrm((N_ODD, SWA_Q_DIM, d), SWA_Q_DIM ** -0.5 * BETA),
        'moe_router': nrm((DEPTH, d, N_EXPERTS), d ** -0.5),
        'moe_router_bias': nrm((DEPTH, N_EXPERTS), 0.01),
        'moe_w_gate': nrm((DEPTH, N_EXPERTS, d, EXPERT_DIM), d ** -0.5),
        'moe_w_up': nrm((DEPTH, N_EXPERTS, d, EXPERT_DIM), d ** -0.5),
        'moe_w_down': nrm((DEPTH, N_EXPERTS, EXPERT_DIM, d), EXPERT_DIM ** -0.5 * BETA),
        'shared_w_gate': nrm((DEPTH, d, SHARED_DIM), d ** -0.5),
        'shared_w_up': nrm((DEPTH, d, SHARED_DIM), d ** -0.5),
        'shared_w_down': nrm((DEPTH, SHARED_DIM, d), SHARED_DIM ** -0.5 * BETA),
    }

def reference(x_prompt, x_sample, cache_mla_ckv, cache_mla_kpe, state_ret_fwd, state_ret_bwd,
              cache_swa_k, cache_swa_v, c, c_ctx, w_mod, b_mod, ln1_g, ln1_b, ln2_g, ln2_b,
              mla_ret_w_in, mla_q_norm, mla_w_uq, mla_kv_norm, mla_w_uk, mla_w_uv,
              ret_decay_fwd, ret_decay_bwd, ret_gn_g, even_w_out, swa_w_in, swa_sink, swa_w_out,
              moe_router, moe_router_bias, moe_w_gate, moe_w_up, moe_w_down,
              shared_w_gate, shared_w_up, shared_w_down):
    rows = x_sample.shape[1] // GRID_W
    rope_mla = _axial_rope(rows, MLA_ROPE_DIM)
    rope_swa = _axial_rope(rows, SWA_HEAD_DIM)
    xp, xs = x_prompt, x_sample
    ckv_l, kpe_l, rf_l, rb_l, sk_l, sv_l = [], [], [], [], [], []
    for l in range(DEPTH):
        mp = _modulation(c_ctx[None, :], w_mod[l], b_mod[l])
        ms = _modulation(c, w_mod[l], b_mod[l])
        hp = _modulate(xp, mp[0], mp[1])
        hs = _modulate(xs, ms[0], ms[1])
        if l % 2 == 0:
            e = l // 2
            ew = (mla_ret_w_in[e], mla_q_norm[e], mla_w_uq[e], mla_kv_norm[e], mla_w_uk[e], mla_w_uv[e],
                  ret_decay_fwd[e], ret_decay_bwd[e], ret_gn_g[e], even_w_out[e])
            out_p, (ckv, kpe, s_f, s_b) = _even_mixer(hp, *ew, rope=None, ctx=None)
            ckv_l.append(ckv)
            kpe_l.append(kpe)
            rf_l.append(s_f)
            rb_l.append(s_b)
            out_s, _ = _even_mixer(hs, *ew, rope=rope_mla,
                                   ctx=(cache_mla_ckv[:, e], cache_mla_kpe[:, e],
                                        state_ret_fwd[:, e], state_ret_bwd[:, e]))
        else:
            o = l // 2
            ow = (swa_w_in[o], swa_sink[o], swa_w_out[o])
            out_p, (k_c, v_c) = _odd_mixer(hp, *ow, rope=None, ctx=None)
            sk_l.append(k_c)
            sv_l.append(v_c)
            out_s, _ = _odd_mixer(hs, *ow, rope=rope_swa, ctx=(cache_swa_k[:, o], cache_swa_v[:, o]))
        xp = _layernorm(ALPHA * xp + mp[2] * out_p, ln1_g[l], ln1_b[l])
        xs = _layernorm(ALPHA * xs + ms[2] * out_s, ln1_g[l], ln1_b[l])
        mw = (moe_router[l], moe_router_bias[l], moe_w_gate[l], moe_w_up[l], moe_w_down[l],
              shared_w_gate[l], shared_w_up[l], shared_w_down[l])
        xp = _layernorm(ALPHA * xp + mp[5] * _moe(_modulate(xp, mp[3], mp[4]), *mw), ln2_g[l], ln2_b[l])
        xs = _layernorm(ALPHA * xs + ms[5] * _moe(_modulate(xs, ms[3], ms[4]), *mw), ln2_g[l], ln2_b[l])
    new_mla_ckv = jnp.stack(ckv_l, axis=1)
    new_mla_kpe = jnp.stack(kpe_l, axis=1)
    new_ret_fwd = jnp.stack(rf_l, axis=1)
    new_ret_bwd = jnp.stack(rb_l, axis=1)
    new_swa_k = jnp.stack(sk_l, axis=1)
    new_swa_v = jnp.stack(sv_l, axis=1)
    return (xp, xs, new_mla_ckv, new_mla_kpe, new_ret_fwd, new_ret_bwd, new_swa_k, new_swa_v)


_drawn_inputs = setup_inputs


def setup_inputs(seed=0):
    import zlib

    import numpy as np

    out = dict(_drawn_inputs(seed))
    spreads = {}
    factors = {'cache_mla_ckv': 7.717,
     'cache_mla_kpe': 8.0,
     'cache_swa_k': 6.287,
     'cache_swa_v': 5.981,
     'mla_q_norm': 8.0,
     'mla_w_uq': 4.285,
     'mla_kv_norm': 2.948,
     'mla_w_uk': 4.797,
     'ret_gn_g': 24.746,
     'swa_sink': 39.729}
    for name, (base, spread) in spreads.items():
        noise = np.random.default_rng([zlib.crc32(name.encode()), seed]).standard_normal(out[name].shape)
        drawn = base * np.exp(spread * noise) if base else spread * noise
        out[name] = jnp.asarray(drawn.astype(out[name].dtype))
    for name, factor in factors.items():
        out[name] = (out[name] * factor).astype(out[name].dtype)
    return out
```

```python
from contextlib import ExitStack

import concourse.bass as bass
from concourse import mybir
import numpy as np

F32 = mybir.dt.float32
U32 = mybir.dt.uint32
I32 = mybir.dt.int32
BF16 = mybir.dt.bfloat16
ALU = mybir.AluOpType
ACT = mybir.ActivationFunctionType
AX = mybir.AxisListType

P = 128
D = 1024
KT = D // P
TILES = 3
TOK = TILES * P
DEPTH = 2
ALPHA = (2.0 * DEPTH) ** 0.25
LN_EPS = 1e-5
RMS_EPS = 1e-6
GRID_W = 64
HEADS = 8
NOPE, ROPE, VD = 64, 32, 64
QK = NOPE + ROPE
Q_RANK, KV_RANK = 256, 128
RH, RD = 8, 64
RW = RH * RD
Z_KV = Q_RANK
Z_PE = Z_KV + KV_RANK
Z_RQ = Z_PE + ROPE
Z_RK, Z_RV, Z_RG = Z_RQ + RW, Z_RQ + 2 * RW, Z_RQ + 3 * RW
EVEN_IN = Z_RG + RW
SH, SKV, SD = 16, 4, 64
SQ_DIM, SKV_DIM = SH * SD, SKV * SD
ODD_IN = SQ_DIM + 2 * SKV_DIM
WINDOW = 128
NE = 64
TOPK = 8
NG = 8
GE = NE // NG
TOPG = 4
FD = 256
ROUTED_SCALE = 2.5
NEG = -1e30
ASSIGNED = TOK * TOPK
OVER_BLOCKS = TILES - 1
OVER_KEYS = 24
FAR = 1.0e6

C_ID = 0
C_TRI = C_ID + P
C_ROPE_E = C_TRI + P
C_ROPE_O = C_ROPE_E + 2 * 2 * (ROPE // 2)
C_MASK = C_ROPE_O + 2 * 2 * (SD // 2)
C_DF = C_MASK + 2 * TOK
C_DB = C_DF + P
C_MF = C_DB + P
C_MB = C_MF + P
C_QF = C_MB + P
C_QB = C_QF + P
C_IOTA = C_QB + P
C_COL = C_IOTA + TOK
C_LT8 = C_COL + 4
C_KEY = C_LT8 + 64
C_END = C_KEY + 2 * NE


def shape_tables():
    c = np.zeros((P, C_END), np.float32)
    r = np.arange(P)
    c[:, C_ID:C_ID + P] = np.eye(P)
    c[:, C_TRI:C_TRI + P] = r[:, None] < r[None, :]
    for at, dim in ((C_ROPE_E, ROPE), (C_ROPE_O, SD)):
        nf = dim // 4
        t = np.arange(2 * P)
        freqs = (np.float32(10000.0) ** (-np.arange(nf, dtype=np.float32) / np.float32(nf))).astype(np.float32)
        row = (t // GRID_W).astype(np.float32)
        col = (t % GRID_W).astype(np.float32)
        ang = np.concatenate([row[:, None] * freqs, col[:, None] * freqs], axis=-1)
        for j, f in enumerate((np.cos, np.sin)):
            tab = f(ang).astype(np.float32).reshape(2, P, 2 * nf)
            for i in range(2):
                o = at + (i * 2 + j) * 2 * nf
                c[:, o:o + 2 * nf] = tab[i]
    for i in range(2):
        q = i * P + r
        k = np.arange(2 * P)
        c[:, C_MASK + i * TOK:C_MASK + i * TOK + 2 * P] = np.where(np.abs(q[:, None] - k[None]) <= WINDOW, 0.0, NEG)
    d = r[None, :] - r[:, None]
    c[:, C_DF:C_DF + P] = np.maximum(d, 0)
    c[:, C_DB:C_DB + P] = np.maximum(-d, 0)
    c[:, C_MF:C_MF + P] = d >= 0
    c[:, C_MB:C_MB + P] = d <= 0
    c[:, C_QF:C_QF + P] = r + 1.0
    c[:, C_QB:C_QB + P] = P - r
    c[:, C_IOTA:C_IOTA + TOK] = np.arange(TOK)
    c[:, C_COL] = P - 1 - r
    c[:, C_COL + 1] = r
    c[:, C_LT8:C_LT8 + 64] = (np.arange(8)[None, :] < np.arange(8)[:, None]).reshape(1, 64)
    c[:, C_KEY:C_KEY + 2 * NE] = np.arange(2 * NE) + 1.0
    return c


class Steps:

    def __init__(self, eng, sem):
        self.eng, self.sem, self.n = eng, sem, 0

    def mark(self, ins):
        self.n += 1
        ins.then_inc(self.sem, 1)

    def wait(self):
        self.eng.wait_ge(self.sem, self.n)

    def then(self, ins):
        self.mark(ins)
        self.wait()


class Kernel:

    def __init__(self, nc, ctx, io):
        self.nc, self.io = nc, io

        def sb(name, shape, dt=F32):
            return ctx.enter_context(nc.sbuf_tensor(name, shape, dt))

        self.const = sb("const", [P, C_END])
        self.ones = sb("ones", [P, P])
        self.x = sb("x_tok", [P, TILES, D])
        self.cat = sb("cat", [P, TILES, D])
        self.ring = sb("weights", [P, 12288])
        self.hT = sb("hT", [P, KT, TOK])
        self.hP = sb("hP", [P, TILES, D])
        self.z = sb("z", [P, TILES * EVEN_IN])
        self.s = sb("scratch", [P, 15104])
        self.slot_u = sb("slot_u", [P, TILES, TOPK], U32)
        self.w8 = sb("w8", [P, TILES, TOPK])
        self.tok_idx = sb("tok_idx", [P, NE], U32)
        self.y_idx = sb("y_idx", [P, NE], U32)
        self.incl = sb("incl", [P, TILES, NE])
        self.bases = sb("bases", [P, 2, NE])
        self.over = sb("over", [P, 32], I32)
        self.ps = [ctx.enter_context(nc.psum_tensor(f"bank{i}", [P, 512], F32)) for i in range(8)]
        self.mod_d = nc.dram_tensor("mod_rows", [DEPTH, 2, 6 * D], F32, kind="Internal").ap()
        self.h_d = nc.dram_tensor("h_rows", [TOK, D], F32, kind="Internal").ap()
        self.y_d = nc.dram_tensor("y_rows", [ASSIGNED, D], F32, kind="Internal").ap()
        self.s_const = ctx.enter_context(nc.semaphore("const_loaded"))
        self.s_ahead = [ctx.enter_context(nc.semaphore(f"ahead{i}_loaded")) for i in range(4)]
        self.ahead = [0] * 4
        names = "rows0_gathered rows1_gathered y_stored ov_gathered ov_stored back0_in back1_in back2_in back3_in"
        self.pool_sems = [[ctx.enter_context(nc.semaphore(f"{n}_{layer}")) for n in names.split()] for layer in range(DEPTH)]

    def c(self, at, n, p=P):
        return self.const[0:p, at:at + n]

    @property
    def ident(self):
        return self.const[:, C_ID:C_ID + P]

    def load_ahead(self, eng, i, out, in_):
        eng.dma_start(out, in_).then_inc(self.s_ahead[i], 16)
        self.ahead[i] += 16

    def arrived(self, eng, i):
        eng.wait_ge(self.s_ahead[i], self.ahead[i])


class Stage(ExitStack):

    def __init__(self, nc):
        super().__init__()
        self.nc, self.used = nc, []

    def __exit__(self, *failure):
        super().__exit__(*failure)
        numbers = sorted(s.num for s in self.used)
        while numbers:
            n = 1
            while n < len(numbers) and numbers[n] == numbers[0] + n:
                n += 1
            self.nc.sync.sem_clear(range(numbers[0], numbers[0] + n))
            numbers = numbers[n:]


def sems(nc, ctx, names):
    found = [ctx.enter_context(nc.semaphore(n)) for n in names.split()]
    ctx.used += found
    return found


def stage_setup(k):
    nc, io = k.nc, k.io
    with Stage(nc) as ctx:
        s_x, s_one = sems(nc, ctx, "x_loaded ones_set")
        blk = ctx.enter_context(nc.Block())

        @blk.sync
        def _(sp):
            sp.dma_start(k.const[:], io["tables"]).then_inc(k.s_const, 16)
            sp.dma_start(k.x[:, 0, :], io["x_prompt"].rearrange("b s d -> (b s) d")).then_inc(s_x, 16)
            sp.dma_start(k.x[:, 1:3, :], io["x_sample"].rearrange("b (t p) d -> p (b t) d", p=P)).then_inc(s_x, 16)
            sp.wait_ge(s_x, 32)
            sp.wait_ge(k.s_const, 16)

        @blk.vector
        def _(dve):
            nc.vector.memset(k.ones[:], 1.0).then_inc(s_one, 1)


def stage_mod(k):
    nc, io = k.nc, k.io
    CH = 512
    NCH = 6 * D // CH
    SLOTS = 3
    cond = k.s[:, 0:16].rearrange("p (k r) -> p k r", r=2)
    craw = k.s[:, 16:32].rearrange("p (r k) -> p r k", r=2)
    ce = k.s[:, 32:48].rearrange("p (r k) -> p r k", r=2)
    bmod = k.s[0:1, 64:64 + 6 * D]
    rows = k.s[0:2, 8192:8192 + 6 * D]
    n_all = DEPTH * NCH
    with Stage(nc) as ctx:
        (s_c, s_e, s_d, s_silu, s_mm, s_ev, s_store) = sems(
            nc, ctx, "cond_loaded cond_exp cond_steps cond_silu mod_summed mod_copied mod_stored")
        s_b = sems(nc, ctx, "bias_loaded")[0]
        s_w = sems(nc, ctx, "wmod0_loaded wmod1_loaded wmod2_loaded")
        blk = ctx.enter_context(nc.Block())

        def slot(i):
            return k.ring[:, i * 4096:(i + 1) * 4096].rearrange("p (k n) -> p k n", k=KT)

        @blk.sync
        def _(sp):
            sp.dma_start(craw[:, 0, :], io["c_ctx"].rearrange("(p k) -> p k", k=KT)).then_inc(s_c, 16)
            sp.dma_start(craw[:, 1, :], io["c"].rearrange("b (p k) -> p (b k)", k=KT)).then_inc(s_c, 16)
            for i in range(n_all):
                layer, c = divmod(i, NCH)
                if c == 0:
                    if layer:
                        sp.wait_ge(s_mm, layer * NCH)
                    sp.dma_start(bmod, io["b_mod"][layer:layer + 1, :]).then_inc(s_b, 16)
                if i >= SLOTS:
                    sp.wait_ge(s_mm, i - SLOTS + 1)
                src = io["w_mod"][layer].rearrange("(p k) n -> p k n", k=KT)[:, :, c * CH:(c + 1) * CH]
                sp.dma_start(slot(i % SLOTS), src).then_inc(s_w[i % SLOTS], 16)
                if c == 1 and layer:
                    sp.wait_ge(s_ev, layer * NCH)
                    sp.dma_start(k.mod_d[layer - 1], rows).then_inc(s_store, 16)
            sp.wait_ge(s_ev, n_all)
            sp.dma_start(k.mod_d[DEPTH - 1], rows).then_inc(s_store, 16)
            sp.wait_ge(s_store, 16 * DEPTH)

        @blk.scalar
        def _(act):
            act.wait_ge(s_c, 32)
            nc.scalar.activation(ce, craw, ACT.Exp, scale=-1.0).then_inc(s_e, 1)

        @blk.vector
        def _(dve):
            st = Steps(dve, s_d)
            dve.wait_ge(s_e, 1)
            st.then(nc.vector.tensor_scalar(ce, ce, 1.0, None, ALU.add))
            st.then(nc.vector.reciprocal(ce, ce))
            nc.vector.tensor_tensor(cond.rearrange("p k r -> p r k"), craw, ce, ALU.mult).then_inc(s_silu, 1)
            for i in range(n_all):
                layer, c = divmod(i, NCH)
                dve.wait_ge(s_mm, i + 1)
                if c == 0 and layer:
                    dve.wait_ge(s_store, 16 * layer)
                nc.vector.tensor_copy(rows[:, c * CH:(c + 1) * CH], k.ps[i % 4][0:2, :]).then_inc(s_ev, 1)

        @blk.tensor
        def _(pe):
            pe.wait_ge(s_silu, 1)
            for i in range(n_all):
                layer, c = divmod(i, NCH)
                pe.wait_ge(s_w[i % SLOTS], 16 * (i // SLOTS + 1))
                if c == 0:
                    pe.wait_ge(s_b, 16 * (layer + 1))
                if i >= 4:
                    pe.wait_ge(s_ev, i - 3)
                for kk in range(KT):
                    nc.tensor.matmul(k.ps[i % 4][0:2, :], cond[:, kk, :], slot(i % SLOTS)[:, kk, :], start=(kk == 0), stop=False)
                nc.tensor.matmul(k.ps[i % 4][0:2, :], k.ones[0:1, 0:2], bmod[:, c * CH:(c + 1) * CH], start=False, stop=True).then_inc(s_mm, 1)


def table_load(k, eng, sem, out, layer, cond, part):
    eng.dma_start(out, k.mod_d[layer, cond:cond + 1, part * D:(part + 1) * D].to_broadcast([P, D])).then_inc(sem, 16)


def stage_modulate(k, layer):
    nc = k.nc
    tab = k.s[:, 0:4 * D].rearrange("p (c j n) -> p c j n", c=2, j=2)
    with Stage(nc) as ctx:
        s_t, s_d, = sems(nc, ctx, "table_loaded mod_steps")
        blk = ctx.enter_context(nc.Block())

        @blk.sync
        def _(sp):
            for cnd in range(2):
                for j in range(2):
                    table_load(k, sp, s_t, tab[:, cnd, j, :], layer, cnd, j)

        @blk.vector
        def _(dve):
            st = Steps(dve, s_d)
            dve.wait_ge(s_t, 64)
            for cnd in range(2):
                st.mark(nc.vector.tensor_scalar(tab[:, cnd, 1, :], tab[:, cnd, 1, :], 1.0, None, ALU.add))
            st.wait()
            for t in range(TILES):
                st.mark(nc.vector.tensor_tensor(k.hP[:, t, :], k.x[:, t, :], tab[:, min(t, 1), 1, :], ALU.mult))
            st.wait()
            for t in range(TILES):
                st.mark(nc.vector.tensor_tensor(k.hP[:, t, :], k.hP[:, t, :], tab[:, min(t, 1), 0, :], ALU.add))


def stage_transpose(k, src, ahead=None):
    nc = k.nc
    with Stage(nc) as ctx:
        s_tr, s_a, s_v = sems(nc, ctx, "turned copied_act copied_dve")
        blk = ctx.enter_context(nc.Block())
        n_banks = TILES * KT // 4

        @blk.sync
        def _(sp):
            if ahead:
                ahead(sp)

        @blk.tensor
        def _(pe):
            for b in range(n_banks):
                t, g = divmod(b, 2)
                for j in range(4):
                    kk = 4 * g + j
                    m = nc.tensor.transpose(k.ps[b][:, j * P:(j + 1) * P], src[:, t, kk * P:(kk + 1) * P], k.ident)
                m.then_inc(s_tr, 1)

        def copy(eng_copy, eng, sem, which):
            for b in range(which, n_banks, 2):
                t, g = divmod(b, 2)
                eng.wait_ge(s_tr, b + 1)
                eng_copy(k.hT[:, 4 * g:4 * g + 4, t * P:(t + 1) * P],
                         k.ps[b][:].rearrange("p (j n) -> p j n", j=4)).then_inc(sem, 1)

        @blk.scalar
        def _(act):
            copy(nc.scalar.copy, act, s_a, 0)

        @blk.vector
        def _(dve):
            copy(nc.vector.tensor_copy, dve, s_v, 1)


def ring_slot(k, i):
    return k.ring[:, i * 4096:(i + 1) * 4096].rearrange("p (k n) -> p k n", k=KT)


def chunks_of(n_cols):
    return [(c, min(512, n_cols - c)) for c in range(0, n_cols, 512)]


def first_chunks(k, w, n_cols):
    def ahead(sp):
        for i, (c, n) in enumerate(chunks_of(n_cols)[:3]):
            k.load_ahead(sp, i, ring_slot(k, i)[:, :, 0:n], w.rearrange("(k p) n -> p k n", p=P)[:, :, c:c + n])
    return ahead


def stage_project(k, w, n_cols, out):
    nc = k.nc
    chunks = chunks_of(n_cols)
    with Stage(nc) as ctx:
        s_mm, s_a, s_v = sems(nc, ctx, "product_ready copied_act copied_dve")
        s_w = sems(nc, ctx, "w0_loaded w1_loaded w2_loaded")
        blk = ctx.enter_context(nc.Block())

        @blk.sync
        def _(sp):
            for i, (c, n) in enumerate(chunks[3:]):
                sp.wait_ge(s_mm, TILES * (i + 1))
                sp.dma_start(ring_slot(k, i % 3)[:, :, 0:n], w.rearrange("(k p) n -> p k n", p=P)[:, :, c:c + n]).then_inc(s_w[i % 3], 16)

        @blk.tensor
        def _(pe):
            for i, (c, n) in enumerate(chunks):
                if i < 3:
                    k.arrived(pe, i)
                else:
                    pe.wait_ge(s_w[i % 3], 16 * (i // 3))
                for t in range(TILES):
                    b = i * TILES + t
                    if b >= 8:
                        pe.wait_ge(s_v if b % 2 else s_a, (b - 8) // 2 + 1)
                    for kk in range(KT):
                        m = nc.tensor.matmul(k.ps[b % 8][:, 0:n], k.hT[:, kk, t * P:(t + 1) * P], ring_slot(k, i % 3)[:, kk, 0:n],
                                             start=(kk == 0), stop=(kk == KT - 1))
                    m.then_inc(s_mm, 1)

        def copy(eng_copy, eng, sem, which):
            for b in range(which, len(chunks) * TILES, 2):
                i, t = divmod(b, TILES)
                c, n = chunks[i]
                eng.wait_ge(s_mm, b + 1)
                eng_copy(out(t, c, n), k.ps[b % 8][:, 0:n]).then_inc(sem, 1)

        @blk.scalar
        def _(act):
            copy(nc.scalar.copy, act, s_a, 0)

        @blk.vector
        def _(dve):
            copy(nc.vector.tensor_copy, dve, s_v, 1)


def rope(nc, st, k, at, tile, x, tmp, heads, nf):
    o = at + tile * 4 * nf
    cos = k.const[:, o:o + 2 * nf].rearrange("p (a f) -> p a f", a=2)
    sin = k.const[:, o + 2 * nf:o + 4 * nf].rearrange("p (a f) -> p a f", a=2)
    n = heads * 2 * nf
    t1, t2, t3, t4 = (tmp[:, i * n:(i + 1) * n].rearrange("p (h a f) -> p h a f", a=2, f=nf) for i in range(4))
    for axis in range(2):
        cb = cos[:, axis:axis + 1, :].to_broadcast([P, heads, nf])
        sb = sin[:, axis:axis + 1, :].to_broadcast([P, heads, nf])
        x1, x2 = x[:, :, axis, 0, :], x[:, :, axis, 1, :]
        st.mark(nc.vector.tensor_tensor(t1[:, :, axis, :], x1, cb, ALU.mult))
        st.mark(nc.vector.tensor_tensor(t2[:, :, axis, :], x2, sb, ALU.mult))
        st.mark(nc.vector.tensor_tensor(t3[:, :, axis, :], x2, cb, ALU.mult))
        st.mark(nc.vector.tensor_tensor(t4[:, :, axis, :], x1, sb, ALU.mult))
    st.wait()
    for axis in range(2):
        x1, x2 = x[:, :, axis, 0, :], x[:, :, axis, 1, :]
        st.mark(nc.vector.tensor_tensor(x1, t1[:, :, axis, :], t2[:, :, axis, :], ALU.subtract))
        st.mark(nc.vector.tensor_tensor(x2, t3[:, :, axis, :], t4[:, :, axis, :], ALU.add))
    st.wait()


def stage_mla_norm(k, e):
    nc, io = k.nc, k.io
    z = k.z[:].rearrange("p (t n) -> p t n", t=TILES)
    m = k.mla
    tmp = k.s[:, 14080:14080 + 1024]
    with Stage(nc) as ctx:
        s_l, s_sq, s_d, s_p, s_out = sems(nc, ctx, "norm_loaded squares_summed dve_steps rstd_ready outputs_stored")
        s_ms = sems(nc, ctx, "mean_squares")[0]
        s_n = sems(nc, ctx, "normed")[0]
        blk = ctx.enter_context(nc.Block())

        @blk.sync
        def _(sp):
            sp.dma_start(m["qg"], io["mla_q_norm"][e:e + 1, :].to_broadcast([P, Q_RANK])).then_inc(s_l, 16)
            sp.dma_start(m["kvg"], io["mla_kv_norm"][e:e + 1, :].to_broadcast([P, KV_RANK])).then_inc(s_l, 16)
            sp.dma_start(m["ckv"][:, 3, :], io["cache_mla_ckv"][0, e]).then_inc(s_l, 16)
            sp.dma_start(m["kpe"][:, 3, NOPE:QK], io["cache_mla_kpe"][0, e]).then_inc(s_l, 16)
            k.load_ahead(sp, 0, m["wuq"], io["mla_w_uq"][e].rearrange("(k p) n -> p k n", p=P))
            k.load_ahead(sp, 1, m["wuk"], io["mla_w_uk"][e])
            k.load_ahead(sp, 1, m["wuv"], io["mla_w_uv"][e])
            sp.wait_ge(s_n, 1)
            sp.dma_start(io["new_mla_ckv"][0, e], m["ckv"][:, 0, :]).then_inc(s_out, 16)
            sp.dma_start(io["new_mla_kpe"][0, e], z[:, 0, Z_PE:Z_RQ]).then_inc(s_out, 16)
            sp.wait_ge(s_out, 32)
            sp.wait_ge(s_l, 64)

        @blk.scalar
        def _(act):
            for t in range(TILES):
                nc.scalar.activation(m["junk"][:, 0:Q_RANK], z[:, t, 0:Z_KV], ACT.Square, accum_out=m["ss"][:, t:t + 1]).then_inc(s_sq, 1)
                act.wait_ge(s_sq, 2 * t + 1)
                nc.scalar.activation(m["junk"][:, 0:KV_RANK], z[:, t, Z_KV:Z_PE], ACT.Square, accum_out=m["ss"][:, 3 + t:4 + t]).then_inc(s_sq, 1)
                act.wait_ge(s_sq, 2 * t + 2)

        @blk.gpsimd
        def _(pool):
            pool.wait_ge(s_ms, 2)
            nc.gpsimd.tensor_tensor(m["rstd"], m["ss"], m["half"], ALU.pow).then_inc(s_p, 1)

        @blk.vector
        def _(dve):
            st = Steps(dve, s_d)
            st.mark(nc.vector.memset(m["half"], -0.5))
            st.mark(nc.vector.memset(m["kpe"][:, :, 0:NOPE], 0.0))
            st.wait()
            dve.wait_ge(s_sq, 2 * TILES)
            nc.vector.tensor_scalar(m["ss"][:, 0:3], m["ss"][:, 0:3], 1.0 / Q_RANK, RMS_EPS, ALU.mult, ALU.add).then_inc(s_ms, 1)
            nc.vector.tensor_scalar(m["ss"][:, 3:6], m["ss"][:, 3:6], 1.0 / KV_RANK, RMS_EPS, ALU.mult, ALU.add).then_inc(s_ms, 1)
            dve.wait_ge(s_p, 1)
            dve.wait_ge(s_l, 64)
            for t in range(TILES):
                st.mark(nc.vector.scalar_tensor_tensor(m["qn"][:, t, :], z[:, t, 0:Z_KV], m["rstd"][:, t:t + 1], m["qg"], ALU.mult, ALU.mult))
                st.mark(nc.vector.scalar_tensor_tensor(m["ckv"][:, t, :], z[:, t, Z_KV:Z_PE], m["rstd"][:, 3 + t:4 + t], m["kvg"], ALU.mult, ALU.mult))
            st.mark(nc.vector.tensor_copy(m["kpe"][:, 0, NOPE:QK], z[:, 0, Z_PE:Z_RQ]))
            st.wait()
            nc.vector.memset(m["junk"][:, 0:1], 0.0).then_inc(s_n, 1)
            for t in (1, 2):
                x = z[:, t, Z_PE:Z_RQ].rearrange("p (h a b f) -> p h a b f", h=1, a=2, b=2)
                rope(nc, st, k, C_ROPE_E, t - 1, x, tmp, 1, ROPE // 4)
                st.then(nc.vector.tensor_copy(m["kpe"][:, t, NOPE:QK], z[:, t, Z_PE:Z_RQ]))


def stage_mla_keys(k, e):
    nc = k.nc
    m = k.mla
    tmp = k.s[:, 14080:14080 + 1024]
    with Stage(nc) as ctx:
        s_tr, s_a, s_v, s_d = sems(nc, ctx, "pe_ready copied_act copied_dve dve_steps")
        blk = ctx.enter_context(nc.Block())

        @blk.tensor
        def _(pe):
            for t in range(4):
                mm = nc.tensor.transpose(k.ps[0][:, t * P:(t + 1) * P], m["ckv"][:, t, :], k.ident)
            mm.then_inc(s_tr, 1)
            for t in range(4):
                mm = nc.tensor.transpose(k.ps[1][0:QK, t * P:(t + 1) * P], m["kpe"][:, t, :], k.ident)
            mm.then_inc(s_tr, 1)
            for j in range(2):
                for t in range(TILES):
                    mm = nc.tensor.transpose(k.ps[2 + j][:, t * P:(t + 1) * P], m["qn"][:, t, j * P:(j + 1) * P], k.ident)
                mm.then_inc(s_tr, 1)
            k.arrived(pe, 0)
            pe.wait_ge(s_v, 2)
            for t in range(TILES):
                for j, (c, n) in enumerate(((0, 512), (512, 256))):
                    i = 2 * t + j
                    if i >= 2:
                        pe.wait_ge(s_v, 2 + i - 1)
                    for kk in range(2):
                        mm = nc.tensor.matmul(k.ps[4 + j][:, 0:n], m["qnT"][:, kk, t * P:(t + 1) * P], m["wuq"][:, kk, c:c + n],
                                              start=(kk == 0), stop=(kk == 1))
                    mm.then_inc(s_tr, 1)
            k.arrived(pe, 1)
            pe.wait_ge(s_a, 1)
            for h in range(HEADS):
                if h >= 2:
                    pe.wait_ge(s_a, 2 + h - 1)
                nc.tensor.matmul(k.ps[6 + h % 2][0:NOPE, :], m["wuk"][:, h * NOPE:(h + 1) * NOPE], m["ckvT"], start=True, stop=True).then_inc(s_tr, 1)
            pe.wait_ge(s_a, 2)
            pe.wait_ge(s_v, 2)
            for t in range(4):
                nc.tensor.matmul(k.ps[t][:], m["ckvT"][:, t * P:(t + 1) * P], m["wuv"], start=True, stop=True).then_inc(s_tr, 1)

        @blk.scalar
        def _(act):
            act.wait_ge(s_tr, 1)
            nc.scalar.copy(m["ckvT"], k.ps[0][:]).then_inc(s_a, 1)
            act.wait_ge(s_tr, 2)
            nc.scalar.copy(m["kpeT"][NOPE:QK, :], k.ps[1][NOPE:QK, :]).then_inc(s_a, 1)
            for h in range(HEADS):
                act.wait_ge(s_tr, 11 + h)
                nc.scalar.copy(m["kT"][0:NOPE, h, :], k.ps[6 + h % 2][0:NOPE, :]).then_inc(s_a, 1)
            for t in range(4):
                act.wait_ge(s_tr, 19 + t)
                nc.scalar.copy(m["v"][:, t, :], k.ps[t][:]).then_inc(s_a, 1)

        @blk.vector
        def _(dve):
            st = Steps(dve, s_d)
            for j in range(2):
                dve.wait_ge(s_tr, 3 + j)
                nc.vector.tensor_copy(m["qnT"][:, j, :], k.ps[2 + j][:, 0:TOK]).then_inc(s_v, 1)
            for t in range(TILES):
                for j, (c, n) in enumerate(((0, 512), (512, 256))):
                    dve.wait_ge(s_tr, 5 + 2 * t + j)
                    nc.vector.tensor_copy(m["q"][:, t, c:c + n], k.ps[4 + j][:, 0:n]).then_inc(s_v, 1)
            dve.wait_ge(s_a, 2)
            st.mark(nc.vector.tensor_copy(m["kT"][NOPE:QK, :, :], m["kpeT"][NOPE:QK, :].rearrange("p (o n) -> p o n", o=1).to_broadcast([ROPE, HEADS, 512])))
            dve.wait_ge(s_v, 2 + 2 * TILES)
            for t in (1, 2):
                x = m["q"][:, t, :].rearrange("p (h d) -> p h d", h=HEADS)[:, :, NOPE:QK].rearrange("p h (a b f) -> p h a b f", a=2, b=2)
                rope(nc, st, k, C_ROPE_E, t - 1, x, tmp, HEADS, ROPE // 4)


def stage_turn_heads(k, jobs, dim):
    nc = k.nc
    with Stage(nc) as ctx:
        s_tr, s_a, s_v = sems(nc, ctx, "turned copied_act copied_dve")
        blk = ctx.enter_context(nc.Block())

        @blk.tensor
        def _(pe):
            for b, (srcs, _) in enumerate(jobs):
                if b >= 8:
                    pe.wait_ge(s_v if b % 2 else s_a, (b - 8) // 2 + 1)
                for j, src in enumerate(srcs):
                    m = nc.tensor.transpose(k.ps[b % 8][0:dim, j * P:(j + 1) * P], src, k.ident)
                m.then_inc(s_tr, 1)

        def copy(eng_copy, eng, sem, which):
            for b in range(which, len(jobs), 2):
                eng.wait_ge(s_tr, b + 1)
                srcs, dst = jobs[b]
                eng_copy(dst, k.ps[b % 8][0:dim, 0:len(srcs) * P].rearrange("p (j n) -> p j n", n=P)).then_inc(sem, 1)

        @blk.scalar
        def _(act):
            copy(nc.scalar.copy, act, s_a, 0)

        @blk.vector
        def _(dve):
            copy(nc.vector.tensor_copy, dve, s_v, 1)


def stage_attention(k, heads, scale, ahead=None):
    nc = k.nc
    N = len(heads)
    o = 0
    pr = k.s[:, o:o + 3 * TOK].rearrange("p (b n) -> p b n", b=3)
    o += 3 * TOK
    pt = k.s[:, o:o + 2 * TOK].rearrange("p (b n) -> p b n", b=2)
    o += 2 * TOK
    sc = k.s[:, o:o + 2 * TOK].rearrange("p (b n) -> p b n", b=2)
    o += 2 * TOK
    st_ = k.s[:, o:o + 5 * N]
    mx, nb, sm, si, rc = (st_[:, i * N:(i + 1) * N] for i in range(5))
    with Stage(nc) as ctx:
        s_s, s_mx, s_e, s_t, s_pt, s_o, s_se, s_out, s_d = sems(
            nc, ctx, "scores_ready max_ready probs_ready turned probsT_ready sums_ready sink_exp out_ready dve_steps")
        blk = ctx.enter_context(nc.Block())

        @blk.sync
        def _(sp):
            if ahead:
                ahead(sp)

        @blk.tensor
        def _(pe):
            for i in range(N + 2):
                if i < N:
                    h = heads[i]
                    n = h["keys"].shape[1]
                    if i >= 3:
                        pe.wait_ge(s_e, i - 2)
                    nc.tensor.matmul(k.ps[i % 3][:, 0:n], h["q"], h["keys"], start=True, stop=True).then_inc(s_s, 1)
                if 1 <= i <= N:
                    j = i - 1
                    n = heads[j]["keys"].shape[1]
                    pe.wait_ge(s_e, j + 1)
                    if j >= 2:
                        pe.wait_ge(s_pt, j - 1)
                    for c in range(n // P):
                        m = nc.tensor.transpose(k.ps[3 + j % 2][:, c * P:(c + 1) * P], pr[:, j % 3, c * P:(c + 1) * P], k.ident)
                    m.then_inc(s_t, 1)
                if i >= 2:
                    j = i - 2
                    h = heads[j]
                    n = h["keys"].shape[1]
                    pe.wait_ge(s_pt, j + 1)
                    if j >= 2:
                        pe.wait_ge(s_out, j - 1)
                    for c in range(n // P):
                        m = nc.tensor.matmul(k.ps[5 + j % 2][:, 0:VD], pt[:, j % 2, c * P:(c + 1) * P], h["v"][c],
                                             start=(c == 0), stop=(c == n // P - 1))
                    m.then_inc(s_o, 1)

        @blk.scalar
        def _(act):
            for i in range(N + 1):
                if i < N:
                    n = heads[i]["keys"].shape[1]
                    act.wait_ge(s_mx, i + 1)
                    if i >= 3:
                        act.wait_ge(s_t, i - 2)
                    if heads[i].get("sink") is not None:
                        nc.scalar.activation(si[:, i:i + 1], heads[i]["sink"], ACT.Exp, bias=nb[:, i:i + 1]).then_inc(s_se, 1)
                    src = sc[:, i % 2, 0:n] if heads[i].get("mask") is not None else k.ps[i % 3][:, 0:n]
                    sl = 1.0 if heads[i].get("mask") is not None else scale
                    nc.scalar.activation(pr[:, i % 3, 0:n], src, ACT.Exp, bias=nb[:, i:i + 1], scale=sl,
                                         accum_out=sm[:, i:i + 1]).then_inc(s_e, 1)
                if i >= 1:
                    j = i - 1
                    n = heads[j]["keys"].shape[1]
                    act.wait_ge(s_t, j + 1)
                    if j >= 2:
                        act.wait_ge(s_o, j - 1)
                    nc.scalar.copy(pt[:, j % 2, 0:n], k.ps[3 + j % 2][:, 0:n]).then_inc(s_pt, 1)

        @blk.vector
        def _(dve):
            st = Steps(dve, s_d)
            for i in range(N + 2):
                if i < N:
                    h = heads[i]
                    n = h["keys"].shape[1]
                    dve.wait_ge(s_s, i + 1)
                    src, sl = k.ps[i % 3][:, 0:n], scale
                    if h.get("mask") is not None:
                        if i >= 2:
                            dve.wait_ge(s_e, i - 1)
                        st.then(nc.vector.scalar_tensor_tensor(sc[:, i % 2, 0:n], src, scale, h["mask"], ALU.mult, ALU.add))
                        src, sl = sc[:, i % 2, 0:n], 1.0
                    st.then(nc.vector.tensor_reduce(mx[:, i:i + 1], src, AX.X, ALU.max))
                    if h.get("sink") is not None:
                        st.then(nc.vector.tensor_scalar(mx[:, i:i + 1], mx[:, i:i + 1], sl, h["sink"], ALU.mult, ALU.max))
                        sl = 1.0
                    nc.vector.tensor_scalar(nb[:, i:i + 1], mx[:, i:i + 1], -sl, None, ALU.mult).then_inc(s_mx, 1)
                if i >= 2:
                    j = i - 2
                    h = heads[j]
                    dve.wait_ge(s_e, j + 1)
                    if h.get("sink") is not None:
                        dve.wait_ge(s_se, j + 1)
                        st.then(nc.vector.tensor_tensor(sm[:, j:j + 1], sm[:, j:j + 1], si[:, j:j + 1], ALU.add))
                    st.then(nc.vector.reciprocal(rc[:, j:j + 1], sm[:, j:j + 1]))
                    dve.wait_ge(s_o, j + 1)
                    nc.vector.tensor_scalar(h["out"], k.ps[5 + j % 2][:, 0:VD], rc[:, j:j + 1], None, ALU.mult).then_inc(s_out, 1)


def stage_retention(k, e):
    nc, io = k.nc, k.io
    z = k.z[:].rearrange("p (t n) -> p t n", t=TILES)
    R = k.ring
    qT = R[0:RD, 0:3072].rearrange("p (t h n) -> p t h n", t=TILES, h=RH)
    kT = R[0:RD, 3072:6144].rearrange("p (t h n) -> p t h n", t=TILES, h=RH)
    qd = R[0:RD, 6144:10240].rearrange("p (d t h n) -> p d t h n", d=2, t=2, h=RH)
    kd = R[:, 10240:12288].rearrange("p (j n) -> p j n", j=4)
    o = 0

    def cut(n, p=P):
        nonlocal o
        o += n
        return k.s[0:p, o - n:o]

    lg = cut(16)
    kdec = cut(16).rearrange("p (d h) -> p d h", d=2)
    cdec = cut(16)
    DT = cut(2 * RH * P).rearrange("p (d h n) -> p d h n", d=2, h=RH)
    qdec = cut(2 * RH * P, RD).rearrange("p (d h n) -> p d h n", d=2, h=RH)
    S0 = cut(2 * RW, RD).rearrange("p (d n) -> p d n", d=2)
    S1 = cut(4 * RW, RD).rearrange("p (j n) -> p j n", j=4)
    AT = cut(4 * P).rearrange("p (b d n) -> p b d n", b=2, d=2)
    gn = cut(RW)
    raw = cut(2 * RW).rearrange("p (d n) -> p d n", d=2)
    sq = cut(RW)
    stat = cut(64)
    half = cut(32)
    gate = cut(RW)
    assert o <= 15104
    STATES = ((0, 0), (1, 0), (0, 1), (1, 2))
    with Stage(nc) as ctx:
        s_l, s_g, s_dec, s_d, s_p, s_pw, s_st, s_sc, s_store, s_ss = sems(
            nc, ctx, "params_loaded act_steps decays_ready dve_steps rstd_ready var_ready state_ready state_copied states_stored states_scaled")
        s_at, s_am, s_o, s_or, s_gt, s_q = sems(nc, ctx, "attn_ready attn_masked out_summed out_read gate_exp q_decayed")
        blk = ctx.enter_context(nc.Block())

        @blk.sync
        def _(sp):
            for d, n in enumerate(("ret_decay_fwd", "ret_decay_bwd")):
                sp.dma_start(lg[:, d * RH:(d + 1) * RH], io[n][e:e + 1, :].to_broadcast([P, RH])).then_inc(s_l, 16)
            sp.dma_start(gn, io["ret_gn_g"][e:e + 1, :].to_broadcast([P, RW])).then_inc(s_l, 16)
            for d, n in enumerate(("state_ret_fwd", "state_ret_bwd")):
                sp.dma_start(S0[:, d, :].rearrange("p (h n) -> p h n", h=RH), io[n][0, e].rearrange("h d n -> d h n")).then_inc(s_l, 16)
            sp.wait_ge(s_ss, 2)
            for d, n in enumerate(("new_ret_fwd", "new_ret_bwd")):
                sp.dma_start(io[n][0, e].rearrange("h d n -> d h n"), S1[:, d, :].rearrange("p (h n) -> p h n", h=RH)).then_inc(s_store, 16)
            sp.wait_ge(s_store, 32)

        @blk.scalar
        def _(act):
            st = Steps(act, s_g)
            act.wait_ge(s_l, 80)
            st.then(nc.scalar.activation(lg, lg, ACT.Exp, scale=-1.0))
            st.then(nc.scalar.activation(lg, lg, ACT.Ln, bias=1.0))
            st.then(nc.scalar.mul(lg, lg, -1.0))
            for d in range(2):
                nc.scalar.activation(kdec[:, d, :], lg[:, d * RH:(d + 1) * RH], ACT.Exp, scale=k.const[:, C_COL + d:C_COL + d + 1]).then_inc(s_dec, 1)
                nc.scalar.activation(cdec[:, d * RH:(d + 1) * RH], lg[:, d * RH:(d + 1) * RH], ACT.Exp, scale=float(P)).then_inc(s_dec, 1)
                for h in range(RH):
                    col = lg[:, d * RH + h:d * RH + h + 1]
                    nc.scalar.activation(DT[:, d, h, :], k.c((C_DF, C_DB)[d], P), ACT.Exp, scale=col).then_inc(s_dec, 1)
                    nc.scalar.activation(qdec[:, d, h, :], k.c((C_QF, C_QB)[d], P, RD), ACT.Exp, scale=col[0:RD]).then_inc(s_dec, 1)
            for t in range(TILES):
                if t:
                    act.wait_ge(s_q, 2 + t)
                nc.scalar.activation(gate, z[:, t, Z_RG:EVEN_IN], ACT.Exp, scale=-1.0).then_inc(s_gt, 1)

        @blk.gpsimd
        def _(pool):
            for i in range(2 * TILES):
                pool.wait_ge(s_pw, i + 1)
                c = stat[:, 16 + 8 * (i % 2):24 + 8 * (i % 2)]
                nc.gpsimd.tensor_tensor(c, c, half[:, 0:8], ALU.pow).then_inc(s_p, 1)

        @blk.tensor
        def _(pe):
            pe.wait_ge(s_sc, 1)
            for j, (d, t) in enumerate(STATES):
                for h in range(RH):
                    m = nc.tensor.matmul(k.ps[j][0:RD, h * RD:(h + 1) * RD], kd[:, j, h * RD:(h + 1) * RD],
                                         z[:, t, Z_RV + h * RD:Z_RV + (h + 1) * RD], start=True, stop=True)
                m.then_inc(s_st, 1)
            pe.wait_ge(s_ss, 4)
            pe.wait_ge(s_q, 2)
            for i in range(TILES * RH + 1):
                if i < TILES * RH:
                    t, h = divmod(i, RH)
                    if i >= 2:
                        pe.wait_ge(s_am, 2 * (i - 1))
                    nc.tensor.matmul(k.ps[i % 2][:, 0:P], kT[:, t, h, :], qT[:, t, h, :], start=True, stop=True).then_inc(s_at, 1)
                if i >= 1:
                    j = i - 1
                    t, h = divmod(j, RH)
                    pe.wait_ge(s_am, 2 * (j + 1))
                    if h == 0 and t:
                        pe.wait_ge(s_or, 2 * t)
                    v = z[:, t, Z_RV + h * RD:Z_RV + (h + 1) * RD]
                    for d in range(2):
                        out = k.ps[4 + d][:, h * RD:(h + 1) * RD]
                        m = nc.tensor.matmul(out, AT[:, j % 2, d, :], v, start=True, stop=(t == 0))
                        if t:
                            first = (t == 1) == (d == 0)
                            S = S0[:, d, :] if first else S1[:, 2 + d, :]
                            m = nc.tensor.matmul(out, qd[:, d, t - 1, h, :], S[:, h * RD:(h + 1) * RD], start=False, stop=True)
                    m.then_inc(s_o, 1)

        @blk.vector
        def _(dve):
            st = Steps(dve, s_d)
            st.mark(nc.vector.memset(half, -0.5))
            dve.wait_ge(s_dec, 2 * (2 + 2 * RH))
            for j, (d, t) in enumerate(STATES):
                kv = z[:, t, Z_RK:Z_RV].rearrange("p (h n) -> p h n", h=RH)
                st.mark(nc.vector.tensor_tensor(kd[:, j, :].rearrange("p (h n) -> p h n", h=RH), kv,
                                                kdec[:, d, :].rearrange("p (h o) -> p h o", o=1).to_broadcast([P, RH, RD]), ALU.mult))
            st.wait()
            nc.vector.tensor_scalar(kd, kd, RD ** -0.5, None, ALU.mult).then_inc(s_sc, 1)
            for d in range(2):
                st.mark(nc.vector.tensor_tensor(DT[:, d], DT[:, d], k.c((C_MF, C_MB)[d], P).rearrange("p (o n) -> p o n", o=1).to_broadcast([P, RH, P]), ALU.mult))
            for d in range(2):
                for t in range(2):
                    m = nc.vector.tensor_tensor(qd[:, d, t], qT[:, t + 1], qdec[:, d], ALU.mult)
                    st.mark(m)
            st.wait()
            nc.vector.memset(stat[:, 48:49], 0.0).then_inc(s_q, 2)
            for j, (d, t) in enumerate(STATES):
                dve.wait_ge(s_st, j + 1)
                if t == 0:
                    nc.vector.tensor_copy(S1[:, j, :], k.ps[j][0:RD, :]).then_inc(s_ss, 1)
                else:
                    sv = S1[:, j, :].rearrange("p (h n) -> p h n", h=RH)
                    st.then(nc.vector.tensor_tensor(sv, S0[:, d, :].rearrange("p (h n) -> p h n", h=RH),
                                                    cdec[0:RD, d * RH:(d + 1) * RH].rearrange("p (h o) -> p h o", o=1).to_broadcast([RD, RH, RD]), ALU.mult))
                    nc.vector.tensor_tensor(S1[:, j, :], S1[:, j, :], k.ps[j][0:RD, :], ALU.add).then_inc(s_ss, 1)

            def norm(t):
                for d in range(2):
                    x = raw[:, d, :]
                    xv = x.rearrange("p (h n) -> p h n", h=RH)
                    sv = sq.rearrange("p (h n) -> p h n", h=RH)
                    mu, var = stat[:, 0:8], stat[:, 16 + 8 * d:24 + 8 * d]
                    st.mark(nc.vector.tensor_copy(x, k.ps[4 + d][:]))
                    st.wait()
                    nc.vector.memset(stat[:, 49:50], 0.0).then_inc(s_or, 1)
                    st.then(nc.vector.tensor_reduce(mu, xv, AX.X, ALU.add))
                    st.then(nc.vector.tensor_scalar(mu, mu, 1.0 / RD, None, ALU.mult))
                    st.then(nc.vector.tensor_tensor(xv, xv, mu.rearrange("p (h o) -> p h o", o=1).to_broadcast([P, RH, RD]), ALU.subtract))
                    st.then(nc.vector.tensor_tensor(sq, x, x, ALU.mult))
                    st.then(nc.vector.tensor_reduce(var, sv, AX.X, ALU.add))
                    nc.vector.tensor_scalar(var, var, 1.0 / RD, LN_EPS, ALU.mult, ALU.add).then_inc(s_pw, 1)
                for d in range(2):
                    xv = raw[:, d, :].rearrange("p (h n) -> p h n", h=RH)
                    var = stat[:, 16 + 8 * d:24 + 8 * d]
                    dve.wait_ge(s_p, 2 * t + d + 1)
                    st.mark(nc.vector.tensor_tensor(xv, xv, var.rearrange("p (h o) -> p h o", o=1).to_broadcast([P, RH, RD]), ALU.mult))
                st.wait()
                st.then(nc.vector.tensor_tensor(sq, raw[:, 0, :], raw[:, 1, :], ALU.add))
                st.then(nc.vector.tensor_tensor(sq, sq, gn, ALU.mult))
                dve.wait_ge(s_gt, t + 1)
                st.then(nc.vector.tensor_scalar(gate, gate, 1.0, None, ALU.add))
                st.then(nc.vector.reciprocal(gate, gate))
                st.then(nc.vector.tensor_tensor(sq, sq, gate, ALU.mult))
                st.then(nc.vector.tensor_tensor(k.cat[:, t, HEADS * VD:D], sq, z[:, t, Z_RG:EVEN_IN], ALU.mult))
                nc.vector.memset(stat[:, 50:51], 0.0).then_inc(s_q, 1)

            for i in range(TILES * RH):
                t, h = divmod(i, RH)
                dve.wait_ge(s_at, i + 1)
                if i >= 2:
                    dve.wait_ge(s_o, i - 1)
                for d in range(2):
                    nc.vector.scalar_tensor_tensor(AT[:, i % 2, d, :], k.ps[i % 2][:, 0:P], RD ** -0.5, DT[:, d, h, :], ALU.mult, ALU.mult).then_inc(s_am, 1)
                if h == RH - 1:
                    dve.wait_ge(s_o, i + 1)
                    norm(t)


def retention_jobs(k):
    z = k.z[:].rearrange("p (t n) -> p t n", t=TILES)
    R = k.ring
    jobs = []
    for base, at in ((Z_RQ, 0), (Z_RK, 3072)):
        dst = R[0:RD, at:at + 3072].rearrange("p (t h n) -> p t h n", t=TILES, h=RH)
        for t in range(TILES):
            for g in range(2):
                jobs.append(([z[:, t, base + (4 * g + j) * RD:base + (4 * g + j + 1) * RD] for j in range(4)], dst[:, t, 4 * g:4 * g + 4, :]))
    return jobs


def stage_swa_prep(k, o):
    nc, io = k.nc, k.io
    z = k.zo
    tmp = k.s[:, 0:4 * SH * SD // 2]
    with Stage(nc) as ctx:
        s_l, s_d, s_out = sems(nc, ctx, "context_loaded dve_steps outputs_stored")
        blk = ctx.enter_context(nc.Block())

        @blk.sync
        def _(sp):
            sp.dma_start(k.kctx, io["cache_swa_k"][0, o].rearrange("s h d -> s (h d)")).then_inc(s_l, 16)
            sp.dma_start(k.vctx, io["cache_swa_v"][0, o].rearrange("s h d -> s (h d)")).then_inc(s_l, 16)
            sp.dma_start(k.sink, io["swa_sink"][o:o + 1, :].to_broadcast([P, SH])).then_inc(s_l, 16)
            sp.dma_start(io["new_swa_k"][0, o].rearrange("s h d -> s (h d)"), z[:, 0, SQ_DIM:SQ_DIM + SKV_DIM]).then_inc(s_out, 16)
            sp.dma_start(io["new_swa_v"][0, o].rearrange("s h d -> s (h d)"), z[:, 0, SQ_DIM + SKV_DIM:ODD_IN]).then_inc(s_out, 16)
            sp.wait_ge(s_l, 48)
            sp.wait_ge(s_out, 32)

        @blk.vector
        def _(dve):
            st = Steps(dve, s_d)
            for t in (1, 2):
                for at, hh in ((0, SH), (SQ_DIM, SKV)):
                    x = z[:, t, at:at + hh * SD].rearrange("p (h a b f) -> p h a b f", h=hh, a=2, b=2)
                    rope(nc, st, k, C_ROPE_O, t - 1, x, tmp, hh, SD // 4)


def stage_norm(k, layer, which, last):
    nc, io = k.nc, k.io
    T = k.z[:, 0:6144].rearrange("p (c j n) -> p c j n", c=2, j=3)
    gb = k.s[:, 0:2048].rearrange("p (j n) -> p j n", j=2)
    stats = k.s[:, 2048:2048 + 12 * TILES].rearrange("p (t j n) -> p t j n", t=TILES, j=2)
    mv = k.s[:, 2100:2100 + 2 * TILES].rearrange("p (t n) -> p t n", t=TILES)
    half = k.s[:, 2120:2121]
    f = k.hP if which == 1 else k.cat
    parts = (2, 3, 4) if which == 1 else (5,)
    with Stage(nc) as ctx:
        s_t, s_d, s_v, s_p, s_n, s_out, s_f, s_g2 = sems(nc, ctx, "tables_loaded dve_steps var_ready rstd_ready normed outputs_stored gated pool_steps")
        blk = ctx.enter_context(nc.Block())

        @blk.sync
        def _(sp):
            for cnd in range(2):
                for j, part in enumerate(parts):
                    table_load(k, sp, s_t, T[:, cnd, j, :], layer, cnd, part)
            for j, n in enumerate("gb"):
                sp.dma_start(gb[:, j, :], io[f"ln{which}_{n}"][layer:layer + 1, :].to_broadcast([P, D])).then_inc(s_t, 16)
            if which == 1:
                for t in range(TILES):
                    sp.wait_ge(s_n, t + 1)
                    sp.dma_start(k.h_d[t * P:(t + 1) * P, :], k.hP[:, t, :]).then_inc(s_out, 16)
                sp.wait_ge(s_out, 16 * TILES)
            elif last:
                sp.wait_ge(s_n, TILES)
                sp.dma_start(io["y_prompt"].rearrange("b s d -> (b s) d"), k.x[:, 0, :]).then_inc(s_out, 16)
                sp.dma_start(io["y_sample"].rearrange("b (t p) d -> p (b t) d", p=P), k.x[:, 1:3, :]).then_inc(s_out, 16)
                sp.wait_ge(s_out, 32)

        @blk.gpsimd
        def _(pool):
            pool.wait_ge(s_t, 16 * (2 * len(parts) + 2))
            for t in range(TILES):
                nc.gpsimd.tensor_tensor(f[:, t, :], f[:, t, :], T[:, min(t, 1), 0, :], ALU.mult).then_inc(s_f, 1)
            for t in range(TILES):
                pool.wait_ge(s_v, t + 1)
                nc.gpsimd.tensor_tensor(mv[:, t, 1:2], mv[:, t, 1:2], half, ALU.pow).then_inc(s_p, 1)

        @blk.vector
        def _(dve):
            st = Steps(dve, s_d)
            st.mark(nc.vector.memset(half, -0.5))
            dve.wait_ge(s_t, 16 * (2 * len(parts) + 2))
            if which == 1:
                for cnd in range(2):
                    st.mark(nc.vector.tensor_scalar(T[:, cnd, 2, :], T[:, cnd, 2, :], 1.0, None, ALU.add))
            for t in range(TILES):
                x = k.x[:, t, :]
                dve.wait_ge(s_f, t + 1)
                st.then(nc.vector.scalar_tensor_tensor(x, x, ALPHA, f[:, t, :], ALU.mult, ALU.add))
                for j in range(2):
                    st.mark(nc.vector.bn_stats(stats[:, t, j, :], x[:, j * 512:(j + 1) * 512]))
                st.wait()
                st.then(nc.vector.bn_aggr(mv[:, t, :], stats[:, t, :, :]))
                st.wait()
                nc.vector.tensor_scalar(mv[:, t, 1:2], mv[:, t, 1:2], LN_EPS, None, ALU.add).then_inc(s_v, 1)
            for t in range(TILES):
                x = k.x[:, t, :]
                c = min(t, 1)
                dve.wait_ge(s_p, t + 1)
                st.then(nc.vector.tensor_scalar(x, x, mv[:, t, 0:1], mv[:, t, 1:2], ALU.subtract, ALU.mult))
                st.then(nc.vector.tensor_tensor(x, x, gb[:, 0, :], ALU.mult))
                if which == 2:
                    nc.vector.tensor_tensor(x, x, gb[:, 1, :], ALU.add).then_inc(s_n, 1)
                    continue
                st.then(nc.vector.tensor_tensor(x, x, gb[:, 1, :], ALU.add))
                hv = k.hP[:, t, :].rearrange("p (k q) -> p k q", k=KT)
                st.then(nc.vector.tensor_tensor(hv, x.rearrange("p (q k) -> p k q", k=KT), T[:, c, 2, :].rearrange("p (q k) -> p k q", k=KT), ALU.mult))
                nc.vector.tensor_tensor(hv, hv, T[:, c, 1, :].rearrange("p (q k) -> p k q", k=KT), ALU.add).then_inc(s_n, 1)


def bc(ap, shape):
    return ap.to_broadcast(shape)


def stage_route(k, layer):
    nc, io = k.nc, k.io
    o = 0

    def cut(n):
        nonlocal o
        o += n
        return k.z[:, o - n:o]

    E3 = TILES * NE
    scores, sel, mask, W, V, junk, ex = (cut(E3) for _ in range(7))
    g8 = cut(TILES * NG * 8)
    grp, rank, pen = (cut(TILES * NG) for _ in range(3))
    gt, eq = (cut(TILES * NG * NG) for _ in range(2))
    t8 = cut(8 * TILES)
    v8 = cut(8 * TILES)
    wsum = cut(4)
    CB = cut(P)
    bias = cut(NE)
    keys = cut(2 * NE)
    okey = cut(OVER_KEYS + 8)
    yf = cut(NE)
    onesb = cut(4)[:, 0:2].bitcast(BF16)[:, 0:1]
    le = cut(2 * TILES * 512).bitcast(BF16).rearrange("p (b t e n) -> p b t e n", b=2, t=TILES, e=8)
    assert o <= TILES * EVEN_IN, o
    rw = k.s[:, 0:KT * NE].rearrange("p (k n) -> p k n", k=KT)
    sg = k.s[:, 512:512 + 4096]
    sd = k.s[:, 4608:4608 + 2048]

    def tile3(v):
        return v.rearrange("p (t e) -> p t e", t=TILES)

    with Stage(nc) as ctx:
        s_l, s_mm, s_e, s_d, s_m, s_cnt, s_cb, s_base, s_le, s_ix = sems(
            nc, ctx, "router_loaded logits_ready exp_ready dve_steps mask_ready counts_ready counts_copied bases_ready le_ready idx_ready")
        blk = ctx.enter_context(nc.Block())

        @blk.sync
        def _(sp):
            sp.dma_start(rw, io["moe_router"][layer].rearrange("(p k) n -> p k n", k=KT)).then_inc(s_l, 16)
            sp.dma_start(bias, io["moe_router_bias"][layer:layer + 1, :].to_broadcast([P, NE])).then_inc(s_l, 16)
            k.load_ahead(sp, 0, sg[:, 0:2048], io["shared_w_gate"][layer].rearrange("(p k) n -> p (k n)", k=KT))
            k.load_ahead(sp, 0, sg[:, 2048:4096], io["shared_w_up"][layer].rearrange("(p k) n -> p (k n)", k=KT))
            k.load_ahead(sp, 0, sd, io["shared_w_down"][layer].rearrange("(p j) n -> p (j n)", j=2))
            for e in range(2):
                load_expert(k, sp, layer, e, e, k.s_ahead[1 + e], k.s_ahead[1 + e])
                k.ahead[1 + e] += 48

        @blk.tensor
        def _(pe):
            pe.wait_ge(s_l, 32)
            for t in range(TILES):
                for kk in range(KT):
                    m = nc.tensor.matmul(k.ps[t][:, 0:NE], k.hT[:, kk, t * P:(t + 1) * P], rw[:, kk, :], start=(kk == 0), stop=(kk == KT - 1))
                m.then_inc(s_mm, 1)
            tri = k.c(C_TRI, P)
            m3 = tile3(mask)
            pe.wait_ge(s_m, 1)
            for t in range(TILES):
                for u in range(t + 1):
                    nc.tensor.matmul(k.ps[3][:, t * NE:(t + 1) * NE], tri if u == t else k.ones[:], m3[:, u, :], start=(u == 0), stop=(u == t))
            for t in range(TILES):
                nc.tensor.matmul(k.ps[4][:, 0:NE], k.ones[:], m3[:, t, :], start=(t == 0), stop=(t == TILES - 1))
            for t in range(TILES):
                m = nc.tensor.matmul(k.ps[5][0:NE, 0:P], m3[:, t, :], k.ones[:], start=(t == 0), stop=(t == TILES - 1))
            m.then_inc(s_cnt, 1)
            pe.wait_ge(s_cb, 1)
            nc.tensor.matmul(k.ps[6][:, 0:NE], CB[0:NE, :], tri[0:NE, 0:NE], start=True, stop=True).then_inc(s_base, 1)
            for g in range(NE // 8):
                pe.wait_ge(s_le, g + 1)
                for e in range(8):
                    for t in range(TILES):
                        m = nc.tensor.matmul(k.ps[7][:, 8 * g + e:8 * g + e + 1], le[:, g % 2, t, e, :], onesb, start=(t == 0), stop=(t == TILES - 1))
                m.then_inc(s_ix, 1)

        @blk.scalar
        def _(act):
            for t in range(TILES):
                act.wait_ge(s_mm, t + 1)
                nc.scalar.activation(tile3(ex)[:, t, :], k.ps[t][:, 0:NE], ACT.Exp, scale=-1.0).then_inc(s_e, 1)
            act.wait_ge(s_cnt, 1)
            nc.scalar.copy(CB[0:NE, :], k.ps[5][0:NE, 0:P]).then_inc(s_cb, 1)

        @blk.vector
        def _(dve):
            st = Steps(dve, s_d)
            st.mark(nc.vector.memset(onesb, 1.0))
            dve.wait_ge(s_e, TILES)
            st.then(nc.vector.tensor_scalar(ex, ex, 1.0, None, ALU.add))
            st.then(nc.vector.reciprocal(scores, ex))
            dve.wait_ge(s_l, 32)
            st.then(nc.vector.tensor_tensor(tile3(sel), tile3(scores), bc(bias.rearrange("p (o e) -> p o e", o=1), [P, TILES, NE]), ALU.add))
            for i in range(TILES * NG):
                st.mark(nc.vector.max(g8[:, 8 * i:8 * i + 8], sel[:, 8 * i:8 * i + 8]))
            st.wait()
            g8v = g8.rearrange("p (g n) -> p g n", n=8)
            st.then(nc.vector.tensor_tensor(grp, g8v[:, :, 0], g8v[:, :, 1], ALU.add))
            S4 = [P, TILES, NG, NG]
            gj = bc(grp.rearrange("p (t o j) -> p t o j", t=TILES, o=1), S4)
            gg = bc(grp.rearrange("p (t g o) -> p t g o", t=TILES, o=1), S4)
            v4 = lambda v: v.rearrange("p (t g j) -> p t g j", t=TILES, g=NG)
            st.mark(nc.vector.tensor_tensor(v4(gt), gj, gg, ALU.is_gt))
            st.then(nc.vector.tensor_tensor(v4(eq), gj, gg, ALU.is_equal))
            st.then(nc.vector.tensor_tensor(tile3(eq), tile3(eq), bc(k.c(C_LT8, 64).rearrange("p (o n) -> p o n", o=1), [P, TILES, 64]), ALU.mult))
            st.then(nc.vector.tensor_tensor(gt, gt, eq, ALU.add))
            st.then(nc.vector.tensor_reduce(rank, gt.rearrange("p (g j) -> p g j", j=NG), AX.X, ALU.add))
            st.then(nc.vector.tensor_scalar(pen, rank, TOPG - 0.5, -NEG, ALU.is_lt, ALU.mult))
            st.then(nc.vector.tensor_scalar(pen, pen, NEG, None, ALU.add))
            st.then(nc.vector.tensor_tensor(sel.rearrange("p (g n) -> p g n", n=8), sel.rearrange("p (g n) -> p g n", n=8),
                                            bc(pen.rearrange("p (g o) -> p g o", o=1), [P, TILES * NG, 8]), ALU.add))
            for t in range(TILES):
                st.mark(nc.vector.max(t8[:, 8 * t:8 * t + 8], tile3(sel)[:, t, :]))
            st.wait()
            for t in range(TILES):
                st.mark(nc.vector.match_replace(tile3(junk)[:, t, :], t8[:, 8 * t:8 * t + 8], tile3(sel)[:, t, :], 1e38))
            st.wait()
            nc.vector.tensor_scalar(mask, junk, 5e37, None, ALU.is_ge).then_inc(s_m, 1)
            dve.wait_ge(s_m, 1)
            st.then(nc.vector.tensor_tensor(W, scores, mask, ALU.mult))
            st.then(nc.vector.tensor_reduce(wsum[:, 0:TILES], tile3(W), AX.X, ALU.add))
            st.then(nc.vector.reciprocal(wsum[:, 0:TILES], wsum[:, 0:TILES]))
            for t in range(TILES):
                st.mark(nc.vector.tensor_scalar(tile3(W)[:, t, :], tile3(W)[:, t, :], wsum[:, t:t + 1], ROUTED_SCALE, ALU.mult, ALU.mult))
            dve.wait_ge(s_cnt, 1)
            st.then(nc.vector.tensor_tensor(k.incl[:], tile3(k.ps[3][:, 0:E3]), tile3(mask), ALU.add))
            for g in range(NE // 8):
                if g >= 2:
                    dve.wait_ge(s_ix, g - 1)
                for t in range(TILES):
                    m = nc.vector.tensor_tensor(le[:, g % 2, t], bc(k.incl[:, t, 8 * g:8 * g + 8].rearrange("p (e o) -> p e o", o=1), [P, 8, P]),
                                                bc(k.c(C_IOTA, P).rearrange("p (o n) -> p o n", o=1), [P, 8, P]), ALU.is_le)
                    if t == TILES - 1:
                        m.then_inc(s_le, 1)
            dve.wait_ge(s_base, 1)
            base, end = k.bases[:, 0, :], k.bases[:, 1, :]
            st.then(nc.vector.tensor_copy(base, k.ps[6][:, 0:NE]))
            st.then(nc.vector.tensor_tensor(end, base, k.ps[4][:, 0:NE], ALU.add))
            st.then(nc.vector.tensor_tensor(tile3(V), k.incl[:], bc(base.rearrange("p (o e) -> p o e", o=1), [P, TILES, NE]), ALU.add))
            st.then(nc.vector.tensor_tensor(V, V, mask, ALU.mult))
            for t in range(TILES):
                st.mark(nc.vector.max(v8[:, 8 * t:8 * t + 8], tile3(V)[:, t, :]))
            st.wait()
            st.mark(nc.vector.tensor_scalar(k.slot_u[:].rearrange("p t n -> p (t n)"), v8, -1.0, None, ALU.add))
            for t in range(TILES):
                for j in range(TOPK):
                    st.then(nc.vector.scalar_tensor_tensor(tile3(junk)[:, t, :], tile3(V)[:, t, :], v8[:, 8 * t + j:8 * t + j + 1], tile3(W)[:, t, :],
                                                           ALU.is_equal, ALU.mult, accum_out=k.w8[:, t, j:j + 1]))
            col = k.const[:, C_COL + 1:C_COL + 2]
            st.then(nc.vector.tensor_scalar(yf, base, col, None, ALU.add))
            st.then(nc.vector.tensor_tensor(junk[:, 0:NE], yf, end, ALU.is_ge))
            st.then(nc.vector.scalar_tensor_tensor(yf, junk[:, 0:NE], FAR, yf, ALU.mult, ALU.add))
            st.mark(nc.vector.tensor_copy(k.y_idx[:], yf))
            for b in range(OVER_BLOCKS):
                st.then(nc.vector.tensor_scalar(keys[:, b * NE:(b + 1) * NE], k.ps[4][:, 0:NE], P * (b + 1.0), None, ALU.is_gt))
            st.then(nc.vector.tensor_tensor(keys, keys, k.c(C_KEY, 2 * NE), ALU.mult))
            for i in range(OVER_KEYS // 8):
                st.then(nc.vector.max(okey[:, 8 * i:8 * i + 8], keys))
                st.then(nc.vector.match_replace(keys, okey[:, 8 * i:8 * i + 8], keys, -1.0))
            st.then(nc.vector.tensor_scalar(junk[:, 0:OVER_KEYS], okey[:, 0:OVER_KEYS], 0.5, None, ALU.is_gt))
            st.then(nc.vector.tensor_reduce(okey[:, OVER_KEYS:OVER_KEYS + 1], junk[:, 0:OVER_KEYS], AX.X, ALU.add))
            st.then(nc.vector.tensor_scalar(okey[:, 0:OVER_KEYS], okey[:, 0:OVER_KEYS], -1.0, 0.0, ALU.add, ALU.max))
            st.mark(nc.vector.tensor_copy(k.over[:, 0:OVER_KEYS + 1], okey[:, 0:OVER_KEYS + 1]))
            dve.wait_ge(s_ix, NE // 8)
            st.mark(nc.vector.tensor_copy(k.tok_idx[:], k.ps[7][:, 0:NE]))


def expert_views(k, b):
    w = k.ring[:, b * 6144:(b + 1) * 6144]
    return (w[:, 0:2048], w[:, 2048:4096], w[:, 4096:6144],
            w[:, 0:4096].rearrange("p (j k n) -> p k j n", j=2, k=KT), w[:, 4096:6144].rearrange("p (j n) -> p j n", j=2))


def load_gate_up(k, eng, layer, e, b, sem):
    for name, v in zip(("moe_w_gate", "moe_w_up"), expert_views(k, b)):
        src = k.io[name][layer, bass.ds(e, 1)].rearrange("o (p k) n -> p (o k n)", k=KT)
        eng.dma_start(v, src).then_inc(sem, 16)


def load_down(k, eng, layer, e, b, sem):
    src = k.io["moe_w_down"][layer, bass.ds(e, 1)].rearrange("o (p j) n -> p (o j n)", j=2)
    eng.dma_start(expert_views(k, b)[2], src).then_inc(sem, 16)


def load_expert(k, eng, layer, e, b, sem_gu, sem_d):
    load_gate_up(k, eng, layer, e, b, sem_gu)
    load_down(k, eng, layer, e, b, sem_d)


def stage_shared(k):
    nc = k.nc
    sg = k.s[:, 512:512 + 4096].rearrange("p (j k n) -> p k j n", j=2, k=KT)
    sd = k.s[:, 4608:4608 + 2048].rearrange("p (j n) -> p j n", j=2)
    ex = k.s[:, 7000:7000 + FD * TILES].rearrange("p (t n) -> p t n", t=TILES)
    h = k.s[:, 8000:8000 + FD * TILES].rearrange("p (t j n) -> p t j n", t=TILES, j=2)
    hT = k.s[:, 9000:9000 + FD * TILES].rearrange("p (t n) -> p t n", t=TILES)
    with Stage(nc) as ctx:
        s_gu, s_e, s_h, s_ht, s_hc, s_d, s_y, s_v = sems(
            nc, ctx, "gate_up_ready exp_ready h_ready h_turned hT_ready down_ready y_copied dve_steps")
        blk = ctx.enter_context(nc.Block())

        @blk.tensor
        def _(pe):
            k.arrived(pe, 0)
            for t in range(TILES):
                for kk in range(KT):
                    m = nc.tensor.matmul(k.ps[t][:], k.hT[:, kk, t * P:(t + 1) * P], sg[:, kk], start=(kk == 0), stop=(kk == KT - 1))
                m.then_inc(s_gu, 1)
            for t in range(TILES):
                pe.wait_ge(s_h, t + 1)
                for j in range(2):
                    m = nc.tensor.transpose(k.ps[3][:, j * P:(j + 1) * P], h[:, t, j, :], k.ident)
                m.then_inc(s_ht, 1)
                pe.wait_ge(s_hc, t + 1)
                if t >= 2:
                    pe.wait_ge(s_y, 2 * (t - 1))
                for c in range(2):
                    for j in range(2):
                        m = nc.tensor.matmul(k.ps[4 + 2 * (t % 2) + c][:], hT[:, t, j * P:(j + 1) * P], sd[:, j, c * 512:(c + 1) * 512],
                                             start=(j == 0), stop=(j == 1))
                    m.then_inc(s_d, 1)

        @blk.scalar
        def _(act):
            for t in range(TILES):
                act.wait_ge(s_gu, t + 1)
                nc.scalar.activation(ex[:, t, :], k.ps[t][:, 0:FD], ACT.Exp, scale=-1.0).then_inc(s_e, 1)
            for t in range(TILES):
                act.wait_ge(s_ht, t + 1)
                nc.scalar.copy(hT[:, t, :], k.ps[3][:, 0:FD]).then_inc(s_hc, 1)
                for c in range(2):
                    act.wait_ge(s_d, 2 * t + c + 1)
                    nc.scalar.copy(k.cat[:, t, c * 512:(c + 1) * 512], k.ps[4 + 2 * (t % 2) + c][:]).then_inc(s_y, 1)

        @blk.vector
        def _(dve):
            st = Steps(dve, s_v)
            st.mark(nc.vector.memset(k.hP[:], 0.0))
            for t in range(TILES):
                dve.wait_ge(s_e, t + 1)
                st.then(nc.vector.tensor_scalar(ex[:, t, :], ex[:, t, :], 1.0, None, ALU.add))
                st.then(nc.vector.reciprocal(ex[:, t, :], ex[:, t, :]))
                st.then(nc.vector.tensor_tensor(ex[:, t, :], ex[:, t, :], k.ps[t][:, 0:FD], ALU.mult))
                nc.vector.tensor_tensor(h[:, t].rearrange("p j q -> p q j"), ex[:, t, :].rearrange("p (q j) -> p q j", j=2),
                                        k.ps[t][:, FD:2 * FD].rearrange("p (q j) -> p q j", j=2), ALU.mult).then_inc(s_h, 1)


class MoeBuffers:

    def __init__(self, k):
        self.xg = k.hP[:, 0:2, :]
        f = k.s
        self.xT = f[:, 0:1024]
        self.ex = [f[:, 1024 + i * FD:1024 + (i + 1) * FD] for i in range(2)]
        self.h = [f[:, 1536 + i * FD:1536 + (i + 1) * FD] for i in range(2)]
        self.hT = f[:, 2048:2048 + FD]
        self.y = [f[:, 2560 + i * D:2560 + (i + 1) * D] for i in range(2)]
        self.gi = f[:, 4700:4701].bitcast(U32)
        self.si = f[:, 4710:4711].bitcast(U32)


def pe_turn_rows(k, B, b):
    for kk in range(KT):
        m = k.nc.tensor.transpose(k.ps[kk // 4][:, (kk % 4) * P:(kk % 4 + 1) * P], B.xg[:, b, kk * P:(kk + 1) * P], k.ident)
    return m


def pe_gate_up(k, B, b, bank):
    for kk in range(KT):
        m = k.nc.tensor.matmul(k.ps[bank][:], B.xT[:, kk * P:(kk + 1) * P], expert_views(k, b)[3][:, kk], start=(kk == 0), stop=(kk == KT - 1))
    return m


def pe_turn_h(k, B, b):
    for j in range(2):
        m = k.nc.tensor.transpose(k.ps[4][:, j * P:(j + 1) * P], B.h[b][:, j * P:(j + 1) * P], k.ident)
    return m


def pe_down(k, B, b):
    for c in range(2):
        for j in range(2):
            m = k.nc.tensor.matmul(k.ps[5 + c][:], B.hT[:, j * P:(j + 1) * P], expert_views(k, b)[4][:, j, c * 512:(c + 1) * 512],
                                   start=(j == 0), stop=(j == 1))
    return m


def dve_hidden(k, B, b, bank, eng, sem, n):
    nc = k.nc
    g, u = k.ps[bank][:, 0:FD], k.ps[bank][:, FD:2 * FD]
    nc.vector.tensor_scalar(B.ex[b], B.ex[b], 1.0, None, ALU.add).then_inc(sem, 1)
    eng.wait_ge(sem, n + 1)
    nc.vector.reciprocal(B.ex[b], B.ex[b]).then_inc(sem, 1)
    eng.wait_ge(sem, n + 2)
    nc.vector.tensor_tensor(B.ex[b], B.ex[b], g, ALU.mult).then_inc(sem, 1)
    eng.wait_ge(sem, n + 3)
    return nc.vector.tensor_tensor(B.h[b].rearrange("p (j q) -> p q j", j=2), B.ex[b].rearrange("p (q j) -> p q j", j=2),
                                   u.rearrange("p (q j) -> p q j", j=2), ALU.mult)


def gather(k, out, table, last, idx):
    return k.nc.gpsimd.indirect_dma_start(out=out, out_offset=None, in_=table, in_offset=bass.IndirectOffsetOnAxis(ap=idx, axis=0),
                                          bounds_check=last, oob_is_err=False)


def scatter(k, table, last, idx, in_):
    return k.nc.gpsimd.indirect_dma_start(out=table, out_offset=bass.IndirectOffsetOnAxis(ap=idx, axis=0), in_=in_, in_offset=None,
                                          bounds_check=last, oob_is_err=False)


def bounds(pool):
    regs = []
    for v in (TOK - 1, ASSIGNED - 1):
        r = pool.alloc_register()
        pool.reg_mov(r, v)
        regs.append(r)
    return regs


def for_experts(eng, step, last):
    for e in range(3):
        step(e, e // 2, e % 2)
    pairs = (last - 2) // 2
    with eng.Fori(0, pairs) as i:
        step(2 * i + 3, i + 1, 1)
        step(2 * i + 4, i + 2, 0)
    for e in range(3 + 2 * pairs, last + 1):
        step(e, e // 2, e % 2)


def ge(eng, sem, v):
    if not isinstance(v, int) or v > 0:
        eng.wait_ge(sem, v)


def stage_experts(k, layer):
    nc = k.nc
    B = MoeBuffers(k)
    with Stage(nc) as ctx:
        s_xt, s_xa, s_xv, s_gu, s_e, s_hs, s_h, s_ht, s_hc, s_d, s_ya, s_yv = sems(
            nc, ctx, "x_turned xT_copied_act xT_copied_dve gate_up_ready exp_ready h_steps h_ready "
                     "h_turned hT_ready down_ready y_copied_act y_copied_dve")
        s_g, s_sc = k.pool_sems[layer][0:2], k.pool_sems[layer][2]
        s_wg = sems(nc, ctx, "gate_up0_loaded gate_up1_loaded")
        s_wd = sems(nc, ctx, "down0_loaded down1_loaded")
        blk = ctx.enter_context(nc.Block())

        @blk.sync
        def _(sp):
            def step(e, half, b):
                sp.wait_ge(s_gu, e + 1)
                load_gate_up(k, sp, layer, e + 2, b, s_wg[b])
                if not isinstance(e, int) or e >= 1:
                    sp.wait_ge(s_d, e)
                    load_down(k, sp, layer, e + 1, 1 - b, s_wd[1 - b])
            for_experts(sp, step, NE - 3)
            sp.wait_ge(s_d, NE - 2)
            load_down(k, sp, layer, NE - 1, 1, s_wd[1])

        @blk.gpsimd
        def _(pool):
            last_tok, last_row = bounds(pool)

            def get(e, b):
                ge(pool, s_xt, e - 1)
                gather(k, B.xg[:, b, :], k.h_d, last_tok, k.tok_idx[:, e:e + 1]).then_inc(s_g[b], 16)

            def put(e, b):
                pool.wait_ge(s_ya, e + 1)
                pool.wait_ge(s_yv, e + 1)
                ge(pool, s_sc, 16 * e)
                scatter(k, k.y_d, last_row, k.y_idx[:, e:e + 1], B.y[b]).then_inc(s_sc, 16)

            get(0, 0)
            get(1, 1)
            for e in range(NE - 2):
                get(e + 2, e % 2)
                if e >= 1:
                    put(e - 1, (e - 1) % 2)
            for e in range(NE - 3, NE):
                put(e, e % 2)
            pool.wait_ge(s_sc, 16 * NE)

        @blk.tensor
        def _(pe):
            def turn_rows(e, half, b):
                pe.wait_ge(s_g[b], 16 * (half + 1))
                ge(pe, s_xa, e)
                ge(pe, s_xv, e)
                pe_turn_rows(k, B, b).then_inc(s_xt, 1)

            def gate_up(e, half, b):
                pe.wait_ge(s_xa, e + 1)
                pe.wait_ge(s_xv, e + 1)
                if isinstance(e, int) and e < 2:
                    k.arrived(pe, 1 + e)
                else:
                    pe.wait_ge(s_wg[b], 32 * half)
                ge(pe, s_h, e - 1)
                pe_gate_up(k, B, b, 2 + b).then_inc(s_gu, 1)

            def finish(e, half, b):
                pe.wait_ge(s_h, e + 1)
                pe_turn_h(k, B, b).then_inc(s_ht, 1)
                pe.wait_ge(s_hc, e + 1)
                if isinstance(e, int) and e < 2:
                    k.arrived(pe, 1 + e)
                else:
                    pe.wait_ge(s_wd[b], 16 * half)
                ge(pe, s_ya, e)
                ge(pe, s_yv, e)
                pe_down(k, B, b).then_inc(s_d, 1)

            def step(e, half, b):
                gate_up(e, half, b)
                turn_rows(e + 1, half + b, 1 - b)
                if not isinstance(e, int) or e >= 1:
                    finish(e - 1, half - 1 + b, 1 - b)
            turn_rows(0, 0, 0)
            for_experts(pe, step, NE - 2)
            gate_up(NE - 1, NE // 2 - 1, 1)
            finish(NE - 2, NE // 2 - 1, 0)
            finish(NE - 1, NE // 2 - 1, 1)

        @blk.scalar
        def _(act):
            def copy_x(e):
                act.wait_ge(s_xt, e + 1)
                nc.scalar.copy(B.xT[:, 0:512], k.ps[0][:]).then_inc(s_xa, 1)

            def hidden(e, b):
                act.wait_ge(s_gu, e + 1)
                ge(act, s_h, e - 1)
                nc.scalar.activation(B.ex[b], k.ps[2 + b][:, 0:FD], ACT.Exp, scale=-1.0).then_inc(s_e, 1)

            def finish(e, b):
                act.wait_ge(s_ht, e + 1)
                nc.scalar.copy(B.hT, k.ps[4][:, 0:FD]).then_inc(s_hc, 1)
                act.wait_ge(s_d, e + 1)
                ge(act, s_sc, 16 * (e - 1))
                nc.scalar.copy(B.y[b][:, 0:512], k.ps[5][:]).then_inc(s_ya, 1)

            def step(e, half, b):
                hidden(e, b)
                copy_x(e + 1)
                if not isinstance(e, int) or e >= 1:
                    finish(e - 1, 1 - b)
            copy_x(0)
            for_experts(act, step, NE - 2)
            hidden(NE - 1, 1)
            finish(NE - 2, 0)
            finish(NE - 1, 1)

        @blk.vector
        def _(dve):
            def copy_x(e):
                dve.wait_ge(s_xt, e + 1)
                nc.vector.tensor_copy(B.xT[:, 512:1024], k.ps[1][:]).then_inc(s_xv, 1)

            def hidden(e, b):
                dve.wait_ge(s_e, e + 1)
                ge(dve, s_ht, e - 1)
                dve_hidden(k, B, b, 2 + b, dve, s_hs, 3 * e).then_inc(s_h, 1)

            def finish(e, b):
                dve.wait_ge(s_d, e + 1)
                ge(dve, s_sc, 16 * (e - 1))
                nc.vector.tensor_copy(B.y[b][:, 512:1024], k.ps[6][:]).then_inc(s_yv, 1)

            def step(e, half, b):
                hidden(e, b)
                copy_x(e + 1)
                if not isinstance(e, int) or e >= 1:
                    finish(e - 1, 1 - b)
            copy_x(0)
            for_experts(dve, step, NE - 2)
            hidden(NE - 1, 1)
            finish(NE - 2, 0)
            finish(NE - 1, 1)


def stage_overflow(k, layer):
    nc = k.nc
    B = MoeBuffers(k)
    le = k.s[:, 5000:5000 + 3 * 64].bitcast(BF16).rearrange("p (t n) -> p t n", t=TILES)
    onesb = k.s[:, 5200:5202].bitcast(BF16)[:, 0:1]
    row = k.s[:, 5210:5211]
    far = k.s[:, 5212:5213]
    with Stage(nc) as ctx:
        s_w, s_le, s_ix, s_si, s_gi, s_xt, s_x, s_gu, s_e, s_hs, s_h, s_ht, s_hc, s_d, s_y, s_v, s_one, s_free = sems(
            nc, ctx, "ov_loaded ov_le ov_idx ov_rows ov_gidx ov_turned ov_xT ov_gate_up ov_exp ov_hsteps ov_h ov_hturned ov_hT ov_down ov_y "
                     "ov_steps ov_ones ov_free")
        s_g, s_sc = k.pool_sems[layer][3:5]
        blk = ctx.enter_context(nc.Block())

        def items(eng, body):
            n = eng.value_load(k.over[0:1, OVER_KEYS:OVER_KEYS + 1], min_val=0, max_val=OVER_KEYS)
            with eng.If(n > 0):
                with eng.Fori(0, n) as i:
                    body(i)
            with eng.Else():
                pass

        def item(eng, i):
            return eng.value_load(k.over[0:1, bass.ds(i, 1)], min_val=0, max_val=2 * NE - 1)

        @blk.sync
        def _(sp):
            def body(i):
                key = item(sp, i)
                sp.wait_ge(s_free, i + 1)
                load_expert(k, sp, layer, key % NE, 0, s_w, s_w)
            items(sp, body)

        @blk.gpsimd
        def _(pool):
            last_tok, last_row = bounds(pool)

            n = pool.value_load(k.over[0:1, OVER_KEYS:OVER_KEYS + 1], min_val=0, max_val=OVER_KEYS)
            pool.sem_inc(s_free, 1)
            for i in range(OVER_KEYS):
                with pool.If(n > i):
                    pool.wait_ge(s_gi, i + 1)
                    gather(k, B.xg[:, 0, :], k.h_d, last_tok, B.gi).then_inc(s_g, 16)
                    pool.wait_ge(s_si, i + 1)
                    pool.wait_ge(s_y, 2 * i + 2)
                    scatter(k, k.y_d, last_row, B.si, B.y[0]).then_inc(s_sc, 16)
                    pool.wait_ge(s_sc, 16 * i + 16)
                    pool.sem_inc(s_free, 1)
                with pool.Else():
                    pass

        @blk.tensor
        def _(pe):
            def body(i):
                pe.wait_ge(s_le, 3 * i + 3)
                for t in range(TILES):
                    m = nc.tensor.matmul(k.ps[7][:, 0:1], le[:, t, :], onesb, start=(t == 0), stop=(t == TILES - 1))
                m.then_inc(s_ix, 1)
                pe.wait_ge(s_g, 16 * i + 16)
                pe_turn_rows(k, B, 0).then_inc(s_xt, 1)
                pe.wait_ge(s_x, 2 * i + 2)
                pe.wait_ge(s_w, 48 * i + 48)
                pe_gate_up(k, B, 0, 2).then_inc(s_gu, 1)
                pe.wait_ge(s_h, i + 1)
                pe_turn_h(k, B, 0).then_inc(s_ht, 1)
                pe.wait_ge(s_hc, i + 1)
                pe_down(k, B, 0).then_inc(s_d, 1)
            items(pe, body)

        @blk.scalar
        def _(act):
            def body(i):
                act.wait_ge(s_xt, i + 1)
                for j in range(2):
                    nc.scalar.copy(B.xT[:, j * 512:(j + 1) * 512], k.ps[j][:]).then_inc(s_x, 1)
                act.wait_ge(s_gu, i + 1)
                nc.scalar.activation(B.ex[0], k.ps[2][:, 0:FD], ACT.Exp, scale=-1.0).then_inc(s_e, 1)
                act.wait_ge(s_ht, i + 1)
                nc.scalar.copy(B.hT, k.ps[4][:, 0:FD]).then_inc(s_hc, 1)
                act.wait_ge(s_d, i + 1)
                for j in range(2):
                    nc.scalar.copy(B.y[0][:, j * 512:(j + 1) * 512], k.ps[5 + j][:]).then_inc(s_y, 1)
            items(act, body)

        @blk.vector
        def _(dve):
            nc.vector.memset(onesb, 1.0).then_inc(s_one, 1)
            dve.wait_ge(s_one, 1)

            def body(i):
                key = item(dve, i)
                e, blk_no = key % NE, key // NE
                dve.wait_ge(s_free, i + 1)
                for t in range(TILES):
                    nc.vector.tensor_scalar(le[:, t, :], k.const[:, bass.ds(C_IOTA + P + blk_no * P, P)], k.incl[:, t, bass.ds(e, 1)], None,
                                            ALU.is_ge).then_inc(s_le, 1)
                first = k.const[:, bass.ds(C_IOTA + P + blk_no * P, 1)]
                nc.vector.tensor_tensor(row, k.bases[:, 0, bass.ds(e, 1)], first, ALU.add).then_inc(s_v, 1)
                dve.wait_ge(s_v, 4 * i + 1)
                nc.vector.tensor_tensor(row, row, k.const[:, C_COL + 1:C_COL + 2], ALU.add).then_inc(s_v, 1)
                dve.wait_ge(s_v, 4 * i + 2)
                nc.vector.tensor_tensor(far, row, k.bases[:, 1, bass.ds(e, 1)], ALU.is_ge).then_inc(s_v, 1)
                dve.wait_ge(s_v, 4 * i + 3)
                nc.vector.scalar_tensor_tensor(row, far, FAR, row, ALU.mult, ALU.add).then_inc(s_v, 1)
                dve.wait_ge(s_v, 4 * i + 4)
                nc.vector.tensor_copy(B.si, row).then_inc(s_si, 1)
                dve.wait_ge(s_ix, i + 1)
                nc.vector.tensor_copy(B.gi, k.ps[7][:, 0:1]).then_inc(s_gi, 1)
                dve.wait_ge(s_e, i + 1)
                dve_hidden(k, B, 0, 2, dve, s_hs, 3 * i).then_inc(s_h, 1)
            items(dve, body)


def stage_combine(k, layer):
    nc = k.nc
    N = TILES * TOPK
    buf = k.s[:, 0:4 * D].rearrange("p (b n) -> p b n", b=4)
    with Stage(nc) as ctx:
        s_acc = sems(nc, ctx, "row_added")[0]
        s_g = k.pool_sems[layer][5:9]
        blk = ctx.enter_context(nc.Block())
        order = [(t, j) for j in range(TOPK) for t in range(TILES)]

        @blk.gpsimd
        def _(pool):
            last_tok, last_row = bounds(pool)
            for i, (t, j) in enumerate(order):
                if i >= 4:
                    pool.wait_ge(s_acc, i - 3)
                gather(k, buf[:, i % 4, :], k.y_d, last_row, k.slot_u[:, t, j:j + 1]).then_inc(s_g[i % 4], 16)

        @blk.vector
        def _(dve):
            for i, (t, j) in enumerate(order):
                dve.wait_ge(s_g[i % 4], 16 * (i // 4 + 1))
                if i >= TILES:
                    dve.wait_ge(s_acc, i - TILES + 1)
                nc.vector.scalar_tensor_tensor(k.cat[:, t, :], buf[:, i % 4, :], k.w8[:, t, j:j + 1], k.cat[:, t, :], ALU.mult, ALU.add).then_inc(s_acc, 1)


def even_mixer(k, e):
    z = k.z[:].rearrange("p (t n) -> p t n", t=TILES)
    R, S = k.ring, k.s
    stage_project(k, k.io["mla_ret_w_in"][e], EVEN_IN, lambda t, c, n: z[:, t, c:c + n])
    m = k.mla = {}
    m["kT"] = R[0:QK, 0:4096].rearrange("p (h n) -> p h n", h=HEADS)
    m["v"] = R[:, 4096:6144].rearrange("p (t n) -> p t n", t=4)
    m["qT"] = R[0:QK, 6144:9216].rearrange("p (t h n) -> p t h n", t=TILES, h=HEADS)
    m["q"] = R[:, 9216:11520].rearrange("p (t n) -> p t n", t=TILES)
    m["qn"] = R[:, 11520:12288].rearrange("p (t n) -> p t n", t=TILES)
    o = 3200
    for name, n in (("qnT", 768), ("ckv", 512), ("kpe", 384), ("ckvT", 512), ("kpeT", 512), ("wuq", 1536), ("wuk", 512), ("wuv", 512),
                    ("qg", Q_RANK), ("kvg", KV_RANK), ("junk", Q_RANK), ("ss", 6), ("rstd", 6), ("half", 6)):
        m[name] = S[:, o:o + n]
        o += n + n % 2
    m["qnT"] = m["qnT"].rearrange("p (k n) -> p k n", k=2)
    m["ckv"] = m["ckv"].rearrange("p (t n) -> p t n", t=4)
    m["kpe"] = m["kpe"].rearrange("p (t n) -> p t n", t=4)
    m["wuq"] = m["wuq"].rearrange("p (k n) -> p k n", k=2)
    stage_mla_norm(k, e)
    stage_mla_keys(k, e)
    stage_turn_heads(k, [([m["q"][:, t, (4 * g + j) * QK:(4 * g + j + 1) * QK] for j in range(4)], m["qT"][:, t, 4 * g:4 * g + 4, :])
                         for t in range(TILES) for g in range(2)], QK)
    heads = []
    for t in range(TILES):
        for h in range(HEADS):
            lo, hi = (0, 1) if t == 0 else (1, 4)
            heads.append(dict(q=m["qT"][:, t, h, :], keys=m["kT"][:, h, lo * P:hi * P],
                              v=[m["v"][:, i, h * VD:(h + 1) * VD] for i in range(lo, hi)], out=k.cat[:, t, h * VD:(h + 1) * VD]))
    stage_attention(k, heads, QK ** -0.5)
    stage_turn_heads(k, retention_jobs(k), RD)
    stage_retention(k, e)


def odd_mixer(k, o):
    z = k.zo = k.z[:, 0:TILES * ODD_IN].rearrange("p (t n) -> p t n", t=TILES)
    R, S = k.ring, k.s
    stage_project(k, k.io["swa_w_in"][o], ODD_IN, lambda t, c, n: z[:, t, c:c + n])
    k.kctx, k.vctx, k.sink = S[:, 3200:3456], S[:, 3456:3712], S[:, 3712:3728]
    stage_swa_prep(k, o)
    qT = R[0:SD, 0:6144].rearrange("p (t h n) -> p t h n", t=TILES, h=SH)
    kT = R[0:SD, 6144:8192].rearrange("p (h j n) -> p h j n", h=SKV, j=4)
    jobs = [([z[:, t, (4 * g + j) * SD:(4 * g + j + 1) * SD] for j in range(4)], qT[:, t, 4 * g:4 * g + 4, :])
            for t in range(TILES) for g in range(4)]
    for h in range(SKV):
        a = SQ_DIM + h * SD
        jobs.append(([z[:, t, a:a + SD] for t in range(TILES)] + [k.kctx[:, h * SD:(h + 1) * SD]], kT[:, h]))
    stage_turn_heads(k, jobs, SD)
    heads = []
    for t in range(TILES):
        for h in range(SH):
            g = h // (SH // SKV)
            lo, hi = (0, 1) if t == 0 else (1, 4)
            a = SQ_DIM + SKV_DIM + g * SD
            vs = [z[:, i, a:a + SD] for i in range(TILES)] + [k.vctx[:, g * SD:(g + 1) * SD]]
            heads.append(dict(q=qT[:, t, h, :], keys=kT[:, g, lo:hi, :].rearrange("p j n -> p (j n)"), v=vs[lo:hi],
                              out=k.cat[:, t, h * SD:(h + 1) * SD], sink=k.sink[:, h:h + 1],
                              mask=k.c(C_MASK + (t - 1) * TOK, TOK) if t else None))
    stage_attention(k, heads, SD ** -0.5)


def backbone(nc, io):
    with ExitStack() as ctx:
        k = Kernel(nc, ctx, io)
        stage_setup(k)
        stage_mod(k)
        for layer in range(DEPTH):
            w_in, n_in = ((io["mla_ret_w_in"][layer // 2], EVEN_IN), (io["swa_w_in"][layer // 2], ODD_IN))[layer % 2]
            w_out = io[("even_w_out", "swa_w_out")[layer % 2]][layer // 2]
            stage_modulate(k, layer)
            stage_transpose(k, k.hP, first_chunks(k, w_in, n_in))
            (even_mixer, odd_mixer)[layer % 2](k, layer // 2)
            stage_transpose(k, k.cat, first_chunks(k, w_out, D))
            stage_project(k, w_out, D, lambda t, c, n: k.hP[:, t, c:c + n])
            stage_norm(k, layer, 1, False)
            stage_transpose(k, k.hP)
            stage_route(k, layer)
            stage_shared(k)
            stage_experts(k, layer)
            stage_overflow(k, layer)
            stage_combine(k, layer)
            stage_norm(k, layer, 2, layer == DEPTH - 1)


_OUTS = [("y_prompt", (1, P, D)), ("y_sample", (1, 2 * P, D)), ("new_mla_ckv", (1, 1, P, KV_RANK)), ("new_mla_kpe", (1, 1, P, ROPE)),
         ("new_ret_fwd", (1, 1, RH, RD, RD)), ("new_ret_bwd", (1, 1, RH, RD, RD)), ("new_swa_k", (1, 1, P, SKV, SD)), ("new_swa_v", (1, 1, P, SKV, SD))]


def kernel(**inputs):
    import numpy as _np
    import concourse.bacc as _bacc
    from concourse import mybir as _mybir
    from concourse.bass_utils import run_bass_kernel_spmd as _run

    nc = _bacc.Bacc("TRN2", target_bir_lowering=False, num_devices=1)
    arrays, io = {}, {}
    for name, value in [*inputs.items(), ("tables", shape_tables())]:
        a = _np.ascontiguousarray(value)
        if name == "c_ctx":
            a = a.reshape(-1)
        arrays[f"in_{name}"] = a
        io[name] = nc.dram_tensor(f"in_{name}", a.shape, _mybir.dt.from_np(a.dtype), kind="ExternalInput").ap()
    for name, shape in _OUTS:
        io[name] = nc.dram_tensor(f"out_{name}", shape, _mybir.dt.float32, kind="ExternalOutput").ap()
    backbone(nc, io)
    r = _run(nc, [arrays], core_ids=[0])
    return tuple(r.results[0][f"out_{name}"] for name, _ in _OUTS)
```

```python
from contextlib import ExitStack

import concourse.bass as bass
from concourse import mybir
import numpy as np

F32 = mybir.dt.float32
U32 = mybir.dt.uint32
I32 = mybir.dt.int32
BF16 = mybir.dt.bfloat16
ALU = mybir.AluOpType
ACT = mybir.ActivationFunctionType
AX = mybir.AxisListType

P = 128
D = 1024
KT = D // P
TILES = 3
TOK = TILES * P
DEPTH = 2
ALPHA = (2.0 * DEPTH) ** 0.25
LN_EPS = 1e-5
RMS_EPS = 1e-6
GRID_W = 64
HEADS = 8
NOPE, ROPE, VD = 64, 32, 64
QK = NOPE + ROPE
Q_RANK, KV_RANK = 256, 128
RH, RD = 8, 64
RW = RH * RD
Z_KV = Q_RANK
Z_PE = Z_KV + KV_RANK
Z_RQ = Z_PE + ROPE
Z_RK, Z_RV, Z_RG = Z_RQ + RW, Z_RQ + 2 * RW, Z_RQ + 3 * RW
EVEN_IN = Z_RG + RW
SH, SKV, SD = 16, 4, 64
SQ_DIM, SKV_DIM = SH * SD, SKV * SD
ODD_IN = SQ_DIM + 2 * SKV_DIM
WINDOW = 128
NE = 64
TOPK = 8
NG = 8
GE = NE // NG
TOPG = 4
FD = 256
ROUTED_SCALE = 2.5
NEG = -1e30
ASSIGNED = TOK * TOPK
OVER_BLOCKS = TILES - 1
OVER_KEYS = 24
FAR = 1.0e6

C_ID = 0
C_TRI = C_ID + P
C_ROPE_E = C_TRI + P
C_ROPE_O = C_ROPE_E + 2 * 2 * (ROPE // 2)
C_MASK = C_ROPE_O + 2 * 2 * (SD // 2)
C_DF = C_MASK + 2 * TOK
C_DB = C_DF + P
C_MF = C_DB + P
C_MB = C_MF + P
C_QF = C_MB + P
C_QB = C_QF + P
C_IOTA = C_QB + P
C_COL = C_IOTA + TOK
C_LT8 = C_COL + 4
C_KEY = C_LT8 + 64
C_END = C_KEY + 2 * NE


def shape_tables():
    c = np.zeros((P, C_END), np.float32)
    r = np.arange(P)
    c[:, C_ID:C_ID + P] = np.eye(P)
    c[:, C_TRI:C_TRI + P] = r[:, None] < r[None, :]
    for at, dim in ((C_ROPE_E, ROPE), (C_ROPE_O, SD)):
        nf = dim // 4
        t = np.arange(2 * P)
        freqs = (np.float32(10000.0) ** (-np.arange(nf, dtype=np.float32) / np.float32(nf))).astype(np.float32)
        row = (t // GRID_W).astype(np.float32)
        col = (t % GRID_W).astype(np.float32)
        ang = np.concatenate([row[:, None] * freqs, col[:, None] * freqs], axis=-1)
        for j, f in enumerate((np.cos, np.sin)):
            tab = f(ang).astype(np.float32).reshape(2, P, 2 * nf)
            for i in range(2):
                o = at + (i * 2 + j) * 2 * nf
                c[:, o:o + 2 * nf] = tab[i]
    for i in range(2):
        q = i * P + r
        k = np.arange(2 * P)
        c[:, C_MASK + i * TOK:C_MASK + i * TOK + 2 * P] = np.where(np.abs(q[:, None] - k[None]) <= WINDOW, 0.0, NEG)
    d = r[None, :] - r[:, None]
    c[:, C_DF:C_DF + P] = np.maximum(d, 0)
    c[:, C_DB:C_DB + P] = np.maximum(-d, 0)
    c[:, C_MF:C_MF + P] = d >= 0
    c[:, C_MB:C_MB + P] = d <= 0
    c[:, C_QF:C_QF + P] = r + 1.0
    c[:, C_QB:C_QB + P] = P - r
    c[:, C_IOTA:C_IOTA + TOK] = np.arange(TOK)
    c[:, C_COL] = P - 1 - r
    c[:, C_COL + 1] = r
    c[:, C_LT8:C_LT8 + 64] = (np.arange(8)[None, :] < np.arange(8)[:, None]).reshape(1, 64)
    c[:, C_KEY:C_KEY + 2 * NE] = np.arange(2 * NE) + 1.0
    return c


class Steps:

    def __init__(self, eng, sem):
        self.eng, self.sem, self.n = eng, sem, 0

    def mark(self, ins):
        self.n += 1
        ins.then_inc(self.sem, 1)

    def wait(self):
        self.eng.wait_ge(self.sem, self.n)

    def then(self, ins):
        self.mark(ins)
        self.wait()


class Kernel:

    def __init__(self, nc, ctx, io):
        self.nc, self.io = nc, io

        def sb(name, shape, dt=F32):
            return ctx.enter_context(nc.sbuf_tensor(name, shape, dt))

        self.const = sb("const", [P, C_END])
        self.ones = sb("ones", [P, P])
        self.x = sb("x_tok", [P, TILES, D])
        self.cat = sb("cat", [P, TILES, D])
        self.ring = sb("weights", [P, 12288])
        self.hT = sb("hT", [P, KT, TOK])
        self.hP = sb("hP", [P, TILES, D])
        self.z = sb("z", [P, TILES * EVEN_IN])
        self.s = sb("scratch", [P, 15104])
        self.slot_u = sb("slot_u", [P, TILES, TOPK], U32)
        self.w8 = sb("w8", [P, TILES, TOPK])
        self.tok_idx = sb("tok_idx", [P, NE], U32)
        self.y_idx = sb("y_idx", [P, NE], U32)
        self.incl = sb("incl", [P, TILES, NE])
        self.bases = sb("bases", [P, 2, NE])
        self.over = sb("over", [P, 32], I32)
        self.ps = [ctx.enter_context(nc.psum_tensor(f"bank{i}", [P, 512], F32)) for i in range(8)]
        self.mod_d = nc.dram_tensor("mod_rows", [DEPTH, 2, 6 * D], F32, kind="Internal").ap()
        self.h_d = nc.dram_tensor("h_rows", [TOK, D], F32, kind="Internal").ap()
        self.y_d = nc.dram_tensor("y_rows", [ASSIGNED, D], F32, kind="Internal").ap()
        self.s_const = ctx.enter_context(nc.semaphore("const_loaded"))
        self.s_ahead = [ctx.enter_context(nc.semaphore(f"ahead{i}_loaded")) for i in range(5)]
        self.ahead = [0] * 5
        names = "rows0_gathered rows1_gathered y_stored ov_gathered ov_stored back0_in back1_in back2_in back3_in back4_in back5_in back6_in back7_in"
        self.pool_sems = [[ctx.enter_context(nc.semaphore(f"{n}_{layer}")) for n in names.split()] for layer in range(DEPTH)]

    def c(self, at, n, p=P):
        return self.const[0:p, at:at + n]

    @property
    def ident(self):
        return self.const[:, C_ID:C_ID + P]

    def load_ahead(self, eng, i, out, in_):
        eng.dma_start(out, in_).then_inc(self.s_ahead[i], 16)
        self.ahead[i] += 16

    def arrived(self, eng, i):
        eng.wait_ge(self.s_ahead[i], self.ahead[i])


class Stage(ExitStack):

    def __init__(self, nc):
        super().__init__()
        self.nc, self.used = nc, []

    def __exit__(self, *failure):
        super().__exit__(*failure)
        numbers = sorted(s.num for s in self.used)
        while numbers:
            n = 1
            while n < len(numbers) and numbers[n] == numbers[0] + n:
                n += 1
            self.nc.sync.sem_clear(range(numbers[0], numbers[0] + n))
            numbers = numbers[n:]


def sems(nc, ctx, names):
    found = [ctx.enter_context(nc.semaphore(n)) for n in names.split()]
    ctx.used += found
    return found


def stage_setup(k):
    nc, io = k.nc, k.io
    with Stage(nc) as ctx:
        s_x, s_one = sems(nc, ctx, "x_loaded ones_set")
        blk = ctx.enter_context(nc.Block())

        @blk.sync
        def _(sp):
            sp.dma_start(k.const[:], io["tables"]).then_inc(k.s_const, 16)
            sp.dma_start(k.x[:, 0, :], io["x_prompt"].rearrange("b s d -> (b s) d")).then_inc(s_x, 16)
            sp.dma_start(k.x[:, 1:3, :], io["x_sample"].rearrange("b (t p) d -> p (b t) d", p=P)).then_inc(s_x, 16)
            sp.wait_ge(s_x, 32)
            sp.wait_ge(k.s_const, 16)

        @blk.vector
        def _(dve):
            nc.vector.memset(k.ones[:], 1.0).then_inc(s_one, 1)


def stage_mod(k):
    nc, io = k.nc, k.io
    CH = 512
    NCH = 6 * D // CH
    SLOTS = 3
    cond = k.s[:, 0:16].rearrange("p (k r) -> p k r", r=2)
    craw = k.s[:, 16:32].rearrange("p (r k) -> p r k", r=2)
    ce = k.s[:, 32:48].rearrange("p (r k) -> p r k", r=2)
    bmod = k.s[0:1, 64:64 + 6 * D]
    rows = k.s[0:2, 8192:8192 + 6 * D]
    n_all = DEPTH * NCH
    with Stage(nc) as ctx:
        (s_c, s_e, s_d, s_silu, s_mm, s_ev, s_store) = sems(
            nc, ctx, "cond_loaded cond_exp cond_steps cond_silu mod_summed mod_copied mod_stored")
        s_b = sems(nc, ctx, "bias_loaded")[0]
        s_w = sems(nc, ctx, "wmod0_loaded wmod1_loaded wmod2_loaded")
        blk = ctx.enter_context(nc.Block())

        def slot(i):
            return k.ring[:, i * 4096:(i + 1) * 4096].rearrange("p (k n) -> p k n", k=KT)

        @blk.sync
        def _(sp):
            sp.dma_start(craw[:, 0, :], io["c_ctx"].rearrange("(p k) -> p k", k=KT)).then_inc(s_c, 16)
            sp.dma_start(craw[:, 1, :], io["c"].rearrange("b (p k) -> p (b k)", k=KT)).then_inc(s_c, 16)
            for i in range(n_all):
                layer, c = divmod(i, NCH)
                if c == 0:
                    if layer:
                        sp.wait_ge(s_mm, layer * NCH)
                    sp.dma_start(bmod, io["b_mod"][layer:layer + 1, :]).then_inc(s_b, 16)
                if i >= SLOTS:
                    sp.wait_ge(s_mm, i - SLOTS + 1)
                src = io["w_mod"][layer].rearrange("(p k) n -> p k n", k=KT)[:, :, c * CH:(c + 1) * CH]
                sp.dma_start(slot(i % SLOTS), src).then_inc(s_w[i % SLOTS], 16)
                if c == 1 and layer:
                    sp.wait_ge(s_ev, layer * NCH)
                    sp.dma_start(k.mod_d[layer - 1], rows).then_inc(s_store, 16)
            sp.wait_ge(s_ev, n_all)
            sp.dma_start(k.mod_d[DEPTH - 1], rows).then_inc(s_store, 16)
            sp.wait_ge(s_store, 16 * DEPTH)

        @blk.scalar
        def _(act):
            act.wait_ge(s_c, 32)
            nc.scalar.activation(ce, craw, ACT.Exp, scale=-1.0).then_inc(s_e, 1)

        @blk.vector
        def _(dve):
            st = Steps(dve, s_d)
            dve.wait_ge(s_e, 1)
            st.then(nc.vector.tensor_scalar(ce, ce, 1.0, None, ALU.add))
            st.then(nc.vector.reciprocal(ce, ce))
            nc.vector.tensor_tensor(cond.rearrange("p k r -> p r k"), craw, ce, ALU.mult).then_inc(s_silu, 1)
            for i in range(n_all):
                layer, c = divmod(i, NCH)
                dve.wait_ge(s_mm, i + 1)
                if c == 0 and layer:
                    dve.wait_ge(s_store, 16 * layer)
                nc.vector.tensor_copy(rows[:, c * CH:(c + 1) * CH], k.ps[i % 4][0:2, :]).then_inc(s_ev, 1)

        @blk.tensor
        def _(pe):
            pe.wait_ge(s_silu, 1)
            for i in range(n_all):
                layer, c = divmod(i, NCH)
                pe.wait_ge(s_w[i % SLOTS], 16 * (i // SLOTS + 1))
                if c == 0:
                    pe.wait_ge(s_b, 16 * (layer + 1))
                if i >= 4:
                    pe.wait_ge(s_ev, i - 3)
                for kk in range(KT):
                    nc.tensor.matmul(k.ps[i % 4][0:2, :], cond[:, kk, :], slot(i % SLOTS)[:, kk, :], start=(kk == 0), stop=False)
                nc.tensor.matmul(k.ps[i % 4][0:2, :], k.ones[0:1, 0:2], bmod[:, c * CH:(c + 1) * CH], start=False, stop=True).then_inc(s_mm, 1)


def table_load(k, eng, sem, out, layer, cond, part):
    eng.dma_start(out, k.mod_d[layer, cond:cond + 1, part * D:(part + 1) * D].to_broadcast([P, D])).then_inc(sem, 16)


def stage_modulate(k, layer):
    nc = k.nc
    tab = k.s[:, 0:4 * D].rearrange("p (c j n) -> p c j n", c=2, j=2)
    with Stage(nc) as ctx:
        s_t, s_d, = sems(nc, ctx, "table_loaded mod_steps")
        blk = ctx.enter_context(nc.Block())

        @blk.sync
        def _(sp):
            for cnd in range(2):
                for j in range(2):
                    table_load(k, sp, s_t, tab[:, cnd, j, :], layer, cnd, j)

        @blk.vector
        def _(dve):
            st = Steps(dve, s_d)
            dve.wait_ge(s_t, 64)
            for cnd in range(2):
                st.mark(nc.vector.tensor_scalar(tab[:, cnd, 1, :], tab[:, cnd, 1, :], 1.0, None, ALU.add))
            st.wait()
            for t in range(TILES):
                st.mark(nc.vector.tensor_tensor(k.hP[:, t, :], k.x[:, t, :], tab[:, min(t, 1), 1, :], ALU.mult))
            st.wait()
            for t in range(TILES):
                st.mark(nc.vector.tensor_tensor(k.hP[:, t, :], k.hP[:, t, :], tab[:, min(t, 1), 0, :], ALU.add))


def stage_transpose(k, src, ahead=None):
    nc = k.nc
    with Stage(nc) as ctx:
        s_tr, s_a, s_v = sems(nc, ctx, "turned copied_act copied_dve")
        blk = ctx.enter_context(nc.Block())
        n_banks = TILES * KT // 4

        @blk.sync
        def _(sp):
            if ahead:
                ahead(sp)

        @blk.tensor
        def _(pe):
            for b in range(n_banks):
                t, g = divmod(b, 2)
                for j in range(4):
                    kk = 4 * g + j
                    m = nc.tensor.transpose(k.ps[b][:, j * P:(j + 1) * P], src[:, t, kk * P:(kk + 1) * P], k.ident)
                m.then_inc(s_tr, 1)

        def copy(eng_copy, eng, sem, which):
            for b in range(which, n_banks, 2):
                t, g = divmod(b, 2)
                eng.wait_ge(s_tr, b + 1)
                eng_copy(k.hT[:, 4 * g:4 * g + 4, t * P:(t + 1) * P],
                         k.ps[b][:].rearrange("p (j n) -> p j n", j=4)).then_inc(sem, 1)

        @blk.scalar
        def _(act):
            copy(nc.scalar.copy, act, s_a, 0)

        @blk.vector
        def _(dve):
            copy(nc.vector.tensor_copy, dve, s_v, 1)


def ring_slot(k, i):
    return k.ring[:, i * 4096:(i + 1) * 4096].rearrange("p (k n) -> p k n", k=KT)


def chunks_of(n_cols):
    return [(c, min(512, n_cols - c)) for c in range(0, n_cols, 512)]


def early_slot(k):
    return k.s[:, 15104 - 4096:15104].rearrange("p (k n) -> p k n", k=KT)


def out_chunk(k, w, c):
    def ahead(sp):
        k.load_ahead(sp, c, (early_slot(k), ring_slot(k, 1))[c], w.rearrange("(k p) n -> p k n", p=P)[:, :, c * 512:(c + 1) * 512])
    return ahead


def first_chunks(k, w):
    def ahead(sp):
        for i, (c, n) in enumerate(chunks_of(w.shape[1])[:3]):
            k.load_ahead(sp, i, ring_slot(k, i)[:, :, 0:n], w.rearrange("(k p) n -> p k n", p=P)[:, :, c:c + n])
    return ahead


def stage_project(k, w, n_cols, out):
    nc = k.nc
    chunks = chunks_of(n_cols)
    with Stage(nc) as ctx:
        s_mm, s_a, s_v = sems(nc, ctx, "product_ready copied_act copied_dve")
        s_w = sems(nc, ctx, "w0_loaded w1_loaded w2_loaded")
        blk = ctx.enter_context(nc.Block())

        @blk.sync
        def _(sp):
            for i, (c, n) in enumerate(chunks[3:]):
                sp.wait_ge(s_mm, TILES * (i + 1))
                sp.dma_start(ring_slot(k, i % 3)[:, :, 0:n], w.rearrange("(k p) n -> p k n", p=P)[:, :, c:c + n]).then_inc(s_w[i % 3], 16)

        @blk.tensor
        def _(pe):
            for i, (c, n) in enumerate(chunks):
                if i < 3:
                    k.arrived(pe, i)
                else:
                    pe.wait_ge(s_w[i % 3], 16 * (i // 3))
                for t in range(TILES):
                    b = i * TILES + t
                    if b >= 8:
                        pe.wait_ge(s_v if b % 2 else s_a, (b - 8) // 2 + 1)
                    for kk in range(KT):
                        m = nc.tensor.matmul(k.ps[b % 8][:, 0:n], k.hT[:, kk, t * P:(t + 1) * P], ring_slot(k, i % 3)[:, kk, 0:n],
                                             start=(kk == 0), stop=(kk == KT - 1))
                    m.then_inc(s_mm, 1)

        def copy(eng_copy, eng, sem, which):
            for b in range(which, len(chunks) * TILES, 2):
                i, t = divmod(b, TILES)
                c, n = chunks[i]
                eng.wait_ge(s_mm, b + 1)
                eng_copy(out(t, c, n), k.ps[b % 8][:, 0:n]).then_inc(sem, 1)

        @blk.scalar
        def _(act):
            copy(nc.scalar.copy, act, s_a, 0)

        @blk.vector
        def _(dve):
            copy(nc.vector.tensor_copy, dve, s_v, 1)


def rope(nc, st, k, at, tile, x, tmp, heads, nf):
    o = at + tile * 4 * nf
    cos = k.const[:, o:o + 2 * nf].rearrange("p (a f) -> p a f", a=2)
    sin = k.const[:, o + 2 * nf:o + 4 * nf].rearrange("p (a f) -> p a f", a=2)
    n = heads * 2 * nf
    t1, t2, t3, t4 = (tmp[:, i * n:(i + 1) * n].rearrange("p (h a f) -> p h a f", a=2, f=nf) for i in range(4))
    for axis in range(2):
        cb = cos[:, axis:axis + 1, :].to_broadcast([P, heads, nf])
        sb = sin[:, axis:axis + 1, :].to_broadcast([P, heads, nf])
        x1, x2 = x[:, :, axis, 0, :], x[:, :, axis, 1, :]
        st.mark(nc.vector.tensor_tensor(t1[:, :, axis, :], x1, cb, ALU.mult))
        st.mark(nc.vector.tensor_tensor(t2[:, :, axis, :], x2, sb, ALU.mult))
        st.mark(nc.vector.tensor_tensor(t3[:, :, axis, :], x2, cb, ALU.mult))
        st.mark(nc.vector.tensor_tensor(t4[:, :, axis, :], x1, sb, ALU.mult))
    st.wait()
    for axis in range(2):
        x1, x2 = x[:, :, axis, 0, :], x[:, :, axis, 1, :]
        st.mark(nc.vector.tensor_tensor(x1, t1[:, :, axis, :], t2[:, :, axis, :], ALU.subtract))
        st.mark(nc.vector.tensor_tensor(x2, t3[:, :, axis, :], t4[:, :, axis, :], ALU.add))
    st.wait()


def stage_mla_norm(k, e):
    nc, io = k.nc, k.io
    z = k.z[:].rearrange("p (t n) -> p t n", t=TILES)
    m = k.mla
    tmp = k.s[:, 14080:14080 + 1024]
    with Stage(nc) as ctx:
        s_l, s_sq, s_d, s_p, s_out = sems(nc, ctx, "norm_loaded squares_summed dve_steps rstd_ready outputs_stored")
        s_ms = sems(nc, ctx, "mean_squares")[0]
        s_n = sems(nc, ctx, "normed")[0]
        blk = ctx.enter_context(nc.Block())

        @blk.sync
        def _(sp):
            sp.dma_start(m["qg"], io["mla_q_norm"][e:e + 1, :].to_broadcast([P, Q_RANK])).then_inc(s_l, 16)
            sp.dma_start(m["kvg"], io["mla_kv_norm"][e:e + 1, :].to_broadcast([P, KV_RANK])).then_inc(s_l, 16)
            sp.dma_start(m["ckv"][:, 3, :], io["cache_mla_ckv"][0, e]).then_inc(s_l, 16)
            sp.dma_start(m["kpe"][:, 3, NOPE:QK], io["cache_mla_kpe"][0, e]).then_inc(s_l, 16)
            k.load_ahead(sp, 0, m["wuq"], io["mla_w_uq"][e].rearrange("(k p) n -> p k n", p=P))
            k.load_ahead(sp, 1, m["wuk"], io["mla_w_uk"][e])
            k.load_ahead(sp, 1, m["wuv"], io["mla_w_uv"][e])
            sp.wait_ge(s_n, 1)
            sp.dma_start(io["new_mla_ckv"][0, e], m["ckv"][:, 0, :]).then_inc(s_out, 16)
            sp.dma_start(io["new_mla_kpe"][0, e], z[:, 0, Z_PE:Z_RQ]).then_inc(s_out, 16)
            sp.wait_ge(s_out, 32)
            sp.wait_ge(s_l, 64)

        @blk.scalar
        def _(act):
            for t in range(TILES):
                nc.scalar.activation(m["junk"][:, 0:Q_RANK], z[:, t, 0:Z_KV], ACT.Square, accum_out=m["ss"][:, t:t + 1]).then_inc(s_sq, 1)
                act.wait_ge(s_sq, 2 * t + 1)
                nc.scalar.activation(m["junk"][:, 0:KV_RANK], z[:, t, Z_KV:Z_PE], ACT.Square, accum_out=m["ss"][:, 3 + t:4 + t]).then_inc(s_sq, 1)
                act.wait_ge(s_sq, 2 * t + 2)

        @blk.gpsimd
        def _(pool):
            pool.wait_ge(s_ms, 2)
            nc.gpsimd.tensor_tensor(m["rstd"], m["ss"], m["half"], ALU.pow).then_inc(s_p, 1)

        @blk.vector
        def _(dve):
            st = Steps(dve, s_d)
            st.mark(nc.vector.memset(m["half"], -0.5))
            st.mark(nc.vector.memset(m["kpe"][:, :, 0:NOPE], 0.0))
            st.wait()
            dve.wait_ge(s_sq, 2 * TILES)
            nc.vector.tensor_scalar(m["ss"][:, 0:3], m["ss"][:, 0:3], 1.0 / Q_RANK, RMS_EPS, ALU.mult, ALU.add).then_inc(s_ms, 1)
            nc.vector.tensor_scalar(m["ss"][:, 3:6], m["ss"][:, 3:6], 1.0 / KV_RANK, RMS_EPS, ALU.mult, ALU.add).then_inc(s_ms, 1)
            dve.wait_ge(s_p, 1)
            dve.wait_ge(s_l, 64)
            for t in range(TILES):
                st.mark(nc.vector.scalar_tensor_tensor(m["qn"][:, t, :], z[:, t, 0:Z_KV], m["rstd"][:, t:t + 1], m["qg"], ALU.mult, ALU.mult))
                st.mark(nc.vector.scalar_tensor_tensor(m["ckv"][:, t, :], z[:, t, Z_KV:Z_PE], m["rstd"][:, 3 + t:4 + t], m["kvg"], ALU.mult, ALU.mult))
            st.mark(nc.vector.tensor_copy(m["kpe"][:, 0, NOPE:QK], z[:, 0, Z_PE:Z_RQ]))
            st.wait()
            nc.vector.memset(m["junk"][:, 0:1], 0.0).then_inc(s_n, 1)
            for t in (1, 2):
                x = z[:, t, Z_PE:Z_RQ].rearrange("p (h a b f) -> p h a b f", h=1, a=2, b=2)
                rope(nc, st, k, C_ROPE_E, t - 1, x, tmp, 1, ROPE // 4)
                st.then(nc.vector.tensor_copy(m["kpe"][:, t, NOPE:QK], z[:, t, Z_PE:Z_RQ]))


def stage_mla_keys(k, e):
    nc = k.nc
    m = k.mla
    tmp = k.s[:, 14080:14080 + 1024]
    with Stage(nc) as ctx:
        s_tr, s_a, s_v, s_d = sems(nc, ctx, "pe_ready copied_act copied_dve dve_steps")
        blk = ctx.enter_context(nc.Block())

        @blk.tensor
        def _(pe):
            for t in range(4):
                mm = nc.tensor.transpose(k.ps[0][:, t * P:(t + 1) * P], m["ckv"][:, t, :], k.ident)
            mm.then_inc(s_tr, 1)
            for t in range(4):
                mm = nc.tensor.transpose(k.ps[1][0:QK, t * P:(t + 1) * P], m["kpe"][:, t, :], k.ident)
            mm.then_inc(s_tr, 1)
            for j in range(2):
                for t in range(TILES):
                    mm = nc.tensor.transpose(k.ps[2 + j][:, t * P:(t + 1) * P], m["qn"][:, t, j * P:(j + 1) * P], k.ident)
                mm.then_inc(s_tr, 1)
            k.arrived(pe, 0)
            pe.wait_ge(s_v, 2)
            for t in range(TILES):
                for j, (c, n) in enumerate(((0, 512), (512, 256))):
                    i = 2 * t + j
                    if i >= 2:
                        pe.wait_ge(s_v, 2 + i - 1)
                    for kk in range(2):
                        mm = nc.tensor.matmul(k.ps[4 + j][:, 0:n], m["qnT"][:, kk, t * P:(t + 1) * P], m["wuq"][:, kk, c:c + n],
                                              start=(kk == 0), stop=(kk == 1))
                    mm.then_inc(s_tr, 1)
            k.arrived(pe, 1)
            pe.wait_ge(s_a, 1)
            for h in range(HEADS):
                if h >= 2:
                    pe.wait_ge(s_a, 2 + h - 1)
                nc.tensor.matmul(k.ps[6 + h % 2][0:NOPE, :], m["wuk"][:, h * NOPE:(h + 1) * NOPE], m["ckvT"], start=True, stop=True).then_inc(s_tr, 1)
            pe.wait_ge(s_a, 2)
            pe.wait_ge(s_v, 2)
            for t in range(4):
                nc.tensor.matmul(k.ps[t][:], m["ckvT"][:, t * P:(t + 1) * P], m["wuv"], start=True, stop=True).then_inc(s_tr, 1)

        @blk.scalar
        def _(act):
            act.wait_ge(s_tr, 1)
            nc.scalar.copy(m["ckvT"], k.ps[0][:]).then_inc(s_a, 1)
            act.wait_ge(s_tr, 2)
            nc.scalar.copy(m["kpeT"][NOPE:QK, :], k.ps[1][NOPE:QK, :]).then_inc(s_a, 1)
            for h in range(HEADS):
                act.wait_ge(s_tr, 11 + h)
                nc.scalar.copy(m["kT"][0:NOPE, h, :], k.ps[6 + h % 2][0:NOPE, :]).then_inc(s_a, 1)
            for t in range(4):
                act.wait_ge(s_tr, 19 + t)
                nc.scalar.copy(m["v"][:, t, :], k.ps[t][:]).then_inc(s_a, 1)

        @blk.vector
        def _(dve):
            st = Steps(dve, s_d)
            for j in range(2):
                dve.wait_ge(s_tr, 3 + j)
                nc.vector.tensor_copy(m["qnT"][:, j, :], k.ps[2 + j][:, 0:TOK]).then_inc(s_v, 1)
            for t in range(TILES):
                for j, (c, n) in enumerate(((0, 512), (512, 256))):
                    dve.wait_ge(s_tr, 5 + 2 * t + j)
                    nc.vector.tensor_copy(m["q"][:, t, c:c + n], k.ps[4 + j][:, 0:n]).then_inc(s_v, 1)
            dve.wait_ge(s_a, 2)
            st.mark(nc.vector.tensor_copy(m["kT"][NOPE:QK, :, :], m["kpeT"][NOPE:QK, :].rearrange("p (o n) -> p o n", o=1).to_broadcast([ROPE, HEADS, 512])))
            dve.wait_ge(s_v, 2 + 2 * TILES)
            for t in (1, 2):
                x = m["q"][:, t, :].rearrange("p (h d) -> p h d", h=HEADS)[:, :, NOPE:QK].rearrange("p h (a b f) -> p h a b f", a=2, b=2)
                rope(nc, st, k, C_ROPE_E, t - 1, x, tmp, HEADS, ROPE // 4)


def stage_turn_heads(k, jobs, dim):
    nc = k.nc
    with Stage(nc) as ctx:
        s_tr, s_a, s_v = sems(nc, ctx, "turned copied_act copied_dve")
        blk = ctx.enter_context(nc.Block())

        @blk.tensor
        def _(pe):
            for b, (srcs, _) in enumerate(jobs):
                if b >= 8:
                    pe.wait_ge(s_v if b % 2 else s_a, (b - 8) // 2 + 1)
                for j, src in enumerate(srcs):
                    m = nc.tensor.transpose(k.ps[b % 8][0:dim, j * P:(j + 1) * P], src, k.ident)
                m.then_inc(s_tr, 1)

        def copy(eng_copy, eng, sem, which):
            for b in range(which, len(jobs), 2):
                eng.wait_ge(s_tr, b + 1)
                srcs, dst = jobs[b]
                eng_copy(dst, k.ps[b % 8][0:dim, 0:len(srcs) * P].rearrange("p (j n) -> p j n", n=P)).then_inc(sem, 1)

        @blk.scalar
        def _(act):
            copy(nc.scalar.copy, act, s_a, 0)

        @blk.vector
        def _(dve):
            copy(nc.vector.tensor_copy, dve, s_v, 1)


def stage_attention(k, heads, scale, ahead=None):
    nc = k.nc
    N = len(heads)
    o = 0
    pr = k.s[:, o:o + 3 * TOK].rearrange("p (b n) -> p b n", b=3)
    o += 3 * TOK
    pt = k.s[:, o:o + 2 * TOK].rearrange("p (b n) -> p b n", b=2)
    o += 2 * TOK
    sc = k.s[:, o:o + 2 * TOK].rearrange("p (b n) -> p b n", b=2)
    o += 2 * TOK
    st_ = k.s[:, o:o + 5 * N]
    mx, nb, sm, si, rc = (st_[:, i * N:(i + 1) * N] for i in range(5))
    with Stage(nc) as ctx:
        s_s, s_mx, s_e, s_t, s_pt, s_o, s_se, s_out, s_d = sems(
            nc, ctx, "scores_ready max_ready probs_ready turned probsT_ready sums_ready sink_exp out_ready dve_steps")
        blk = ctx.enter_context(nc.Block())

        @blk.sync
        def _(sp):
            if ahead:
                ahead(sp)

        @blk.tensor
        def _(pe):
            for i in range(N + 2):
                if i < N:
                    h = heads[i]
                    n = h["keys"].shape[1]
                    if i >= 3:
                        pe.wait_ge(s_e, i - 2)
                    nc.tensor.matmul(k.ps[i % 3][:, 0:n], h["q"], h["keys"], start=True, stop=True).then_inc(s_s, 1)
                if 1 <= i <= N:
                    j = i - 1
                    n = heads[j]["keys"].shape[1]
                    pe.wait_ge(s_e, j + 1)
                    if j >= 2:
                        pe.wait_ge(s_pt, j - 1)
                    for c in range(n // P):
                        m = nc.tensor.transpose(k.ps[3 + j % 2][:, c * P:(c + 1) * P], pr[:, j % 3, c * P:(c + 1) * P], k.ident)
                    m.then_inc(s_t, 1)
                if i >= 2:
                    j = i - 2
                    h = heads[j]
                    n = h["keys"].shape[1]
                    pe.wait_ge(s_pt, j + 1)
                    if j >= 2:
                        pe.wait_ge(s_out, j - 1)
                    for c in range(n // P):
                        m = nc.tensor.matmul(k.ps[5 + j % 2][:, 0:VD], pt[:, j % 2, c * P:(c + 1) * P], h["v"][c],
                                             start=(c == 0), stop=(c == n // P - 1))
                    m.then_inc(s_o, 1)

        @blk.scalar
        def _(act):
            for i in range(N + 1):
                if i < N:
                    n = heads[i]["keys"].shape[1]
                    act.wait_ge(s_mx, i + 1)
                    if i >= 3:
                        act.wait_ge(s_t, i - 2)
                    if heads[i].get("sink") is not None:
                        nc.scalar.activation(si[:, i:i + 1], heads[i]["sink"], ACT.Exp, bias=nb[:, i:i + 1]).then_inc(s_se, 1)
                    src = sc[:, i % 2, 0:n] if heads[i].get("mask") is not None else k.ps[i % 3][:, 0:n]
                    sl = 1.0 if heads[i].get("mask") is not None else scale
                    nc.scalar.activation(pr[:, i % 3, 0:n], src, ACT.Exp, bias=nb[:, i:i + 1], scale=sl,
                                         accum_out=sm[:, i:i + 1]).then_inc(s_e, 1)
                if i >= 1:
                    j = i - 1
                    n = heads[j]["keys"].shape[1]
                    act.wait_ge(s_t, j + 1)
                    if j >= 2:
                        act.wait_ge(s_o, j - 1)
                    nc.scalar.copy(pt[:, j % 2, 0:n], k.ps[3 + j % 2][:, 0:n]).then_inc(s_pt, 1)

        @blk.vector
        def _(dve):
            st = Steps(dve, s_d)
            for i in range(N + 2):
                if i < N:
                    h = heads[i]
                    n = h["keys"].shape[1]
                    dve.wait_ge(s_s, i + 1)
                    src, sl = k.ps[i % 3][:, 0:n], scale
                    if h.get("mask") is not None:
                        if i >= 2:
                            dve.wait_ge(s_e, i - 1)
                        st.then(nc.vector.scalar_tensor_tensor(sc[:, i % 2, 0:n], src, scale, h["mask"], ALU.mult, ALU.add))
                        src, sl = sc[:, i % 2, 0:n], 1.0
                    st.then(nc.vector.tensor_reduce(mx[:, i:i + 1], src, AX.X, ALU.max))
                    if h.get("sink") is not None:
                        st.then(nc.vector.tensor_scalar(mx[:, i:i + 1], mx[:, i:i + 1], sl, h["sink"], ALU.mult, ALU.max))
                        sl = 1.0
                    nc.vector.tensor_scalar(nb[:, i:i + 1], mx[:, i:i + 1], -sl, None, ALU.mult).then_inc(s_mx, 1)
                if i >= 2:
                    j = i - 2
                    h = heads[j]
                    dve.wait_ge(s_e, j + 1)
                    if h.get("sink") is not None:
                        dve.wait_ge(s_se, j + 1)
                        st.then(nc.vector.tensor_tensor(sm[:, j:j + 1], sm[:, j:j + 1], si[:, j:j + 1], ALU.add))
                    st.then(nc.vector.reciprocal(rc[:, j:j + 1], sm[:, j:j + 1]))
                    dve.wait_ge(s_o, j + 1)
                    nc.vector.tensor_scalar(h["out"], k.ps[5 + j % 2][:, 0:VD], rc[:, j:j + 1], None, ALU.mult).then_inc(s_out, 1)


def stage_retention(k, e, ahead):
    nc, io = k.nc, k.io
    z = k.z[:].rearrange("p (t n) -> p t n", t=TILES)
    R = k.ring
    qT = R[0:RD, 0:3072].rearrange("p (t h n) -> p t h n", t=TILES, h=RH)
    kT = R[0:RD, 3072:6144].rearrange("p (t h n) -> p t h n", t=TILES, h=RH)
    qd = R[0:RD, 6144:10240].rearrange("p (d t h n) -> p d t h n", d=2, t=2, h=RH)
    kd = R[:, 10240:12288].rearrange("p (j n) -> p j n", j=4)
    o = 0

    def cut(n, p=P):
        nonlocal o
        o += n
        return k.s[0:p, o - n:o]

    lg = cut(16)
    kdec = cut(16).rearrange("p (d h) -> p d h", d=2)
    cdec = cut(16)
    DT = cut(2 * RH * P).rearrange("p (d h n) -> p d h n", d=2, h=RH)
    qdec = cut(2 * RH * P, RD).rearrange("p (d h n) -> p d h n", d=2, h=RH)
    S0 = cut(2 * RW, RD).rearrange("p (d n) -> p d n", d=2)
    S1 = cut(4 * RW, RD).rearrange("p (j n) -> p j n", j=4)
    AT = cut(4 * P).rearrange("p (b d n) -> p b d n", b=2, d=2)
    gn = cut(RW)
    raw = cut(2 * RW).rearrange("p (d n) -> p d n", d=2)
    sq = cut(RW)
    stat = cut(64)
    half = cut(32)
    gate = cut(RW)
    assert o <= 15104 - 4096, o
    STATES = ((0, 0), (1, 0), (0, 1), (1, 2))
    with Stage(nc) as ctx:
        s_l, s_g, s_dec, s_d, s_p, s_pw, s_st, s_sc, s_store, s_ss = sems(
            nc, ctx, "params_loaded act_steps decays_ready dve_steps rstd_ready var_ready state_ready state_copied states_stored states_scaled")
        s_at, s_am, s_o, s_or, s_gt, s_q = sems(nc, ctx, "attn_ready attn_masked out_summed out_read gate_exp q_decayed")
        blk = ctx.enter_context(nc.Block())

        @blk.sync
        def _(sp):
            for d, n in enumerate(("ret_decay_fwd", "ret_decay_bwd")):
                sp.dma_start(lg[:, d * RH:(d + 1) * RH], io[n][e:e + 1, :].to_broadcast([P, RH])).then_inc(s_l, 16)
            sp.dma_start(gn, io["ret_gn_g"][e:e + 1, :].to_broadcast([P, RW])).then_inc(s_l, 16)
            for d, n in enumerate(("state_ret_fwd", "state_ret_bwd")):
                sp.dma_start(S0[:, d, :].rearrange("p (h n) -> p h n", h=RH), io[n][0, e].rearrange("h d n -> d h n")).then_inc(s_l, 16)
            ahead(sp)
            sp.wait_ge(s_ss, 2)
            for d, n in enumerate(("new_ret_fwd", "new_ret_bwd")):
                sp.dma_start(io[n][0, e].rearrange("h d n -> d h n"), S1[:, d, :].rearrange("p (h n) -> p h n", h=RH)).then_inc(s_store, 16)
            sp.wait_ge(s_store, 32)

        @blk.scalar
        def _(act):
            st = Steps(act, s_g)
            act.wait_ge(s_l, 80)
            st.then(nc.scalar.activation(lg, lg, ACT.Exp, scale=-1.0))
            st.then(nc.scalar.activation(lg, lg, ACT.Ln, bias=1.0))
            st.then(nc.scalar.mul(lg, lg, -1.0))
            for d in range(2):
                nc.scalar.activation(kdec[:, d, :], lg[:, d * RH:(d + 1) * RH], ACT.Exp, scale=k.const[:, C_COL + d:C_COL + d + 1]).then_inc(s_dec, 1)
                nc.scalar.activation(cdec[:, d * RH:(d + 1) * RH], lg[:, d * RH:(d + 1) * RH], ACT.Exp, scale=float(P)).then_inc(s_dec, 1)
                for h in range(RH):
                    col = lg[:, d * RH + h:d * RH + h + 1]
                    nc.scalar.activation(DT[:, d, h, :], k.c((C_DF, C_DB)[d], P), ACT.Exp, scale=col).then_inc(s_dec, 1)
                    nc.scalar.activation(qdec[:, d, h, :], k.c((C_QF, C_QB)[d], P, RD), ACT.Exp, scale=col[0:RD]).then_inc(s_dec, 1)
            for t in range(TILES):
                if t:
                    act.wait_ge(s_q, 2 + t)
                nc.scalar.activation(gate, z[:, t, Z_RG:EVEN_IN], ACT.Exp, scale=-1.0).then_inc(s_gt, 1)

        @blk.gpsimd
        def _(pool):
            for i in range(2 * TILES):
                pool.wait_ge(s_pw, i + 1)
                c = stat[:, 16 + 8 * (i % 2):24 + 8 * (i % 2)]
                nc.gpsimd.tensor_tensor(c, c, half[:, 0:8], ALU.pow).then_inc(s_p, 1)

        @blk.tensor
        def _(pe):
            pe.wait_ge(s_sc, 1)
            for j, (d, t) in enumerate(STATES):
                for h in range(RH):
                    m = nc.tensor.matmul(k.ps[j][0:RD, h * RD:(h + 1) * RD], kd[:, j, h * RD:(h + 1) * RD],
                                         z[:, t, Z_RV + h * RD:Z_RV + (h + 1) * RD], start=True, stop=True)
                m.then_inc(s_st, 1)
            pe.wait_ge(s_ss, 4)
            pe.wait_ge(s_q, 2)
            for i in range(TILES * RH + 1):
                if i < TILES * RH:
                    t, h = divmod(i, RH)
                    if i >= 2:
                        pe.wait_ge(s_am, 2 * (i - 1))
                    nc.tensor.matmul(k.ps[i % 2][:, 0:P], kT[:, t, h, :], qT[:, t, h, :], start=True, stop=True).then_inc(s_at, 1)
                if i >= 1:
                    j = i - 1
                    t, h = divmod(j, RH)
                    pe.wait_ge(s_am, 2 * (j + 1))
                    if h == 0 and t:
                        pe.wait_ge(s_or, 2 * t)
                    v = z[:, t, Z_RV + h * RD:Z_RV + (h + 1) * RD]
                    for d in range(2):
                        out = k.ps[4 + d][:, h * RD:(h + 1) * RD]
                        m = nc.tensor.matmul(out, AT[:, j % 2, d, :], v, start=True, stop=(t == 0))
                        if t:
                            first = (t == 1) == (d == 0)
                            S = S0[:, d, :] if first else S1[:, 2 + d, :]
                            m = nc.tensor.matmul(out, qd[:, d, t - 1, h, :], S[:, h * RD:(h + 1) * RD], start=False, stop=True)
                    m.then_inc(s_o, 1)

        @blk.vector
        def _(dve):
            st = Steps(dve, s_d)
            st.mark(nc.vector.memset(half, -0.5))
            dve.wait_ge(s_dec, 2 * (2 + 2 * RH))
            for j, (d, t) in enumerate(STATES):
                kv = z[:, t, Z_RK:Z_RV].rearrange("p (h n) -> p h n", h=RH)
                st.mark(nc.vector.tensor_tensor(kd[:, j, :].rearrange("p (h n) -> p h n", h=RH), kv,
                                                kdec[:, d, :].rearrange("p (h o) -> p h o", o=1).to_broadcast([P, RH, RD]), ALU.mult))
            st.wait()
            nc.vector.tensor_scalar(kd, kd, RD ** -0.5, None, ALU.mult).then_inc(s_sc, 1)
            for d in range(2):
                st.mark(nc.vector.tensor_tensor(DT[:, d], DT[:, d], k.c((C_MF, C_MB)[d], P).rearrange("p (o n) -> p o n", o=1).to_broadcast([P, RH, P]), ALU.mult))
            for d in range(2):
                for t in range(2):
                    m = nc.vector.tensor_tensor(qd[:, d, t], qT[:, t + 1], qdec[:, d], ALU.mult)
                    st.mark(m)
            st.wait()
            nc.vector.memset(stat[:, 48:49], 0.0).then_inc(s_q, 2)
            for j, (d, t) in enumerate(STATES):
                dve.wait_ge(s_st, j + 1)
                if t == 0:
                    nc.vector.tensor_copy(S1[:, j, :], k.ps[j][0:RD, :]).then_inc(s_ss, 1)
                else:
                    sv = S1[:, j, :].rearrange("p (h n) -> p h n", h=RH)
                    st.then(nc.vector.tensor_tensor(sv, S0[:, d, :].rearrange("p (h n) -> p h n", h=RH),
                                                    cdec[0:RD, d * RH:(d + 1) * RH].rearrange("p (h o) -> p h o", o=1).to_broadcast([RD, RH, RD]), ALU.mult))
                    nc.vector.tensor_tensor(S1[:, j, :], S1[:, j, :], k.ps[j][0:RD, :], ALU.add).then_inc(s_ss, 1)

            def norm(t):
                for d in range(2):
                    x = raw[:, d, :]
                    xv = x.rearrange("p (h n) -> p h n", h=RH)
                    sv = sq.rearrange("p (h n) -> p h n", h=RH)
                    mu, var = stat[:, 0:8], stat[:, 16 + 8 * d:24 + 8 * d]
                    st.mark(nc.vector.tensor_copy(x, k.ps[4 + d][:]))
                    st.wait()
                    nc.vector.memset(stat[:, 49:50], 0.0).then_inc(s_or, 1)
                    st.then(nc.vector.tensor_reduce(mu, xv, AX.X, ALU.add))
                    st.then(nc.vector.tensor_scalar(mu, mu, 1.0 / RD, None, ALU.mult))
                    st.then(nc.vector.tensor_tensor(xv, xv, mu.rearrange("p (h o) -> p h o", o=1).to_broadcast([P, RH, RD]), ALU.subtract))
                    st.then(nc.vector.tensor_tensor(sq, x, x, ALU.mult))
                    st.then(nc.vector.tensor_reduce(var, sv, AX.X, ALU.add))
                    nc.vector.tensor_scalar(var, var, 1.0 / RD, LN_EPS, ALU.mult, ALU.add).then_inc(s_pw, 1)
                for d in range(2):
                    xv = raw[:, d, :].rearrange("p (h n) -> p h n", h=RH)
                    var = stat[:, 16 + 8 * d:24 + 8 * d]
                    dve.wait_ge(s_p, 2 * t + d + 1)
                    st.mark(nc.vector.tensor_tensor(xv, xv, var.rearrange("p (h o) -> p h o", o=1).to_broadcast([P, RH, RD]), ALU.mult))
                st.wait()
                st.then(nc.vector.tensor_tensor(sq, raw[:, 0, :], raw[:, 1, :], ALU.add))
                st.then(nc.vector.tensor_tensor(sq, sq, gn, ALU.mult))
                dve.wait_ge(s_gt, t + 1)
                st.then(nc.vector.tensor_scalar(gate, gate, 1.0, None, ALU.add))
                st.then(nc.vector.reciprocal(gate, gate))
                st.then(nc.vector.tensor_tensor(sq, sq, gate, ALU.mult))
                st.then(nc.vector.tensor_tensor(k.cat[:, t, HEADS * VD:D], sq, z[:, t, Z_RG:EVEN_IN], ALU.mult))
                nc.vector.memset(stat[:, 50:51], 0.0).then_inc(s_q, 1)

            for i in range(TILES * RH):
                t, h = divmod(i, RH)
                dve.wait_ge(s_at, i + 1)
                if i >= 2:
                    dve.wait_ge(s_o, i - 1)
                for d in range(2):
                    nc.vector.scalar_tensor_tensor(AT[:, i % 2, d, :], k.ps[i % 2][:, 0:P], RD ** -0.5, DT[:, d, h, :], ALU.mult, ALU.mult).then_inc(s_am, 1)
                if h == RH - 1:
                    dve.wait_ge(s_o, i + 1)
                    norm(t)


def retention_jobs(k):
    z = k.z[:].rearrange("p (t n) -> p t n", t=TILES)
    R = k.ring
    jobs = []
    for base, at in ((Z_RQ, 0), (Z_RK, 3072)):
        dst = R[0:RD, at:at + 3072].rearrange("p (t h n) -> p t h n", t=TILES, h=RH)
        for t in range(TILES):
            for g in range(2):
                jobs.append(([z[:, t, base + (4 * g + j) * RD:base + (4 * g + j + 1) * RD] for j in range(4)], dst[:, t, 4 * g:4 * g + 4, :]))
    return jobs


def stage_swa_prep(k, o):
    nc, io = k.nc, k.io
    z = k.zo
    tmp = k.s[:, 0:4 * SH * SD // 2]
    with Stage(nc) as ctx:
        s_l, s_d, s_out = sems(nc, ctx, "context_loaded dve_steps outputs_stored")
        blk = ctx.enter_context(nc.Block())

        @blk.sync
        def _(sp):
            sp.dma_start(k.kctx, io["cache_swa_k"][0, o].rearrange("s h d -> s (h d)")).then_inc(s_l, 16)
            sp.dma_start(k.vctx, io["cache_swa_v"][0, o].rearrange("s h d -> s (h d)")).then_inc(s_l, 16)
            sp.dma_start(k.sink, io["swa_sink"][o:o + 1, :].to_broadcast([P, SH])).then_inc(s_l, 16)
            sp.dma_start(io["new_swa_k"][0, o].rearrange("s h d -> s (h d)"), z[:, 0, SQ_DIM:SQ_DIM + SKV_DIM]).then_inc(s_out, 16)
            sp.dma_start(io["new_swa_v"][0, o].rearrange("s h d -> s (h d)"), z[:, 0, SQ_DIM + SKV_DIM:ODD_IN]).then_inc(s_out, 16)
            sp.wait_ge(s_l, 48)
            sp.wait_ge(s_out, 32)

        @blk.vector
        def _(dve):
            st = Steps(dve, s_d)
            for t in (1, 2):
                for at, hh in ((0, SH), (SQ_DIM, SKV)):
                    x = z[:, t, at:at + hh * SD].rearrange("p (h a b f) -> p h a b f", h=hh, a=2, b=2)
                    rope(nc, st, k, C_ROPE_O, t - 1, x, tmp, hh, SD // 4)


class NormBuffers:

    def __init__(self, k, which):
        self.T = k.z[:, 0:6 * D].rearrange("p (c j n) -> p c j n", c=2, j=3)
        self.tmp = k.z[:, 6 * D:7 * D]
        o = 7 * D
        self.stats = k.z[:, o:o + 12 * TILES].rearrange("p (t j n) -> p t j n", t=TILES, j=2)
        self.mv = k.z[:, o + 48:o + 48 + 2 * TILES].rearrange("p (t n) -> p t n", t=TILES)
        self.half = k.z[:, o + 60:o + 61]
        o = (7168, 8192)[which - 1]
        self.n = k.s[:, o:o + TILES * D].rearrange("p (t n) -> p t n", t=TILES)
        self.gb = k.cat[:, 0:2, :] if which == 1 else k.s[:, 12288:12288 + 2 * D].rearrange("p (j n) -> p j n", j=2)


def load_norm_tables(k, eng, layer, which, s_gate, s_tab):
    M = NormBuffers(k, which)
    for cnd in range(2):
        table_load(k, eng, s_gate, M.T[:, cnd, 0, :], layer, cnd, (2, 5)[which - 1])
    for j, n in enumerate("gb"):
        eng.dma_start(M.gb[:, j, :], k.io[f"ln{which}_{n}"][layer:layer + 1, :].to_broadcast([P, D])).then_inc(s_tab, 16)
    if which == 1 or layer + 1 < DEPTH:
        for cnd in range(2):
            for j in range(2):
                at = (layer, 3 + j) if which == 1 else (layer + 1, j)
                table_load(k, eng, s_tab, M.T[:, cnd, 1 + j, :], at[0], cnd, at[1])


def fold_steps(M, eng, c, bs):
    tt = eng.tensor_tensor
    g, b = M.gb[:, 0, :], M.gb[:, 1, :]
    shift, scale = M.T[:, c, 1, :], M.T[:, c, 2, :]
    return [lambda: tt(shift, shift, b, ALU.add), lambda: tt(bs, b, scale, ALU.mult), lambda: tt(shift, shift, bs, ALU.add),
            lambda: tt(scale, scale, g, ALU.mult), lambda: tt(scale, scale, g, ALU.add)]


def dve_stats(k, M, st, t, halves):
    for j in halves:
        st.then(k.nc.vector.bn_stats(M.stats[:, t, j, :], k.x[:, t, j * 512:(j + 1) * 512]))


def dve_variance(k, M, st, t, s_v):
    st.then(k.nc.vector.bn_aggr(M.mv[:, t, :], M.stats[:, t, :, :]))
    k.nc.vector.tensor_scalar(M.mv[:, t, 1:2], M.mv[:, t, 1:2], LN_EPS, None, ALU.add).then_inc(s_v, 1)


def pool_rstd(k, M, pool, t, s_v, s_p):
    pool.wait_ge(s_v, t + 1)
    k.nc.gpsimd.tensor_tensor(M.mv[:, t, 1:2], M.mv[:, t, 1:2], M.half, ALU.pow).then_inc(s_p, 1)


def dve_norm(k, M, dve, st, t, s_p, s_n, s_h, permuted):
    x, n, c = k.x[:, t, :], M.n[:, t, :], min(t, 1)
    dve.wait_ge(s_p, t + 1)
    k.nc.vector.tensor_scalar(n, x, M.mv[:, t, 0:1], M.mv[:, t, 1:2], ALU.subtract, ALU.mult).then_inc(s_n, 1)
    dve.wait_ge(s_n, t + 1)
    G, B, h = M.T[:, c, 2, :], M.T[:, c, 1, :], k.hP[:, t, :]
    if permuted:
        n, G, B = (v.rearrange("p (q k) -> p k q", k=KT) for v in (n, G, B))
        h = h.rearrange("p (k q) -> p k q", k=KT)
    st.then(k.nc.vector.tensor_tensor(h, n, G, ALU.mult))
    k.nc.vector.tensor_tensor(h, h, B, ALU.add).then_inc(s_h, 1)


def pool_affine(k, M, pool, t, s_n, s_g2):
    pool.wait_ge(s_n, t + 1)
    k.nc.gpsimd.tensor_tensor(k.x[:, t, :], M.n[:, t, :], M.gb[:, 0, :], ALU.mult).then_inc(s_g2, 1)
    pool.wait_ge(s_g2, t + 1)
    k.nc.gpsimd.tensor_tensor(k.x[:, t, :], k.x[:, t, :], M.gb[:, 1, :], ALU.add)


def pe_turn_tile(k, pe, t, banks, s_h, s_tr):
    pe.wait_ge(s_h, t + 1)
    for g in range(2):
        for j in range(4):
            kk = 4 * g + j
            m = k.nc.tensor.transpose(k.ps[banks[g]][:, j * P:(j + 1) * P], k.hP[:, t, kk * P:(kk + 1) * P], k.ident)
        m.then_inc(s_tr, 1)


def copy_turned(k, act, t, banks, s_tr):
    for g in range(2):
        act.wait_ge(s_tr, 2 * t + g + 1)
        k.nc.scalar.copy(k.hT[:, 4 * g:4 * g + 4, t * P:(t + 1) * P], k.ps[banks[g]][:].rearrange("p (j n) -> p j n", j=4))


def stage_project_norm(k, w, layer):
    nc = k.nc
    M = NormBuffers(k, 1)
    NCH = D // 512
    w_slot = (early_slot(k), ring_slot(k, 1))
    turn_banks = ((6, 7), (0, 1), (2, 3))
    with Stage(nc) as ctx:
        s_gate, s_tab, s_fold, s_mm, s_d, s_ev, s_v, s_p, s_n, s_h, s_g2, s_tr, s_out = sems(
            nc, ctx, "gate_loaded tables_loaded tables_folded product_ready dve_steps product_taken var_ready rstd_ready "
                     "normed h_ready x_scaled turned rows_stored")
        blk = ctx.enter_context(nc.Block())

        @blk.sync
        def _(sp):
            k.arrived(sp, 1)
            load_norm_tables(k, sp, layer, 1, s_gate, s_tab)
            load_router(k, layer)(sp)
            for t in range(TILES):
                sp.wait_ge(s_h, t + 1)
                sp.dma_start(k.h_d[t * P:(t + 1) * P, :], k.hP[:, t, :]).then_inc(s_out, 16)
            sp.wait_ge(s_out, 16 * TILES)

        @blk.gpsimd
        def _(pool):
            pool.wait_ge(s_tab, 16 * 6)
            for i, step in enumerate(fold_steps(M, nc.gpsimd, 1, M.n[:, TILES - 1, :])):
                if i:
                    pool.wait_ge(s_fold, i)
                step().then_inc(s_fold, 1)
            pool_rstd(k, M, pool, 0, s_v, s_p)
            for t in range(TILES):
                pool_affine(k, M, pool, t, s_n, s_g2)
                if t + 1 < TILES:
                    pool_rstd(k, M, pool, t + 1, s_v, s_p)

        @blk.tensor
        def _(pe):
            for c in range(NCH):
                k.arrived(pe, c)
                for t in range(TILES):
                    for kk in range(KT):
                        m = nc.tensor.matmul(k.ps[TILES * c + t][:], k.hT[:, kk, t * P:(t + 1) * P], w_slot[c][:, kk, :],
                                             start=(kk == 0), stop=(kk == KT - 1))
                    m.then_inc(s_mm, 1)
            for t in range(TILES):
                if t:
                    pe.wait_ge(s_ev, TILES * (NCH - 1))
                pe_turn_tile(k, pe, t, turn_banks[t], s_h, s_tr)

        @blk.scalar
        def _(act):
            for t in range(TILES):
                act.wait_ge(s_mm, TILES * (NCH - 1) + t + 1)
                copy_turned(k, act, t, turn_banks[t], s_tr)

        @blk.vector
        def _(dve):
            st = Steps(dve, s_d)
            st.then(nc.vector.memset(M.half, -0.5))
            dve.wait_ge(s_gate, 32)
            for c in range(NCH):
                for t in range(TILES):
                    cols = slice(c * 512, (c + 1) * 512)
                    x, y = k.x[:, t, cols], M.tmp[:, cols]
                    dve.wait_ge(s_mm, TILES * c + t + 1)
                    nc.vector.tensor_tensor(y, k.ps[TILES * c + t][:], M.T[:, min(t, 1), 0, cols], ALU.mult).then_inc(s_ev, 1)
                    dve.wait_ge(s_ev, TILES * c + t + 1)
                    st.then(nc.vector.scalar_tensor_tensor(x, x, ALPHA, y, ALU.mult, ALU.add))
                    dve_stats(k, M, st, t, (c,))
                    if c == NCH - 1:
                        dve_variance(k, M, st, t, s_v)
                        if t == 1:
                            dve.wait_ge(s_fold, 5)
                        dve_norm(k, M, dve, st, t, s_p, s_n, s_h, True)
                    if c == NCH - 2 and t == 1:
                        dve.wait_ge(s_tab, 16 * 6)
                        for step in fold_steps(M, nc.vector, 0, M.tmp):
                            st.then(step())


def bc(ap, shape):
    return ap.to_broadcast(shape)


MOE_BIAS = 6656


def load_router(k, layer):
    def ahead(sp):
        k.load_ahead(sp, 4, k.s[:, 0:KT * NE], k.io["moe_router"][layer].rearrange("(p k) n -> p (k n)", k=KT))
        k.load_ahead(sp, 4, k.s[:, MOE_BIAS:MOE_BIAS + NE], k.io["moe_router_bias"][layer:layer + 1, :].to_broadcast([P, NE]))
    return ahead


def stage_route(k, layer):
    nc, io = k.nc, k.io
    o = 0

    def cut(n):
        nonlocal o
        o += n
        return k.z[:, o - n:o]

    E3 = TILES * NE
    scores, sel, mask, W, V, junk, ex = (cut(E3) for _ in range(7))
    g8 = cut(TILES * NG * 8)
    grp, rank, pen = (cut(TILES * NG) for _ in range(3))
    gt, eq = (cut(TILES * NG * NG) for _ in range(2))
    t8 = cut(8 * TILES)
    v8 = cut(8 * TILES)
    wsum = cut(4)
    CB = cut(P)
    bias = k.s[:, MOE_BIAS:MOE_BIAS + NE]
    keys = cut(2 * NE)
    okey = cut(OVER_KEYS + 8)
    yf = cut(NE)
    onesb = cut(4)[:, 0:2].bitcast(BF16)[:, 0:1]
    le = cut(2 * TILES * 512).bitcast(BF16).rearrange("p (b t e n) -> p b t e n", b=2, t=TILES, e=8)
    assert o <= TILES * EVEN_IN, o
    rw = k.s[:, 0:KT * NE].rearrange("p (k n) -> p k n", k=KT)
    sg = k.s[:, 512:512 + 4096]
    sd = k.s[:, 4608:4608 + 2048]
    sgv = sg.rearrange("p (j k n) -> p k j n", j=2, k=KT)
    sdv = sd.rearrange("p (j n) -> p j n", j=2)
    sex = k.s[:, 7000:7000 + FD * TILES].rearrange("p (t n) -> p t n", t=TILES)
    sh = k.s[:, 8000:8000 + FD * TILES].rearrange("p (t j n) -> p t j n", t=TILES, j=2)
    shT = k.s[:, 9000:9000 + FD * TILES].rearrange("p (t n) -> p t n", t=TILES)

    def tile3(v):
        return v.rearrange("p (t e) -> p t e", t=TILES)

    logits = k.ps[3][:, 0:E3]
    turned = k.ps[3][:, 256:512]
    incl_ps, total = k.ps[4][:, 0:E3], k.ps[4][:, E3:E3 + NE]
    totalT, base_ps, token = k.ps[5][0:NE, 0:P], k.ps[5][:, P:P + NE], k.ps[6][:, 0:NE]
    out_banks = ((7, 0), (1, 7), (2, 0))

    def not_beyond(g, t):
        return nc.vector.tensor_tensor(le[:, g % 2, t], bc(k.incl[:, t, 8 * g:8 * g + 8].rearrange("p (e o) -> p e o", o=1), [P, 8, P]),
                                 bc(k.c(C_IOTA, P).rearrange("p (o n) -> p o n", o=1), [P, 8, P]), ALU.is_le)

    with Stage(nc) as ctx:
        s_mm, s_e, s_d, s_m, s_cnt, s_cb, s_base, s_le, s_ix = sems(
            nc, ctx, "logits_ready exp_ready dve_steps mask_ready counts_ready counts_copied bases_ready le_ready "
                     "idx_ready")
        s_gul, s_dl, s_gu, s_se, s_h, s_ht, s_hc, s_dn, s_y = sems(
            nc, ctx, "shared_gate_up_loaded shared_down_loaded gate_up_ready shared_exp h_ready h_turned hT_ready down_ready y_copied")
        blk = ctx.enter_context(nc.Block())

        @blk.sync
        def _(sp):
            sp.dma_start(sg[:, 0:2048], io["shared_w_gate"][layer].rearrange("(p k) n -> p (k n)", k=KT)).then_inc(s_gul, 16)
            sp.dma_start(sg[:, 2048:4096], io["shared_w_up"][layer].rearrange("(p k) n -> p (k n)", k=KT)).then_inc(s_gul, 16)
            sp.dma_start(sd, io["shared_w_down"][layer].rearrange("(p j) n -> p (j n)", j=2)).then_inc(s_dl, 16)
            for e in range(2):
                load_expert(k, sp, layer, e, e, k.s_ahead[1 + e], k.s_ahead[1 + e])
                k.ahead[1 + e] += 48

        @blk.gpsimd
        def _(pool):
            nc.gpsimd.memset(k.hP[:], 0.0)

        @blk.tensor
        def _(pe):
            tri = k.c(C_TRI, P)
            m3 = tile3(mask)

            def gate_up(t, lo=0, hi=KT):
                for kk in range(lo, hi):
                    m = nc.tensor.matmul(k.ps[t][:], k.hT[:, kk, t * P:(t + 1) * P], sgv[:, kk], start=(kk == 0), stop=(kk == KT - 1))
                if hi == KT:
                    m.then_inc(s_gu, 1)

            def down(t):
                pe.wait_ge(s_h, t + 1)
                if t:
                    pe.wait_ge(s_hc, t)
                for j in range(2):
                    m = nc.tensor.transpose(turned[:, j * P:(j + 1) * P], sh[:, t, j, :], k.ident)
                m.then_inc(s_ht, 1)
                pe.wait_ge(s_hc, t + 1)
                if t:
                    pe.wait_ge(s_y, t)
                for c in range(2):
                    for j in range(2):
                        m = nc.tensor.matmul(k.ps[out_banks[t][c]][:], shT[:, t, j * P:(j + 1) * P], sdv[:, j, c * 512:(c + 1) * 512],
                                             start=(j == 0), stop=(j == 1))
                    m.then_inc(s_dn, 1)

            def count_le(g):
                pe.wait_ge(s_le, g + 1)
                for e in range(8):
                    for t in range(TILES):
                        m = nc.tensor.matmul(token[:, 8 * g + e:8 * g + e + 1], le[:, g % 2, t, e, :], onesb, start=(t == 0), stop=(t == TILES - 1))
                m.then_inc(s_ix, 1)

            k.arrived(pe, 4)
            for t in range(TILES):
                for kk in range(KT):
                    m = nc.tensor.matmul(tile3(logits)[:, t, :], k.hT[:, kk, t * P:(t + 1) * P], rw[:, kk, :], start=(kk == 0), stop=(kk == KT - 1))
            m.then_inc(s_mm, 1)
            pe.wait_ge(s_gul, 32)
            gate_up(0)
            gate_up(1, hi=KT // 2)
            pe.wait_ge(s_m, 1)
            for t in range(TILES):
                for u in range(t + 1):
                    nc.tensor.matmul(tile3(incl_ps)[:, t, :], tri if u == t else k.ones[:], m3[:, u, :], start=(u == 0), stop=(u == t))
            for t in range(TILES):
                nc.tensor.matmul(total, k.ones[:], m3[:, t, :], start=(t == 0), stop=(t == TILES - 1))
            for t in range(TILES):
                m = nc.tensor.matmul(totalT, m3[:, t, :], k.ones[:], start=(t == 0), stop=(t == TILES - 1))
            m.then_inc(s_cnt, 1)
            gate_up(1, lo=KT // 2)
            pe.wait_ge(s_cb, 1)
            nc.tensor.matmul(base_ps, CB[0:NE, :], tri[0:NE, 0:NE], start=True, stop=True).then_inc(s_base, 1)
            gate_up(2)
            pe.wait_ge(s_dl, 16)
            down(0)
            count_le(0)
            count_le(1)
            down(1)
            count_le(2)
            count_le(3)
            down(2)
            for g in range(4, NE // 8):
                count_le(g)

        @blk.scalar
        def _(act):
            def shared_exp(t):
                act.wait_ge(s_gu, t + 1)
                nc.scalar.activation(sex[:, t, :], k.ps[t][:, 0:FD], ACT.Exp, scale=-1.0).then_inc(s_se, 1)

            act.wait_ge(s_mm, 1)
            nc.scalar.activation(ex, logits, ACT.Exp, scale=-1.0).then_inc(s_e, 1)
            shared_exp(0)
            act.wait_ge(s_cnt, 1)
            nc.scalar.copy(CB[0:NE, :], totalT).then_inc(s_cb, 1)
            shared_exp(1)
            shared_exp(2)
            for t in range(TILES):
                act.wait_ge(s_ht, t + 1)
                nc.scalar.copy(shT[:, t, :], turned).then_inc(s_hc, 1)
                for c in range(2):
                    act.wait_ge(s_dn, 2 * t + c + 1)
                    nc.scalar.copy(k.cat[:, t, c * 512:(c + 1) * 512], k.ps[out_banks[t][c]][:]).then_inc(s_y, 1)

        @blk.vector
        def _(dve):
            st = Steps(dve, s_d)
            st.mark(nc.vector.memset(onesb, 1.0))
            dve.wait_ge(s_e, 1)
            st.then(nc.vector.tensor_scalar(ex, ex, 1.0, None, ALU.add))
            st.then(nc.vector.reciprocal(scores, ex))
            k.arrived(dve, 4)
            st.then(nc.vector.tensor_tensor(tile3(sel), tile3(scores), bc(bias.rearrange("p (o e) -> p o e", o=1), [P, TILES, NE]), ALU.add))
            for i in range(TILES * NG):
                st.mark(nc.vector.max(g8[:, 8 * i:8 * i + 8], sel[:, 8 * i:8 * i + 8]))
            st.wait()
            g8v = g8.rearrange("p (g n) -> p g n", n=8)
            st.then(nc.vector.tensor_tensor(grp, g8v[:, :, 0], g8v[:, :, 1], ALU.add))
            S4 = [P, TILES, NG, NG]
            gj = bc(grp.rearrange("p (t o j) -> p t o j", t=TILES, o=1), S4)
            gg = bc(grp.rearrange("p (t g o) -> p t g o", t=TILES, o=1), S4)
            v4 = lambda v: v.rearrange("p (t g j) -> p t g j", t=TILES, g=NG)
            st.mark(nc.vector.tensor_tensor(v4(gt), gj, gg, ALU.is_gt))
            st.then(nc.vector.tensor_tensor(v4(eq), gj, gg, ALU.is_equal))
            st.then(nc.vector.tensor_tensor(tile3(eq), tile3(eq), bc(k.c(C_LT8, 64).rearrange("p (o n) -> p o n", o=1), [P, TILES, 64]), ALU.mult))
            st.then(nc.vector.tensor_tensor(gt, gt, eq, ALU.add))
            st.then(nc.vector.tensor_reduce(rank, gt.rearrange("p (g j) -> p g j", j=NG), AX.X, ALU.add))
            st.then(nc.vector.tensor_scalar(pen, rank, TOPG - 0.5, -NEG, ALU.is_lt, ALU.mult))
            st.then(nc.vector.tensor_scalar(pen, pen, NEG, None, ALU.add))
            st.then(nc.vector.tensor_tensor(sel.rearrange("p (g n) -> p g n", n=8), sel.rearrange("p (g n) -> p g n", n=8),
                                            bc(pen.rearrange("p (g o) -> p g o", o=1), [P, TILES * NG, 8]), ALU.add))
            for t in range(TILES):
                st.mark(nc.vector.max(t8[:, 8 * t:8 * t + 8], tile3(sel)[:, t, :]))
            st.wait()
            for t in range(TILES):
                st.mark(nc.vector.match_replace(tile3(junk)[:, t, :], t8[:, 8 * t:8 * t + 8], tile3(sel)[:, t, :], 1e38))
            st.wait()
            nc.vector.tensor_scalar(mask, junk, 5e37, None, ALU.is_ge).then_inc(s_m, 1)
            dve.wait_ge(s_m, 1)
            st.then(nc.vector.tensor_tensor(W, scores, mask, ALU.mult))
            st.then(nc.vector.tensor_reduce(wsum[:, 0:TILES], tile3(W), AX.X, ALU.add))
            st.then(nc.vector.reciprocal(wsum[:, 0:TILES], wsum[:, 0:TILES]))
            for t in range(TILES):
                st.mark(nc.vector.tensor_scalar(tile3(W)[:, t, :], tile3(W)[:, t, :], wsum[:, t:t + 1], ROUTED_SCALE, ALU.mult, ALU.mult))

            def shared_hidden(t):
                dve.wait_ge(s_se, t + 1)
                st.then(nc.vector.tensor_scalar(sex[:, t, :], sex[:, t, :], 1.0, None, ALU.add))
                st.then(nc.vector.reciprocal(sex[:, t, :], sex[:, t, :]))
                st.then(nc.vector.tensor_tensor(sex[:, t, :], sex[:, t, :], k.ps[t][:, 0:FD], ALU.mult))
                nc.vector.tensor_tensor(sh[:, t].rearrange("p j q -> p q j"), sex[:, t, :].rearrange("p (q j) -> p q j", j=2),
                                        k.ps[t][:, FD:2 * FD].rearrange("p (q j) -> p q j", j=2), ALU.mult).then_inc(s_h, 1)

            def tokens_by_count(g):
                if g >= 2:
                    dve.wait_ge(s_ix, g - 1)
                for t in range(TILES):
                    m = not_beyond(g, t)
                m.then_inc(s_le, 1)

            shared_hidden(0)
            dve.wait_ge(s_cnt, 1)
            st.then(nc.vector.tensor_tensor(k.incl[:], tile3(incl_ps), tile3(mask), ALU.add))
            tokens_by_count(0)
            tokens_by_count(1)
            shared_hidden(1)
            tokens_by_count(2)
            tokens_by_count(3)
            shared_hidden(2)
            dve.wait_ge(s_base, 1)
            base, end = k.bases[:, 0, :], k.bases[:, 1, :]
            st.then(nc.vector.tensor_copy(base, base_ps))
            st.then(nc.vector.tensor_tensor(end, base, total, ALU.add))
            st.then(nc.vector.tensor_tensor(tile3(V), k.incl[:], bc(base.rearrange("p (o e) -> p o e", o=1), [P, TILES, NE]), ALU.add))
            st.then(nc.vector.tensor_tensor(V, V, mask, ALU.mult))
            for t in range(TILES):
                st.mark(nc.vector.max(v8[:, 8 * t:8 * t + 8], tile3(V)[:, t, :]))
            st.wait()
            st.mark(nc.vector.tensor_scalar(k.slot_u[:].rearrange("p t n -> p (t n)"), v8, -1.0, None, ALU.add))
            for t in range(TILES):
                for j in range(TOPK):
                    st.then(nc.vector.scalar_tensor_tensor(tile3(junk)[:, t, :], tile3(V)[:, t, :], v8[:, 8 * t + j:8 * t + j + 1], tile3(W)[:, t, :],
                                                           ALU.is_equal, ALU.mult, accum_out=k.w8[:, t, j:j + 1]))
            col = k.const[:, C_COL + 1:C_COL + 2]
            st.then(nc.vector.tensor_scalar(yf, base, col, None, ALU.add))
            st.then(nc.vector.tensor_tensor(junk[:, 0:NE], yf, end, ALU.is_ge))
            st.then(nc.vector.scalar_tensor_tensor(yf, junk[:, 0:NE], FAR, yf, ALU.mult, ALU.add))
            st.mark(nc.vector.tensor_copy(k.y_idx[:], yf))
            for b in range(OVER_BLOCKS):
                st.then(nc.vector.tensor_scalar(keys[:, b * NE:(b + 1) * NE], total, P * (b + 1.0), None, ALU.is_gt))
            st.then(nc.vector.tensor_tensor(keys, keys, k.c(C_KEY, 2 * NE), ALU.mult))
            for i in range(OVER_KEYS // 8):
                st.then(nc.vector.max(okey[:, 8 * i:8 * i + 8], keys))
                st.then(nc.vector.match_replace(keys, okey[:, 8 * i:8 * i + 8], keys, -1.0))
            st.then(nc.vector.tensor_scalar(junk[:, 0:OVER_KEYS], okey[:, 0:OVER_KEYS], 0.5, None, ALU.is_gt))
            st.then(nc.vector.tensor_reduce(okey[:, OVER_KEYS:OVER_KEYS + 1], junk[:, 0:OVER_KEYS], AX.X, ALU.add))
            st.then(nc.vector.tensor_scalar(okey[:, 0:OVER_KEYS], okey[:, 0:OVER_KEYS], -1.0, 0.0, ALU.add, ALU.max))
            st.mark(nc.vector.tensor_copy(k.over[:, 0:OVER_KEYS + 1], okey[:, 0:OVER_KEYS + 1]))
            for g in range(4, NE // 8):
                tokens_by_count(g)
            dve.wait_ge(s_ix, NE // 8)
            st.mark(nc.vector.tensor_copy(k.tok_idx[:], token))


def expert_views(k, b):
    w = k.ring[:, b * 6144:(b + 1) * 6144]
    return (w[:, 0:2048], w[:, 2048:4096], w[:, 4096:6144],
            w[:, 0:4096].rearrange("p (j k n) -> p k j n", j=2, k=KT), w[:, 4096:6144].rearrange("p (j n) -> p j n", j=2))


def load_gate_up(k, eng, layer, e, b, sem):
    for name, v in zip(("moe_w_gate", "moe_w_up"), expert_views(k, b)):
        src = k.io[name][layer, bass.ds(e, 1)].rearrange("o (p k) n -> p (o k n)", k=KT)
        eng.dma_start(v, src).then_inc(sem, 16)


def load_down(k, eng, layer, e, b, sem):
    src = k.io["moe_w_down"][layer, bass.ds(e, 1)].rearrange("o (p j) n -> p (o j n)", j=2)
    eng.dma_start(expert_views(k, b)[2], src).then_inc(sem, 16)


def load_expert(k, eng, layer, e, b, sem_gu, sem_d):
    load_gate_up(k, eng, layer, e, b, sem_gu)
    load_down(k, eng, layer, e, b, sem_d)


class MoeBuffers:

    def __init__(self, k):
        self.xg = k.hP[:, 0:2, :]
        f = k.s
        self.xT = f[:, 0:1024]
        self.ex = [f[:, 1024 + i * FD:1024 + (i + 1) * FD] for i in range(2)]
        self.h = [f[:, 1536 + i * FD:1536 + (i + 1) * FD] for i in range(2)]
        self.hT = f[:, 2048:2048 + FD]
        self.y = [f[:, 2560 + i * D:2560 + (i + 1) * D] for i in range(2)]
        self.gi = f[:, 4700:4701].bitcast(U32)
        self.si = f[:, 4710:4711].bitcast(U32)


def pe_turn_rows(k, B, b):
    for kk in range(KT):
        m = k.nc.tensor.transpose(k.ps[kk // 4][:, (kk % 4) * P:(kk % 4 + 1) * P], B.xg[:, b, kk * P:(kk + 1) * P], k.ident)
    return m


def pe_gate_up(k, B, b, bank):
    for kk in range(KT):
        m = k.nc.tensor.matmul(k.ps[bank][:], B.xT[:, kk * P:(kk + 1) * P], expert_views(k, b)[3][:, kk], start=(kk == 0), stop=(kk == KT - 1))
    return m


def pe_turn_h(k, B, b):
    for j in range(2):
        m = k.nc.tensor.transpose(k.ps[4][:, j * P:(j + 1) * P], B.h[b][:, j * P:(j + 1) * P], k.ident)
    return m


def pe_down(k, B, b):
    for c in range(2):
        for j in range(2):
            m = k.nc.tensor.matmul(k.ps[5 + c][:], B.hT[:, j * P:(j + 1) * P], expert_views(k, b)[4][:, j, c * 512:(c + 1) * 512],
                                   start=(j == 0), stop=(j == 1))
    return m


def dve_hidden(k, B, b, bank, eng, sem, n):
    nc = k.nc
    g, u = k.ps[bank][:, 0:FD], k.ps[bank][:, FD:2 * FD]
    nc.vector.tensor_scalar(B.ex[b], B.ex[b], 1.0, None, ALU.add).then_inc(sem, 1)
    eng.wait_ge(sem, n + 1)
    nc.vector.reciprocal(B.ex[b], B.ex[b]).then_inc(sem, 1)
    eng.wait_ge(sem, n + 2)
    nc.vector.tensor_tensor(B.ex[b], B.ex[b], g, ALU.mult).then_inc(sem, 1)
    eng.wait_ge(sem, n + 3)
    return nc.vector.tensor_tensor(B.h[b].rearrange("p (j q) -> p q j", j=2), B.ex[b].rearrange("p (q j) -> p q j", j=2),
                                   u.rearrange("p (q j) -> p q j", j=2), ALU.mult)


def gather(k, out, table, last, idx):
    return k.nc.gpsimd.indirect_dma_start(out=out, out_offset=None, in_=table, in_offset=bass.IndirectOffsetOnAxis(ap=idx, axis=0),
                                          bounds_check=last, oob_is_err=False)


def scatter(k, table, last, idx, in_):
    return k.nc.gpsimd.indirect_dma_start(out=table, out_offset=bass.IndirectOffsetOnAxis(ap=idx, axis=0), in_=in_, in_offset=None,
                                          bounds_check=last, oob_is_err=False)


def bounds(pool):
    regs = []
    for v in (TOK - 1, ASSIGNED - 1):
        r = pool.alloc_register()
        pool.reg_mov(r, v)
        regs.append(r)
    return regs


def for_experts(eng, step, last):
    for e in range(3):
        step(e, e // 2, e % 2)
    pairs = (last - 2) // 2
    with eng.Fori(0, pairs) as i:
        step(2 * i + 3, i + 1, 1)
        step(2 * i + 4, i + 2, 0)
    for e in range(3 + 2 * pairs, last + 1):
        step(e, e // 2, e % 2)


def ge(eng, sem, v):
    if not isinstance(v, int) or v > 0:
        eng.wait_ge(sem, v)


FOLD_FROM = 8


def stage_experts(k, layer):
    nc = k.nc
    B = MoeBuffers(k)
    last_layer = layer == DEPTH - 1
    with Stage(nc) as ctx:
        s_xt, s_xa, s_xv, s_gu, s_e, s_hs, s_h, s_ht, s_hc, s_d, s_ya, s_yv = sems(
            nc, ctx, "x_turned xT_copied_act xT_copied_dve gate_up_ready exp_ready h_steps h_ready "
                     "h_turned hT_ready down_ready y_copied_act y_copied_dve")
        s_g, s_sc = k.pool_sems[layer][0:2], k.pool_sems[layer][2]
        s_fold = sems(nc, ctx, "table_folded")[0]
        s_wg = sems(nc, ctx, "gate_up0_loaded gate_up1_loaded")
        s_wd = sems(nc, ctx, "down0_loaded down1_loaded")
        blk = ctx.enter_context(nc.Block())

        @blk.sync
        def _(sp):
            def step(e, half, b):
                sp.wait_ge(s_gu, e + 1)
                load_gate_up(k, sp, layer, e + 2, b, s_wg[b])
                if not isinstance(e, int) or e >= 1:
                    sp.wait_ge(s_d, e)
                    load_down(k, sp, layer, e + 1, 1 - b, s_wd[1 - b])
            load_norm_tables(k, sp, layer, 2, k.s_ahead[3], k.s_ahead[3])
            k.ahead[3] += 16 * (4 if last_layer else 8)
            for_experts(sp, step, NE - 3)
            sp.wait_ge(s_d, NE - 2)
            load_down(k, sp, layer, NE - 1, 1, s_wd[1])

        @blk.gpsimd
        def _(pool):
            last_tok, last_row = bounds(pool)

            def get(e, b):
                ge(pool, s_xt, e - 1)
                gather(k, B.xg[:, b, :], k.h_d, last_tok, k.tok_idx[:, e:e + 1]).then_inc(s_g[b], 16)

            def put(e, b):
                pool.wait_ge(s_ya, e + 1)
                pool.wait_ge(s_yv, e + 1)
                ge(pool, s_sc, 16 * e)
                scatter(k, k.y_d, last_row, k.y_idx[:, e:e + 1], B.y[b]).then_inc(s_sc, 16)

            get(0, 0)
            get(1, 1)
            M = NormBuffers(k, 2)
            folds = [] if last_layer else [f for c in range(2) for f in fold_steps(M, nc.gpsimd, c, M.tmp)]
            for e in range(NE - 2):
                get(e + 2, e % 2)
                if e >= 1:
                    put(e - 1, (e - 1) % 2)
                if e >= FOLD_FROM and (e - FOLD_FROM) % 3 == 0 and (e - FOLD_FROM) // 3 < len(folds):
                    i = (e - FOLD_FROM) // 3
                    if i == 0:
                        k.arrived(pool, 3)
                    else:
                        pool.wait_ge(s_fold, i)
                    folds[i]().then_inc(s_fold, 1)
            for e in range(NE - 3, NE):
                put(e, e % 2)
            pool.wait_ge(s_sc, 16 * NE)

        @blk.tensor
        def _(pe):
            def turn_rows(e, half, b):
                pe.wait_ge(s_g[b], 16 * (half + 1))
                ge(pe, s_xa, e)
                ge(pe, s_xv, e)
                pe_turn_rows(k, B, b).then_inc(s_xt, 1)

            def gate_up(e, half, b):
                pe.wait_ge(s_xa, e + 1)
                pe.wait_ge(s_xv, e + 1)
                if isinstance(e, int) and e < 2:
                    k.arrived(pe, 1 + e)
                else:
                    pe.wait_ge(s_wg[b], 32 * half)
                ge(pe, s_h, e - 1)
                pe_gate_up(k, B, b, 2 + b).then_inc(s_gu, 1)

            def turn_h(e, half, b):
                pe.wait_ge(s_h, e + 1)
                ge(pe, s_hc, e)
                pe_turn_h(k, B, b).then_inc(s_ht, 1)

            def down(e, half, b):
                pe.wait_ge(s_hc, e + 1)
                if isinstance(e, int) and e < 2:
                    k.arrived(pe, 1 + e)
                else:
                    pe.wait_ge(s_wd[b], 16 * half)
                ge(pe, s_ya, e)
                ge(pe, s_yv, e)
                pe_down(k, B, b).then_inc(s_d, 1)

            def step(e, half, b):
                gate_up(e, half, b)
                if not isinstance(e, int) or e >= 1:
                    turn_h(e - 1, half - 1 + b, 1 - b)
                turn_rows(e + 1, half + b, 1 - b)
                if not isinstance(e, int) or e >= 1:
                    down(e - 1, half - 1 + b, 1 - b)
            turn_rows(0, 0, 0)
            for_experts(pe, step, NE - 2)
            gate_up(NE - 1, NE // 2 - 1, 1)
            for e, b in ((NE - 2, 0), (NE - 1, 1)):
                turn_h(e, NE // 2 - 1, b)
                down(e, NE // 2 - 1, b)

        @blk.scalar
        def _(act):
            def copy_x(e):
                act.wait_ge(s_xt, e + 1)
                nc.scalar.copy(B.xT[:, 0:512], k.ps[0][:]).then_inc(s_xa, 1)

            def hidden(e, b):
                act.wait_ge(s_gu, e + 1)
                ge(act, s_h, e - 1)
                nc.scalar.activation(B.ex[b], k.ps[2 + b][:, 0:FD], ACT.Exp, scale=-1.0).then_inc(s_e, 1)

            def copy_h(e):
                act.wait_ge(s_ht, e + 1)
                nc.scalar.copy(B.hT, k.ps[4][:, 0:FD]).then_inc(s_hc, 1)

            def finish(e, b):
                act.wait_ge(s_d, e + 1)
                ge(act, s_sc, 16 * (e - 1))
                nc.scalar.copy(B.y[b][:, 0:512], k.ps[5][:]).then_inc(s_ya, 1)

            def step(e, half, b):
                hidden(e, b)
                if not isinstance(e, int) or e >= 1:
                    copy_h(e - 1)
                copy_x(e + 1)
                if not isinstance(e, int) or e >= 1:
                    finish(e - 1, 1 - b)
            copy_x(0)
            for_experts(act, step, NE - 2)
            hidden(NE - 1, 1)
            for e, b in ((NE - 2, 0), (NE - 1, 1)):
                copy_h(e)
                finish(e, b)

        @blk.vector
        def _(dve):
            def copy_x(e):
                dve.wait_ge(s_xt, e + 1)
                nc.vector.tensor_copy(B.xT[:, 512:1024], k.ps[1][:]).then_inc(s_xv, 1)

            def hidden(e, b):
                dve.wait_ge(s_e, e + 1)
                ge(dve, s_ht, e - 1)
                dve_hidden(k, B, b, 2 + b, dve, s_hs, 3 * e).then_inc(s_h, 1)

            def finish(e, b):
                dve.wait_ge(s_d, e + 1)
                ge(dve, s_sc, 16 * (e - 1))
                nc.vector.tensor_copy(B.y[b][:, 512:1024], k.ps[6][:]).then_inc(s_yv, 1)

            def step(e, half, b):
                hidden(e, b)
                copy_x(e + 1)
                if not isinstance(e, int) or e >= 1:
                    finish(e - 1, 1 - b)
            copy_x(0)
            for_experts(dve, step, NE - 2)
            hidden(NE - 1, 1)
            finish(NE - 2, 0)
            finish(NE - 1, 1)


def stage_overflow(k, layer):
    nc = k.nc
    B = MoeBuffers(k)
    le = k.s[:, 5000:5000 + 3 * 64].bitcast(BF16).rearrange("p (t n) -> p t n", t=TILES)
    onesb = k.s[:, 5200:5202].bitcast(BF16)[:, 0:1]
    row = k.s[:, 5210:5211]
    far = k.s[:, 5212:5213]
    with Stage(nc) as ctx:
        s_w, s_le, s_ix, s_si, s_gi, s_xt, s_x, s_gu, s_e, s_hs, s_h, s_ht, s_hc, s_d, s_y, s_v, s_one, s_free = sems(
            nc, ctx, "ov_loaded ov_le ov_idx ov_rows ov_gidx ov_turned ov_xT ov_gate_up ov_exp ov_hsteps ov_h ov_hturned ov_hT ov_down ov_y "
                     "ov_steps ov_ones ov_free")
        s_g, s_sc = k.pool_sems[layer][3:5]
        blk = ctx.enter_context(nc.Block())

        def items(eng, body):
            n = eng.value_load(k.over[0:1, OVER_KEYS:OVER_KEYS + 1], min_val=0, max_val=OVER_KEYS)
            with eng.If(n > 0):
                with eng.Fori(0, n) as i:
                    body(i)
            with eng.Else():
                pass

        def item(eng, i):
            return eng.value_load(k.over[0:1, bass.ds(i, 1)], min_val=0, max_val=2 * NE - 1)

        @blk.sync
        def _(sp):
            def body(i):
                key = item(sp, i)
                sp.wait_ge(s_free, i + 1)
                load_expert(k, sp, layer, key % NE, 0, s_w, s_w)
            items(sp, body)

        @blk.gpsimd
        def _(pool):
            last_tok, last_row = bounds(pool)

            n = pool.value_load(k.over[0:1, OVER_KEYS:OVER_KEYS + 1], min_val=0, max_val=OVER_KEYS)
            pool.sem_inc(s_free, 1)
            for i in range(OVER_KEYS):
                with pool.If(n > i):
                    pool.wait_ge(s_gi, i + 1)
                    gather(k, B.xg[:, 0, :], k.h_d, last_tok, B.gi).then_inc(s_g, 16)
                    pool.wait_ge(s_si, i + 1)
                    pool.wait_ge(s_y, 2 * i + 2)
                    scatter(k, k.y_d, last_row, B.si, B.y[0]).then_inc(s_sc, 16)
                    pool.wait_ge(s_sc, 16 * i + 16)
                    pool.sem_inc(s_free, 1)
                with pool.Else():
                    pass

        @blk.tensor
        def _(pe):
            def body(i):
                pe.wait_ge(s_le, 3 * i + 3)
                for t in range(TILES):
                    m = nc.tensor.matmul(k.ps[7][:, 0:1], le[:, t, :], onesb, start=(t == 0), stop=(t == TILES - 1))
                m.then_inc(s_ix, 1)
                pe.wait_ge(s_g, 16 * i + 16)
                pe_turn_rows(k, B, 0).then_inc(s_xt, 1)
                pe.wait_ge(s_x, 2 * i + 2)
                pe.wait_ge(s_w, 48 * i + 48)
                pe_gate_up(k, B, 0, 2).then_inc(s_gu, 1)
                pe.wait_ge(s_h, i + 1)
                pe_turn_h(k, B, 0).then_inc(s_ht, 1)
                pe.wait_ge(s_hc, i + 1)
                pe_down(k, B, 0).then_inc(s_d, 1)
            items(pe, body)

        @blk.scalar
        def _(act):
            def body(i):
                act.wait_ge(s_xt, i + 1)
                for j in range(2):
                    nc.scalar.copy(B.xT[:, j * 512:(j + 1) * 512], k.ps[j][:]).then_inc(s_x, 1)
                act.wait_ge(s_gu, i + 1)
                nc.scalar.activation(B.ex[0], k.ps[2][:, 0:FD], ACT.Exp, scale=-1.0).then_inc(s_e, 1)
                act.wait_ge(s_ht, i + 1)
                nc.scalar.copy(B.hT, k.ps[4][:, 0:FD]).then_inc(s_hc, 1)
                act.wait_ge(s_d, i + 1)
                for j in range(2):
                    nc.scalar.copy(B.y[0][:, j * 512:(j + 1) * 512], k.ps[5 + j][:]).then_inc(s_y, 1)
            items(act, body)

        @blk.vector
        def _(dve):
            nc.vector.memset(onesb, 1.0).then_inc(s_one, 1)
            dve.wait_ge(s_one, 1)

            def body(i):
                key = item(dve, i)
                e, blk_no = key % NE, key // NE
                dve.wait_ge(s_free, i + 1)
                for t in range(TILES):
                    nc.vector.tensor_scalar(le[:, t, :], k.const[:, bass.ds(C_IOTA + P + blk_no * P, P)], k.incl[:, t, bass.ds(e, 1)], None,
                                            ALU.is_ge).then_inc(s_le, 1)
                first = k.const[:, bass.ds(C_IOTA + P + blk_no * P, 1)]
                nc.vector.tensor_tensor(row, k.bases[:, 0, bass.ds(e, 1)], first, ALU.add).then_inc(s_v, 1)
                dve.wait_ge(s_v, 4 * i + 1)
                nc.vector.tensor_tensor(row, row, k.const[:, C_COL + 1:C_COL + 2], ALU.add).then_inc(s_v, 1)
                dve.wait_ge(s_v, 4 * i + 2)
                nc.vector.tensor_tensor(far, row, k.bases[:, 1, bass.ds(e, 1)], ALU.is_ge).then_inc(s_v, 1)
                dve.wait_ge(s_v, 4 * i + 3)
                nc.vector.scalar_tensor_tensor(row, far, FAR, row, ALU.mult, ALU.add).then_inc(s_v, 1)
                dve.wait_ge(s_v, 4 * i + 4)
                nc.vector.tensor_copy(B.si, row).then_inc(s_si, 1)
                dve.wait_ge(s_ix, i + 1)
                nc.vector.tensor_copy(B.gi, k.ps[7][:, 0:1]).then_inc(s_gi, 1)
                dve.wait_ge(s_e, i + 1)
                dve_hidden(k, B, 0, 2, dve, s_hs, 3 * i).then_inc(s_h, 1)
            items(dve, body)


def stage_combine_norm(k, layer, ahead=None):
    nc, io = k.nc, k.io
    M = NormBuffers(k, 2)
    last = layer == DEPTH - 1
    NB = 8
    buf = k.s[:, 0:NB * D].rearrange("p (b n) -> p b n", b=NB)
    order = [(t, j) for t in range(TILES) for j in range(TOPK)]
    with Stage(nc) as ctx:
        s_acc, s_d, s_v, s_p, s_n, s_h, s_g2, s_tr, s_out = sems(
            nc, ctx, "row_added dve_steps var_ready rstd_ready normed h_ready x_scaled turned outputs_stored")
        s_g = k.pool_sems[layer][5:5 + NB]
        blk = ctx.enter_context(nc.Block())

        @blk.sync
        def _(sp):
            if last:
                for t in range(TILES):
                    sp.wait_ge(s_h, t + 1)
                    dst = io["y_prompt"][0] if t == 0 else io["y_sample"][0, (t - 1) * P:t * P, :]
                    sp.dma_start(dst, k.x[:, t, :]).then_inc(s_out, 16)
                sp.wait_ge(s_out, 16 * TILES)
            else:
                sp.wait_ge(s_acc, len(order) - NB)
                ahead(sp)

        @blk.gpsimd
        def _(pool):
            last_tok, last_row = bounds(pool)

            def rows(tile):
                for i, (t, j) in enumerate(order):
                    if t == tile:
                        if i >= NB:
                            pool.wait_ge(s_acc, i - NB + 1)
                        gather(k, buf[:, i % NB, :], k.y_d, last_row, k.slot_u[:, t, j:j + 1]).then_inc(s_g[i % NB], 16)

            rows(0)
            rows(1)
            pool_rstd(k, M, pool, 0, s_v, s_p)
            rows(2)
            pool_rstd(k, M, pool, 1, s_v, s_p)
            if last:
                pool_rstd(k, M, pool, 2, s_v, s_p)
            else:
                pool_affine(k, M, pool, 0, s_n, s_g2)
                pool_rstd(k, M, pool, 2, s_v, s_p)
                pool_affine(k, M, pool, 1, s_n, s_g2)
                pool_affine(k, M, pool, 2, s_n, s_g2)

        @blk.tensor
        def _(pe):
            for t in range(0 if last else TILES):
                pe_turn_tile(k, pe, t, (2 * t, 2 * t + 1), s_h, s_tr)

        @blk.scalar
        def _(act):
            for t in range(0 if last else TILES):
                copy_turned(k, act, t, (2 * t, 2 * t + 1), s_tr)

        @blk.vector
        def _(dve):
            st = Steps(dve, s_d)
            st.mark(nc.vector.memset(M.half, -0.5))

            def add_rows(tile):
                for i, (t, j) in enumerate(order):
                    if t == tile:
                        dve.wait_ge(s_g[i % NB], 16 * (i // NB + 1))
                        ge(dve, s_acc, i)
                        nc.vector.scalar_tensor_tensor(k.cat[:, t, :], buf[:, i % NB, :], k.w8[:, t, j:j + 1], k.cat[:, t, :],
                                                       ALU.mult, ALU.add).then_inc(s_acc, 1)

            def residual(t):
                x, f = k.x[:, t, :], k.cat[:, t, :]
                if t == 0:
                    k.arrived(dve, 3)
                dve.wait_ge(s_acc, TOPK * (t + 1))
                st.then(nc.vector.tensor_tensor(f, f, M.T[:, min(t, 1), 0, :], ALU.mult))
                st.then(nc.vector.scalar_tensor_tensor(x, x, ALPHA, f, ALU.mult, ALU.add))
                dve_stats(k, M, st, t, range(2))
                dve_variance(k, M, st, t, s_v)

            def norm(t):
                if not last:
                    dve_norm(k, M, dve, st, t, s_p, s_n, s_h, False)
                    return
                x = k.x[:, t, :]
                dve.wait_ge(s_p, t + 1)
                st.then(nc.vector.tensor_scalar(x, x, M.mv[:, t, 0:1], M.mv[:, t, 1:2], ALU.subtract, ALU.mult))
                st.then(nc.vector.tensor_tensor(x, x, M.gb[:, 0, :], ALU.mult))
                nc.vector.tensor_tensor(x, x, M.gb[:, 1, :], ALU.add).then_inc(s_h, 1)

            for t in range(TILES):
                add_rows(t)
                if t:
                    norm(t - 1)
                residual(t)
            norm(TILES - 1)


def even_mixer(k, e, ahead):
    z = k.z[:].rearrange("p (t n) -> p t n", t=TILES)
    R, S = k.ring, k.s
    stage_project(k, k.io["mla_ret_w_in"][e], EVEN_IN, lambda t, c, n: z[:, t, c:c + n])
    m = k.mla = {}
    m["kT"] = R[0:QK, 0:4096].rearrange("p (h n) -> p h n", h=HEADS)
    m["v"] = R[:, 4096:6144].rearrange("p (t n) -> p t n", t=4)
    m["qT"] = R[0:QK, 6144:9216].rearrange("p (t h n) -> p t h n", t=TILES, h=HEADS)
    m["q"] = R[:, 9216:11520].rearrange("p (t n) -> p t n", t=TILES)
    m["qn"] = R[:, 11520:12288].rearrange("p (t n) -> p t n", t=TILES)
    o = 3200
    for name, n in (("qnT", 768), ("ckv", 512), ("kpe", 384), ("ckvT", 512), ("kpeT", 512), ("wuq", 1536), ("wuk", 512), ("wuv", 512),
                    ("qg", Q_RANK), ("kvg", KV_RANK), ("junk", Q_RANK), ("ss", 6), ("rstd", 6), ("half", 6)):
        m[name] = S[:, o:o + n]
        o += n + n % 2
    m["qnT"] = m["qnT"].rearrange("p (k n) -> p k n", k=2)
    m["ckv"] = m["ckv"].rearrange("p (t n) -> p t n", t=4)
    m["kpe"] = m["kpe"].rearrange("p (t n) -> p t n", t=4)
    m["wuq"] = m["wuq"].rearrange("p (k n) -> p k n", k=2)
    stage_mla_norm(k, e)
    stage_mla_keys(k, e)
    stage_turn_heads(k, [([m["q"][:, t, (4 * g + j) * QK:(4 * g + j + 1) * QK] for j in range(4)], m["qT"][:, t, 4 * g:4 * g + 4, :])
                         for t in range(TILES) for g in range(2)], QK)
    heads = []
    for t in range(TILES):
        for h in range(HEADS):
            lo, hi = (0, 1) if t == 0 else (1, 4)
            heads.append(dict(q=m["qT"][:, t, h, :], keys=m["kT"][:, h, lo * P:hi * P],
                              v=[m["v"][:, i, h * VD:(h + 1) * VD] for i in range(lo, hi)], out=k.cat[:, t, h * VD:(h + 1) * VD]))
    stage_attention(k, heads, QK ** -0.5)
    stage_turn_heads(k, retention_jobs(k), RD)
    stage_retention(k, e, ahead)


def odd_mixer(k, o, ahead):
    z = k.zo = k.z[:, 0:TILES * ODD_IN].rearrange("p (t n) -> p t n", t=TILES)
    R, S = k.ring, k.s
    stage_project(k, k.io["swa_w_in"][o], ODD_IN, lambda t, c, n: z[:, t, c:c + n])
    k.kctx, k.vctx, k.sink = S[:, 3200:3456], S[:, 3456:3712], S[:, 3712:3728]
    stage_swa_prep(k, o)
    qT = R[0:SD, 0:6144].rearrange("p (t h n) -> p t h n", t=TILES, h=SH)
    kT = R[0:SD, 6144:8192].rearrange("p (h j n) -> p h j n", h=SKV, j=4)
    jobs = [([z[:, t, (4 * g + j) * SD:(4 * g + j + 1) * SD] for j in range(4)], qT[:, t, 4 * g:4 * g + 4, :])
            for t in range(TILES) for g in range(4)]
    for h in range(SKV):
        a = SQ_DIM + h * SD
        jobs.append(([z[:, t, a:a + SD] for t in range(TILES)] + [k.kctx[:, h * SD:(h + 1) * SD]], kT[:, h]))
    stage_turn_heads(k, jobs, SD)
    heads = []
    for t in range(TILES):
        for h in range(SH):
            g = h // (SH // SKV)
            lo, hi = (0, 1) if t == 0 else (1, 4)
            a = SQ_DIM + SKV_DIM + g * SD
            vs = [z[:, i, a:a + SD] for i in range(TILES)] + [k.vctx[:, g * SD:(g + 1) * SD]]
            heads.append(dict(q=qT[:, t, h, :], keys=kT[:, g, lo:hi, :].rearrange("p j n -> p (j n)"), v=vs[lo:hi],
                              out=k.cat[:, t, h * SD:(h + 1) * SD], sink=k.sink[:, h:h + 1],
                              mask=k.c(C_MASK + (t - 1) * TOK, TOK) if t else None))
    stage_attention(k, heads, SD ** -0.5, ahead)


def backbone(nc, io):
    def w_in(layer):
        return io[("mla_ret_w_in", "swa_w_in")[layer % 2]][layer // 2]

    with ExitStack() as ctx:
        k = Kernel(nc, ctx, io)
        stage_setup(k)
        stage_mod(k)
        for layer in range(DEPTH):
            w_out = io[("even_w_out", "swa_w_out")[layer % 2]][layer // 2]
            if layer == 0:
                stage_modulate(k, layer)
                stage_transpose(k, k.hP, first_chunks(k, w_in(0)))
            (even_mixer, odd_mixer)[layer % 2](k, layer // 2, out_chunk(k, w_out, 0))
            stage_transpose(k, k.cat, out_chunk(k, w_out, 1))
            stage_project_norm(k, w_out, layer)
            stage_route(k, layer)
            stage_experts(k, layer)
            stage_overflow(k, layer)
            stage_combine_norm(k, layer, None if layer == DEPTH - 1 else first_chunks(k, w_in(layer + 1)))


_OUTS = [("y_prompt", (1, P, D)), ("y_sample", (1, 2 * P, D)), ("new_mla_ckv", (1, 1, P, KV_RANK)), ("new_mla_kpe", (1, 1, P, ROPE)),
         ("new_ret_fwd", (1, 1, RH, RD, RD)), ("new_ret_bwd", (1, 1, RH, RD, RD)), ("new_swa_k", (1, 1, P, SKV, SD)), ("new_swa_v", (1, 1, P, SKV, SD))]


def kernel(**inputs):
    import numpy as _np
    import concourse.bacc as _bacc
    from concourse import mybir as _mybir
    from concourse.bass_utils import run_bass_kernel_spmd as _run

    nc = _bacc.Bacc("TRN2", target_bir_lowering=False, num_devices=1)
    arrays, io = {}, {}
    for name, value in [*inputs.items(), ("tables", shape_tables())]:
        a = _np.ascontiguousarray(value)
        if name == "c_ctx":
            a = a.reshape(-1)
        arrays[f"in_{name}"] = a
        io[name] = nc.dram_tensor(f"in_{name}", a.shape, _mybir.dt.from_np(a.dtype), kind="ExternalInput").ap()
    for name, shape in _OUTS:
        io[name] = nc.dram_tensor(f"out_{name}", shape, _mybir.dt.float32, kind="ExternalOutput").ap()
    backbone(nc, io)
    r = _run(nc, [arrays], core_ids=[0])
    return tuple(r.results[0][f"out_{name}"] for name, _ in _OUTS)
```

```python
from contextlib import ExitStack

import concourse.bass as bass
from concourse import mybir
import numpy as np

F32 = mybir.dt.float32
F32R = mybir.dt.float32r
U32 = mybir.dt.uint32
I32 = mybir.dt.int32
BF16 = mybir.dt.bfloat16
ALU = mybir.AluOpType
ACT = mybir.ActivationFunctionType
AX = mybir.AxisListType

P = 128
D = 1024
KT = D // P
TILES = 3
TOK = TILES * P
DEPTH = 2
ALPHA = (2.0 * DEPTH) ** 0.25
LN_EPS = 1e-5
RMS_EPS = 1e-6
GRID_W = 64
HEADS = 8
NOPE, ROPE, VD = 64, 32, 64
QK = NOPE + ROPE
Q_RANK, KV_RANK = 256, 128
RH, RD = 8, 64
RW = RH * RD
Z_KV = Q_RANK
Z_PE = Z_KV + KV_RANK
Z_RQ = Z_PE + ROPE
Z_RK, Z_RV, Z_RG = Z_RQ + RW, Z_RQ + 2 * RW, Z_RQ + 3 * RW
EVEN_IN = Z_RG + RW
SH, SKV, SD = 16, 4, 64
SQ_DIM, SKV_DIM = SH * SD, SKV * SD
ODD_IN = SQ_DIM + 2 * SKV_DIM
WINDOW = 128
NE = 64
TOPK = 8
NG = 8
GE = NE // NG
TOPG = 4
FD = 256
ROUTED_SCALE = 2.5
NEG = -1e30
ASSIGNED = TOK * TOPK
OVER_BLOCKS = TILES - 1
OVER_KEYS = 24
FAR = 1.0e6

C_ID = 0
C_TRI = C_ID + P
C_ROPE_E = C_TRI + P
C_ROPE_O = C_ROPE_E + 2 * 2 * (ROPE // 2)
C_MASK = C_ROPE_O + 2 * 2 * (SD // 2)
C_DF = C_MASK + 2 * TOK
C_DB = C_DF + P
C_MF = C_DB + P
C_MB = C_MF + P
C_QF = C_MB + P
C_QB = C_QF + P
C_IOTA = C_QB + P
C_COL = C_IOTA + TOK
C_LT8 = C_COL + 4
C_KEY = C_LT8 + 64
C_SUM = C_KEY + 2 * NE
C_END = C_SUM + 2


def shape_tables():
    c = np.zeros((P, C_END), np.float32)
    r = np.arange(P)
    c[:, C_ID:C_ID + P] = np.eye(P)
    c[:, C_TRI:C_TRI + P] = r[:, None] < r[None, :]
    for at, dim in ((C_ROPE_E, ROPE), (C_ROPE_O, SD)):
        nf = dim // 4
        t = np.arange(2 * P)
        freqs = (np.float32(10000.0) ** (-np.arange(nf, dtype=np.float32) / np.float32(nf))).astype(np.float32)
        row = (t // GRID_W).astype(np.float32)
        col = (t % GRID_W).astype(np.float32)
        ang = np.concatenate([row[:, None] * freqs, col[:, None] * freqs], axis=-1)
        for j, f in enumerate((np.cos, np.sin)):
            tab = f(ang).astype(np.float32).reshape(2, P, 2 * nf)
            for i in range(2):
                o = at + (i * 2 + j) * 2 * nf
                c[:, o:o + 2 * nf] = tab[i]
    for i in range(2):
        q = i * P + r
        k = np.arange(2 * P)
        c[:, C_MASK + i * TOK:C_MASK + i * TOK + 2 * P] = np.where(np.abs(q[:, None] - k[None]) <= WINDOW, 0.0, NEG)
    d = r[None, :] - r[:, None]
    c[:, C_DF:C_DF + P] = np.maximum(d, 0)
    c[:, C_DB:C_DB + P] = np.maximum(-d, 0)
    c[:, C_MF:C_MF + P] = d >= 0
    c[:, C_MB:C_MB + P] = d <= 0
    c[:, C_QF:C_QF + P] = r + 1.0
    c[:, C_QB:C_QB + P] = P - r
    c[:, C_IOTA:C_IOTA + TOK] = np.arange(TOK)
    c[:, C_COL] = P - 1 - r
    c[:, C_COL + 1] = r
    c[:, C_LT8:C_LT8 + 64] = (np.arange(8)[None, :] < np.arange(8)[:, None]).reshape(1, 64)
    c[:, C_KEY:C_KEY + 2 * NE] = np.arange(2 * NE) + 1.0
    c[0:5, C_SUM:C_SUM + 2] = ((1, 0), (0, 1), (1, 0), (0, 1), (1, 1))
    return c


class Steps:

    def __init__(self, eng, sem):
        self.eng, self.sem, self.n = eng, sem, 0

    def mark(self, ins):
        self.n += 1
        ins.then_inc(self.sem, 1)

    def wait(self):
        self.eng.wait_ge(self.sem, self.n)

    def then(self, ins):
        self.mark(ins)
        self.wait()


class Kernel:

    def __init__(self, nc, ctx, io):
        self.nc, self.io = nc, io

        def sb(name, shape, dt=F32):
            return ctx.enter_context(nc.sbuf_tensor(name, shape, dt))

        self.const = sb("const", [P, C_END])
        self.ones = sb("ones", [P, P])
        self.x = sb("x_tok", [P, TILES, D])
        self.ring = sb("weights", [P, 12288])
        self.slot_u = sb("slot_u", [P, TILES, TOPK], U32)
        self.w8 = sb("w8", [P, TILES, TOPK])
        self.tok_idx = sb("tok_idx", [P, NE], U32)
        self.y_idx = sb("y_idx", [P, NE], U32)
        self.incl = sb("incl", [P, TILES, NE])
        self.bases = sb("bases", [P, 2, NE])
        self.over = sb("over", [P, 32], I32)
        self.ps = [ctx.enter_context(nc.psum_tensor(f"bank{i}", [P, 512], F32)) for i in range(8)]
        self.mod_d = nc.dram_tensor("mod_rows", [DEPTH, 2, 6 * D], F32, kind="Internal").ap()
        self.h_d = nc.dram_tensor("h_rows", [TOK, D], F32, kind="Internal").ap()
        self.y_d = nc.dram_tensor("y_rows", [ASSIGNED, D], F32, kind="Internal").ap()
        self.s_const = ctx.enter_context(nc.semaphore("const_loaded"))
        self.s_ahead = [ctx.enter_context(nc.semaphore(f"ahead{i}_loaded")) for i in range(5)]
        self.ahead = [0] * 5
        names = "rows0_gathered rows1_gathered y_stored ov_gathered ov_stored back0_in back1_in back2_in back3_in back4_in back5_in back6_in back7_in"
        self.pool_sems = [[ctx.enter_context(nc.semaphore(f"{n}_{layer}")) for n in names.split()] for layer in range(DEPTH)]

    def work_memory(self, ctx):
        def sb(name, shape, dt=F32):
            return ctx.enter_context(self.nc.sbuf_tensor(name, shape, dt))

        self.hT = sb("hT", [P, KT, TOK])
        self.z = sb("z", [P, TILES * EVEN_IN])
        self.uses = 0
        self.take_upper()
        ctx.callback(self.give_upper)

    def take_upper(self):
        self.upper = ExitStack()
        self.uses += 1

        def sb(name, shape):
            return self.upper.enter_context(self.nc.sbuf_tensor(f"{name}_{self.uses}", shape, F32))

        self.cat = sb("cat", [P, TILES, D])
        self.hP = sb("hP", [P, TILES, D])
        self.s = sb("scratch", [P, 15104])

    def give_upper(self):
        self.upper.close()

    def c(self, at, n, p=P):
        return self.const[0:p, at:at + n]

    @property
    def ident(self):
        return self.const[:, C_ID:C_ID + P]

    def load_ahead(self, eng, i, out, in_):
        eng.dma_start(out, in_).then_inc(self.s_ahead[i], 16)
        self.ahead[i] += 16

    def arrived(self, eng, i):
        eng.wait_ge(self.s_ahead[i], self.ahead[i])


class Stage(ExitStack):

    def __init__(self, nc):
        super().__init__()
        self.nc, self.used = nc, []

    def __exit__(self, *failure):
        super().__exit__(*failure)
        numbers = sorted(s.num for s in self.used)
        while numbers:
            n = 1
            while n < len(numbers) and numbers[n] == numbers[0] + n:
                n += 1
            self.nc.sync.sem_clear(range(numbers[0], numbers[0] + n))
            numbers = numbers[n:]


def sems(nc, ctx, names):
    found = [ctx.enter_context(nc.semaphore(n)) for n in names.split()]
    ctx.used += found
    return found


def stage_setup(k):
    nc, io = k.nc, k.io
    with Stage(nc) as ctx:
        s_x, s_one = sems(nc, ctx, "x_loaded ones_set")
        blk = ctx.enter_context(nc.Block())

        @blk.sync
        def _(sp):
            sp.dma_start(k.const[:], io["tables"]).then_inc(k.s_const, 16)
            sp.dma_start(k.x[:, 0, :], io["x_prompt"].rearrange("b s d -> (b s) d")).then_inc(s_x, 16)
            sp.dma_start(k.x[:, 1:3, :], io["x_sample"].rearrange("b (t p) d -> p (b t) d", p=P)).then_inc(s_x, 16)
            sp.wait_ge(s_x, 32)
            sp.wait_ge(k.s_const, 16)

        @blk.vector
        def _(dve):
            nc.vector.memset(k.ones[:], 1.0).then_inc(s_one, 1)


def stage_mod(k):
    nc, io = k.nc, k.io
    CH = 512
    NCH = 6 * D // CH
    SLOTS = 3
    n_all = DEPTH * NCH
    DVE_ROWS = KT - 1
    with Stage(nc) as ctx:
        def sb(name, shape, dt=F32):
            return ctx.enter_context(nc.sbuf_tensor(name, shape, dt))

        craw, ce = sb("cond_raw", [P, 2, KT]), sb("cond_exp", [P, 2, KT])
        cond, cond4 = sb("cond", [P, KT, 2]), sb("cond_parts", [P, KT, 4], F32R)
        w_hi, w_lo = sb("wmod_hi", [P, 2, KT, CH], F32R), sb("wmod_lo", [P, 2, KT, CH], F32R)
        parts = sb("mod_parts", [5, 6 * D])
        rows = sb("mod_row", [2, 6 * D])
        (s_c, s_e, s_d, s_silu, s_hi, s_lo, s_lop, s_mm, s_ev, s_sum, s_row, s_store, s_b) = sems(
            nc, ctx, "cond_loaded cond_exp cond_steps cond_silu wmod_rounded wmod_rest wmod_rest_pool parts_ready parts_copied "
                     "row_summed row_copied mod_stored bias_loaded")
        s_w = sems(nc, ctx, "wmod0_loaded wmod1_loaded wmod2_loaded")
        blk = ctx.enter_context(nc.Block())

        def slot(i):
            i %= SLOTS
            return k.ring[:, i * 4096:(i + 1) * 4096].rearrange("p (k n) -> p k n", k=KT)

        def cols(i):
            return slice(i % NCH * CH, (i % NCH + 1) * CH)

        @blk.sync
        def _(sp):
            sp.dma_start(craw[:, 0, :], io["c_ctx"].rearrange("(p k) -> p k", k=KT)).then_inc(s_c, 16)
            sp.dma_start(craw[:, 1, :], io["c"].rearrange("b (p k) -> p (b k)", k=KT)).then_inc(s_c, 16)
            sp.dma_start(parts[4:5, :], io["b_mod"][0:1, :]).then_inc(s_b, 16)
            for i in range(n_all):
                layer, c = divmod(i, NCH)
                if i >= SLOTS:
                    sp.wait_ge(s_lo, i - SLOTS + 1)
                    sp.wait_ge(s_lop, i - SLOTS + 1)
                src = io["w_mod"][layer].rearrange("(p k) n -> p k n", k=KT)[:, :, c * CH:(c + 1) * CH]
                sp.dma_start(slot(i), src).then_inc(s_w[i % SLOTS], 16)
                if c == SLOTS and layer:
                    sp.wait_ge(s_sum, layer * NCH)
                    sp.dma_start(parts[4:5, :], io["b_mod"][layer:layer + 1, :]).then_inc(s_b, 16)
                    sp.wait_ge(s_row, layer * NCH)
                    sp.dma_start(k.mod_d[layer - 1], rows[:]).then_inc(s_store, 16)
            sp.wait_ge(s_row, n_all)
            sp.dma_start(k.mod_d[DEPTH - 1], rows[:]).then_inc(s_store, 16)
            sp.wait_ge(s_store, 16 * DEPTH)

        @blk.scalar
        def _(act):
            act.wait_ge(s_c, 32)
            nc.scalar.activation(ce[:], craw[:], ACT.Exp, scale=-1.0).then_inc(s_e, 1)
            for i in range(n_all + 1):
                if i < n_all:
                    act.wait_ge(s_w[i % SLOTS], 16 * (i // SLOTS + 1))
                    if i >= 2:
                        act.wait_ge(s_mm, i - 1)
                    nc.scalar.copy(w_hi[:, i % 2], slot(i)).then_inc(s_hi, 1)
                if i >= 1:
                    j = i - 1
                    act.wait_ge(s_mm, j + 1)
                    if j >= NCH:
                        act.wait_ge(s_sum, j - NCH + 1)
                    nc.scalar.copy(parts[0:4, cols(j)], k.ps[j % 4][0:4, :]).then_inc(s_ev, 1)

        @blk.gpsimd
        def _(pool):
            for i in range(n_all):
                pool.wait_ge(s_hi, i + 1)
                nc.gpsimd.tensor_tensor(w_lo[:, i % 2, DVE_ROWS:KT], slot(i)[:, DVE_ROWS:KT], w_hi[:, i % 2, DVE_ROWS:KT].bitcast(F32),
                                        ALU.subtract).then_inc(s_lop, 1)

        @blk.vector
        def _(dve):
            st = Steps(dve, s_d)
            dve.wait_ge(s_e, 1)
            st.then(nc.vector.tensor_scalar(ce[:], ce[:], 1.0, None, ALU.add))
            st.then(nc.vector.reciprocal(ce[:], ce[:]))
            st.then(nc.vector.tensor_tensor(cond[:].rearrange("p k r -> p r k"), craw[:], ce[:], ALU.mult))
            st.then(nc.vector.tensor_copy(cond4[:, :, 0:2], cond[:]))
            nc.vector.tensor_tensor(cond4[:, :, 2:4], cond[:], cond4[:, :, 0:2].bitcast(F32), ALU.subtract).then_inc(s_silu, 1)
            for i in range(n_all + 2):
                if i < n_all:
                    dve.wait_ge(s_hi, i + 1)
                    nc.vector.tensor_tensor(w_lo[:, i % 2, 0:DVE_ROWS], slot(i)[:, 0:DVE_ROWS], w_hi[:, i % 2, 0:DVE_ROWS].bitcast(F32),
                                            ALU.subtract).then_inc(s_lo, 1)
                if i >= 2:
                    j = i - 2
                    dve.wait_ge(s_sum, j + 1)
                    if j >= NCH:
                        dve.wait_ge(s_store, 16 * (j // NCH))
                    nc.vector.tensor_copy(rows[:, cols(j)], k.ps[4 + j % 4][0:2, :]).then_inc(s_row, 1)

        @blk.tensor
        def _(pe):
            pe.wait_ge(s_silu, 1)
            for i in range(n_all + 1):
                if i < n_all:
                    pe.wait_ge(s_hi, i + 1)
                    if i >= 4:
                        pe.wait_ge(s_ev, i - 3)
                    for p, w in enumerate((w_hi, w_lo)):
                        if p:
                            pe.wait_ge(s_lo, i + 1)
                            pe.wait_ge(s_lop, i + 1)
                        for kk in range(KT):
                            m = nc.tensor.matmul(k.ps[i % 4][0:4, :], cond4[:, kk, :], w[:, i % 2, kk, :],
                                                 start=(p == 0 and kk == 0), stop=(p == 1 and kk == KT - 1))
                    m.then_inc(s_mm, 1)
                if i >= 1:
                    j = i - 1
                    pe.wait_ge(s_ev, j + 1)
                    pe.wait_ge(s_b, 16 * (j // NCH + 1))
                    if j >= 4:
                        pe.wait_ge(s_row, j - 3)
                    nc.tensor.matmul(k.ps[4 + j % 4][0:2, :], k.c(C_SUM, 2, 5), parts[:, cols(j)], start=True, stop=True).then_inc(s_sum, 1)


def table_load(k, eng, sem, out, layer, cond, part):
    eng.dma_start(out, k.mod_d[layer, cond:cond + 1, part * D:(part + 1) * D].to_broadcast([P, D])).then_inc(sem, 16)


def stage_modulate(k, layer, ahead):
    nc = k.nc
    tab = k.s[:, 0:4 * D].rearrange("p (c j n) -> p c j n", c=2, j=2)
    with Stage(nc) as ctx:
        s_p, s_t, s_d, s_h, s_tr = sems(nc, ctx, "prompt_table_loaded sample_table_loaded mod_steps h_ready turned")
        blk = ctx.enter_context(nc.Block())

        @blk.sync
        def _(sp):
            for cnd, sem in enumerate((s_p, s_t)):
                for j in (1, 0):
                    table_load(k, sp, sem, tab[:, cnd, j, :], layer, cnd, j)
            ahead(sp)

        @blk.tensor
        def _(pe):
            for t in range(TILES):
                pe_turn_tile(k, pe, t, (2 * t, 2 * t + 1), s_h, s_tr)

        @blk.scalar
        def _(act):
            for t in range(TILES):
                copy_turned(k, act, t, (2 * t, 2 * t + 1), s_tr)

        @blk.vector
        def _(dve):
            st = Steps(dve, s_d)
            for t in range(TILES):
                dve.wait_ge(s_t if t else s_p, 32)
                c = min(t, 1)
                h = k.hP[:, t, :]
                st.then(nc.vector.scalar_tensor_tensor(h, tab[:, c, 1, :], 1.0, k.x[:, t, :], ALU.add, ALU.mult))
                nc.vector.tensor_tensor(h, h, tab[:, c, 0, :], ALU.add).then_inc(s_h, 1)


def stage_transpose(k, src, ahead=None):
    nc = k.nc
    with Stage(nc) as ctx:
        s_tr, s_a, s_v = sems(nc, ctx, "turned copied_act copied_dve")
        blk = ctx.enter_context(nc.Block())
        n_banks = TILES * KT // 4

        @blk.sync
        def _(sp):
            if ahead:
                ahead(sp)

        @blk.tensor
        def _(pe):
            for b in range(n_banks):
                t, g = divmod(b, 2)
                for j in range(4):
                    kk = 4 * g + j
                    m = nc.tensor.transpose(k.ps[b][:, j * P:(j + 1) * P], src[:, t, kk * P:(kk + 1) * P], k.ident)
                m.then_inc(s_tr, 1)

        def copy(eng_copy, eng, sem, which):
            for b in range(which, n_banks, 2):
                t, g = divmod(b, 2)
                eng.wait_ge(s_tr, b + 1)
                eng_copy(k.hT[:, 4 * g:4 * g + 4, t * P:(t + 1) * P],
                         k.ps[b][:].rearrange("p (j n) -> p j n", j=4)).then_inc(sem, 1)

        @blk.scalar
        def _(act):
            copy(nc.scalar.copy, act, s_a, 0)

        @blk.vector
        def _(dve):
            copy(nc.vector.tensor_copy, dve, s_v, 1)


def ring_slot(k, i):
    return k.ring[:, i * 4096:(i + 1) * 4096].rearrange("p (k n) -> p k n", k=KT)


def chunks_of(n_cols):
    return [(c, min(512, n_cols - c)) for c in range(0, n_cols, 512)]


def early_slot(k):
    return k.s[:, 15104 - 4096:15104].rearrange("p (k n) -> p k n", k=KT)


def out_chunk(k, w, c):
    def ahead(sp):
        k.load_ahead(sp, c, (early_slot(k), ring_slot(k, 1))[c], w.rearrange("(k p) n -> p k n", p=P)[:, :, c * 512:(c + 1) * 512])
    return ahead


def first_chunks(k, w):
    def ahead(sp):
        for i, (c, n) in enumerate(chunks_of(w.shape[1])[:3]):
            k.load_ahead(sp, i, ring_slot(k, i)[:, :, 0:n], w.rearrange("(k p) n -> p k n", p=P)[:, :, c:c + n])
    return ahead


def stage_project(k, w, n_cols, out):
    nc = k.nc
    chunks = chunks_of(n_cols)
    N = len(chunks)
    KH = KT // 2
    k.give_upper()
    with Stage(nc) as ctx:
        def sb(name, shape):
            return ctx.enter_context(nc.sbuf_tensor(f"{name}_{k.uses}", shape, F32R))

        x_hi, x_lo = sb("x_hi", [P, KT, TOK]), sb("x_lo", [P, KT, TOK])
        w_hi, w_lo = sb("w_hi", [P, 2, KT, 512]), sb("w_lo", [P, 2, KT, 512])
        s_xh, s_xl, s_wh, s_wl, s_mm, s_a, s_v = sems(
            nc, ctx, "x_rounded x_rest w_rounded w_rest product_ready copied_act copied_dve")
        s_w = sems(nc, ctx, "w0_loaded w1_loaded w2_loaded")
        blk = ctx.enter_context(nc.Block())

        def half(v, h, n):
            return v[:, h * KH:(h + 1) * KH, 0:n]

        def tokens(v, t):
            return v[:, :, t * P:(t + 1) * P]

        @blk.sync
        def _(sp):
            for i, (c, n) in enumerate(chunks[3:]):
                sp.wait_ge(s_wl, 2 * (i + 1))
                sp.dma_start(ring_slot(k, i % 3)[:, :, 0:n], w.rearrange("(k p) n -> p k n", p=P)[:, :, c:c + n]).then_inc(s_w[i % 3], 16)

        @blk.tensor
        def _(pe):
            for i, (c, n) in enumerate(chunks):
                for t in range(TILES):
                    b = i * TILES + t
                    if b >= 8:
                        pe.wait_ge(s_v if b % 2 else s_a, (b - 8) // 2 + 1)
                    passes = ((x_hi, w_hi, s_xh, s_wh), (x_lo, w_hi, s_xl, s_wh), (x_hi, w_lo, s_xh, s_wl))
                    for a, (x, wp, s_x, s_wp) in enumerate(passes):
                        if i == 0:
                            pe.wait_ge(s_x, t + 1)
                        for kk in range(KT):
                            if t == 0 and kk % KH == 0:
                                pe.wait_ge(s_wp, 2 * i + kk // KH + 1)
                            m = nc.tensor.matmul(k.ps[b % 8][:, 0:n], x[:, kk, t * P:(t + 1) * P], wp[:, i % 2, kk, 0:n],
                                                 start=(a == 0 and kk == 0), stop=(a == 2 and kk == KT - 1))
                    m.then_inc(s_mm, 1)

        def copy(eng_copy, eng, sem, which, i):
            for b in range(TILES * i, TILES * (i + 1)):
                if b % 2 == which:
                    c, n = chunks[i]
                    eng.wait_ge(s_mm, b + 1)
                    eng_copy(out(b % TILES, c, n), k.ps[b % 8][:, 0:n]).then_inc(sem, 1)

        @blk.scalar
        def _(act):
            def round_x(t):
                nc.scalar.copy(tokens(x_hi, t), tokens(k.hT, t)).then_inc(s_xh, 1)

            def round_w(i):
                n = chunks[i][1]
                if i < 3:
                    k.arrived(act, i)
                else:
                    act.wait_ge(s_w[i % 3], 16 * (i // 3))
                if i >= 2:
                    act.wait_ge(s_mm, TILES * (i - 1))
                for h in range(2):
                    nc.scalar.copy(half(w_hi[:, i % 2], h, n), half(ring_slot(k, i % 3), h, n)).then_inc(s_wh, 1)

            round_x(0)
            round_w(0)
            round_x(1)
            round_x(2)
            for i in range(N):
                if i + 1 < N:
                    round_w(i + 1)
                copy(nc.scalar.copy, act, s_a, 0, i)

        @blk.vector
        def _(dve):
            def rest_x(t):
                dve.wait_ge(s_xh, t + 1)
                nc.vector.tensor_tensor(tokens(x_lo, t), tokens(k.hT, t), tokens(x_hi, t).bitcast(F32), ALU.subtract).then_inc(s_xl, 1)

            def rest_w(i):
                n = chunks[i][1]
                if i >= 2:
                    dve.wait_ge(s_mm, TILES * (i - 1))
                for h in range(2):
                    dve.wait_ge(s_wh, 2 * i + h + 1)
                    nc.vector.tensor_tensor(half(w_lo[:, i % 2], h, n), half(ring_slot(k, i % 3), h, n),
                                            half(w_hi[:, i % 2], h, n).bitcast(F32), ALU.subtract).then_inc(s_wl, 1)

            rest_x(0)
            rest_w(0)
            rest_x(1)
            rest_x(2)
            for i in range(N):
                if i + 1 < N:
                    rest_w(i + 1)
                copy(nc.vector.tensor_copy, dve, s_v, 1, i)
    k.take_upper()


def rope(nc, st, k, at, tile, x, tmp, heads, nf):
    o = at + tile * 4 * nf
    cos = k.const[:, o:o + 2 * nf].rearrange("p (a f) -> p a f", a=2)
    sin = k.const[:, o + 2 * nf:o + 4 * nf].rearrange("p (a f) -> p a f", a=2)
    n = heads * 2 * nf
    t1, t2, t3, t4 = (tmp[:, i * n:(i + 1) * n].rearrange("p (h a f) -> p h a f", a=2, f=nf) for i in range(4))
    for axis in range(2):
        cb = cos[:, axis:axis + 1, :].to_broadcast([P, heads, nf])
        sb = sin[:, axis:axis + 1, :].to_broadcast([P, heads, nf])
        x1, x2 = x[:, :, axis, 0, :], x[:, :, axis, 1, :]
        st.mark(nc.vector.tensor_tensor(t1[:, :, axis, :], x1, cb, ALU.mult))
        st.mark(nc.vector.tensor_tensor(t2[:, :, axis, :], x2, sb, ALU.mult))
        st.mark(nc.vector.tensor_tensor(t3[:, :, axis, :], x2, cb, ALU.mult))
        st.mark(nc.vector.tensor_tensor(t4[:, :, axis, :], x1, sb, ALU.mult))
    st.wait()
    for axis in range(2):
        x1, x2 = x[:, :, axis, 0, :], x[:, :, axis, 1, :]
        st.mark(nc.vector.tensor_tensor(x1, t1[:, :, axis, :], t2[:, :, axis, :], ALU.subtract))
        st.mark(nc.vector.tensor_tensor(x2, t3[:, :, axis, :], t4[:, :, axis, :], ALU.add))
    st.wait()


def stage_mla_norm(k, e):
    nc, io = k.nc, k.io
    z = k.z[:].rearrange("p (t n) -> p t n", t=TILES)
    m = k.mla
    tmp = k.s[:, 14080:14080 + 1024]
    with Stage(nc) as ctx:
        s_l, s_sq, s_d, s_p, s_out = sems(nc, ctx, "norm_loaded squares_summed dve_steps rstd_ready outputs_stored")
        s_ms = sems(nc, ctx, "mean_squares")[0]
        s_n = sems(nc, ctx, "normed")[0]
        blk = ctx.enter_context(nc.Block())

        @blk.sync
        def _(sp):
            sp.dma_start(m["qg"], io["mla_q_norm"][e:e + 1, :].to_broadcast([P, Q_RANK])).then_inc(s_l, 16)
            sp.dma_start(m["kvg"], io["mla_kv_norm"][e:e + 1, :].to_broadcast([P, KV_RANK])).then_inc(s_l, 16)
            sp.dma_start(m["ckv"][:, 3, :], io["cache_mla_ckv"][0, e]).then_inc(s_l, 16)
            sp.dma_start(m["kpe"][:, 3, NOPE:QK], io["cache_mla_kpe"][0, e]).then_inc(s_l, 16)
            k.load_ahead(sp, 0, m["wuq"], io["mla_w_uq"][e].rearrange("(k p) n -> p k n", p=P))
            k.load_ahead(sp, 1, m["wuk"], io["mla_w_uk"][e])
            k.load_ahead(sp, 1, m["wuv"], io["mla_w_uv"][e])
            sp.wait_ge(s_n, 1)
            sp.dma_start(io["new_mla_ckv"][0, e], m["ckv"][:, 0, :]).then_inc(s_out, 16)
            sp.dma_start(io["new_mla_kpe"][0, e], z[:, 0, Z_PE:Z_RQ]).then_inc(s_out, 16)
            sp.wait_ge(s_out, 32)
            sp.wait_ge(s_l, 64)

        @blk.scalar
        def _(act):
            for t in range(TILES):
                nc.scalar.activation(m["junk"][:, 0:Q_RANK], z[:, t, 0:Z_KV], ACT.Square, accum_out=m["ss"][:, t:t + 1]).then_inc(s_sq, 1)
                act.wait_ge(s_sq, 2 * t + 1)
                nc.scalar.activation(m["junk"][:, 0:KV_RANK], z[:, t, Z_KV:Z_PE], ACT.Square, accum_out=m["ss"][:, 3 + t:4 + t]).then_inc(s_sq, 1)
                act.wait_ge(s_sq, 2 * t + 2)

        @blk.gpsimd
        def _(pool):
            pool.wait_ge(s_ms, 2)
            nc.gpsimd.tensor_tensor(m["rstd"], m["ss"], m["half"], ALU.pow).then_inc(s_p, 1)

        @blk.vector
        def _(dve):
            st = Steps(dve, s_d)
            st.mark(nc.vector.memset(m["half"], -0.5))
            st.mark(nc.vector.memset(m["kpe"][:, :, 0:NOPE], 0.0))
            st.wait()
            dve.wait_ge(s_sq, 2 * TILES)
            nc.vector.tensor_scalar(m["ss"][:, 0:3], m["ss"][:, 0:3], 1.0 / Q_RANK, RMS_EPS, ALU.mult, ALU.add).then_inc(s_ms, 1)
            nc.vector.tensor_scalar(m["ss"][:, 3:6], m["ss"][:, 3:6], 1.0 / KV_RANK, RMS_EPS, ALU.mult, ALU.add).then_inc(s_ms, 1)
            dve.wait_ge(s_p, 1)
            dve.wait_ge(s_l, 64)
            for t in range(TILES):
                st.mark(nc.vector.scalar_tensor_tensor(m["qn"][:, t, :], z[:, t, 0:Z_KV], m["rstd"][:, t:t + 1], m["qg"], ALU.mult, ALU.mult))
                st.mark(nc.vector.scalar_tensor_tensor(m["ckv"][:, t, :], z[:, t, Z_KV:Z_PE], m["rstd"][:, 3 + t:4 + t], m["kvg"], ALU.mult, ALU.mult))
            st.mark(nc.vector.tensor_copy(m["kpe"][:, 0, NOPE:QK], z[:, 0, Z_PE:Z_RQ]))
            st.wait()
            nc.vector.memset(m["junk"][:, 0:1], 0.0).then_inc(s_n, 1)
            for t in (1, 2):
                x = z[:, t, Z_PE:Z_RQ].rearrange("p (h a b f) -> p h a b f", h=1, a=2, b=2)
                rope(nc, st, k, C_ROPE_E, t - 1, x, tmp, 1, ROPE // 4)
                st.then(nc.vector.tensor_copy(m["kpe"][:, t, NOPE:QK], z[:, t, Z_PE:Z_RQ]))


def stage_mla_keys(k, e):
    nc = k.nc
    m = k.mla
    tmp = k.s[:, 14080:14080 + 1024]
    with Stage(nc) as ctx:
        s_tr, s_a, s_v, s_d = sems(nc, ctx, "pe_ready copied_act copied_dve dve_steps")
        blk = ctx.enter_context(nc.Block())

        @blk.tensor
        def _(pe):
            for t in range(4):
                mm = nc.tensor.transpose(k.ps[0][:, t * P:(t + 1) * P], m["ckv"][:, t, :], k.ident)
            mm.then_inc(s_tr, 1)
            for t in range(4):
                mm = nc.tensor.transpose(k.ps[1][0:QK, t * P:(t + 1) * P], m["kpe"][:, t, :], k.ident)
            mm.then_inc(s_tr, 1)
            for j in range(2):
                for t in range(TILES):
                    mm = nc.tensor.transpose(k.ps[2 + j][:, t * P:(t + 1) * P], m["qn"][:, t, j * P:(j + 1) * P], k.ident)
                mm.then_inc(s_tr, 1)
            k.arrived(pe, 0)
            pe.wait_ge(s_v, 2)
            for t in range(TILES):
                for j, (c, n) in enumerate(((0, 512), (512, 256))):
                    i = 2 * t + j
                    if i >= 2:
                        pe.wait_ge(s_v, 2 + i - 1)
                    for kk in range(2):
                        mm = nc.tensor.matmul(k.ps[4 + j][:, 0:n], m["qnT"][:, kk, t * P:(t + 1) * P], m["wuq"][:, kk, c:c + n],
                                              start=(kk == 0), stop=(kk == 1))
                    mm.then_inc(s_tr, 1)
            k.arrived(pe, 1)
            pe.wait_ge(s_a, 1)
            for h in range(HEADS):
                if h >= 2:
                    pe.wait_ge(s_a, 2 + h - 1)
                nc.tensor.matmul(k.ps[6 + h % 2][0:NOPE, :], m["wuk"][:, h * NOPE:(h + 1) * NOPE], m["ckvT"], start=True, stop=True).then_inc(s_tr, 1)
            pe.wait_ge(s_a, 2)
            pe.wait_ge(s_v, 2)
            for t in range(4):
                nc.tensor.matmul(k.ps[t][:], m["ckvT"][:, t * P:(t + 1) * P], m["wuv"], start=True, stop=True).then_inc(s_tr, 1)

        @blk.scalar
        def _(act):
            act.wait_ge(s_tr, 1)
            nc.scalar.copy(m["ckvT"], k.ps[0][:]).then_inc(s_a, 1)
            act.wait_ge(s_tr, 2)
            nc.scalar.copy(m["kpeT"][NOPE:QK, :], k.ps[1][NOPE:QK, :]).then_inc(s_a, 1)
            for h in range(HEADS):
                act.wait_ge(s_tr, 11 + h)
                nc.scalar.copy(m["kT"][0:NOPE, h, :], k.ps[6 + h % 2][0:NOPE, :]).then_inc(s_a, 1)
            for t in range(4):
                act.wait_ge(s_tr, 19 + t)
                nc.scalar.copy(m["v"][:, t, :], k.ps[t][:]).then_inc(s_a, 1)

        @blk.vector
        def _(dve):
            st = Steps(dve, s_d)
            for j in range(2):
                dve.wait_ge(s_tr, 3 + j)
                nc.vector.tensor_copy(m["qnT"][:, j, :], k.ps[2 + j][:, 0:TOK]).then_inc(s_v, 1)
            for t in range(TILES):
                for j, (c, n) in enumerate(((0, 512), (512, 256))):
                    dve.wait_ge(s_tr, 5 + 2 * t + j)
                    nc.vector.tensor_copy(m["q"][:, t, c:c + n], k.ps[4 + j][:, 0:n]).then_inc(s_v, 1)
            dve.wait_ge(s_a, 2)
            st.mark(nc.vector.tensor_copy(m["kT"][NOPE:QK, :, :], m["kpeT"][NOPE:QK, :].rearrange("p (o n) -> p o n", o=1).to_broadcast([ROPE, HEADS, 512])))
            dve.wait_ge(s_v, 2 + 2 * TILES)
            for t in (1, 2):
                x = m["q"][:, t, :].rearrange("p (h d) -> p h d", h=HEADS)[:, :, NOPE:QK].rearrange("p h (a b f) -> p h a b f", a=2, b=2)
                rope(nc, st, k, C_ROPE_E, t - 1, x, tmp, HEADS, ROPE // 4)


def stage_turn_heads(k, jobs):
    nc = k.nc
    mine, done = ([], []), []
    for b, (_, parts) in enumerate(jobs):
        for part in parts:
            which = (len(mine[0]) + len(mine[1])) % 2
            mine[which].append((b, part))
        done.append((len(mine[0]), len(mine[1])))
    with Stage(nc) as ctx:
        s_tr, s_a, s_v = sems(nc, ctx, "turned copied_act copied_dve")
        blk = ctx.enter_context(nc.Block())

        @blk.tensor
        def _(pe):
            for b, (srcs, _) in enumerate(jobs):
                if b >= 8:
                    ge(pe, s_a, done[b - 8][0])
                    ge(pe, s_v, done[b - 8][1])
                for j, src in enumerate(srcs):
                    m = nc.tensor.transpose(k.ps[b % 8][0:src.shape[1], j * P:(j + 1) * P], src, k.ident)
                m.then_inc(s_tr, 1)

        def copy(eng_copy, eng, sem, which):
            for b, (lo, hi, dst) in mine[which]:
                eng.wait_ge(s_tr, b + 1)
                n = len(jobs[b][0])
                eng_copy(dst, k.ps[b % 8][lo:hi, 0:n * P].rearrange("p (j n) -> p j n", n=P)).then_inc(sem, 1)

        @blk.scalar
        def _(act):
            copy(nc.scalar.copy, act, s_a, 0)

        @blk.vector
        def _(dve):
            copy(nc.vector.tensor_copy, dve, s_v, 1)


GROUP = 4


def stage_attention(k, groups, scale, ahead=None, beside=None):
    nc = k.nc
    G = len(groups)
    masked = [g.get("mask") is not None for g in groups]
    sc = k.s[:, 0:2 * GROUP * TOK].rearrange("p (b h n) -> p b h n", b=2, h=GROUP)
    o = 2 * GROUP * TOK
    pr = k.s[:, o:o + 3 * GROUP * TOK].rearrange("p (b h n) -> p b h n", b=3, h=GROUP)
    o += 3 * GROUP * TOK
    pt = k.s[:, o:o + 2 * TOK].rearrange("p (b n) -> p b n", b=2)
    o += 2 * TOK
    st_ = k.s[:, o:o + 5 * GROUP * G]
    mx, nb, sm, si, rc = (st_[:, i * GROUP * G:(i + 1) * GROUP * G] for i in range(5))
    with Stage(nc) as ctx:
        s_s, s_mk, s_mx, s_e, s_t, s_pt, s_pv, s_se, s_out, s_d = sems(
            nc, ctx, "scores_ready scores_masked max_ready probs_ready turned probsT_ready values_summed sink_exp out_ready dve_steps")
        s_b = sems(nc, ctx, "beside_steps")[0]
        blk = ctx.enter_context(nc.Block())

        @blk.sync
        def _(sp):
            if ahead:
                ahead(sp)

        @blk.tensor
        def _(pe):
            def scores(g):
                h = groups[g]
                for j in range(GROUP):
                    if g >= 1 and masked[g - 1]:
                        pe.wait_ge(s_mk, GROUP * sum(masked[:g - 1]) + j + 1)
                    elif g >= 1:
                        pe.wait_ge(s_e, GROUP * (g - 1) + j + 1)
                    nc.tensor.matmul(k.ps[j][:, 0:h["n"]], h["q"][j], h["keys"][j], start=True, stop=True).then_inc(s_s, 1)

            def turn(i):
                g, j = divmod(i, GROUP)
                pe.wait_ge(s_e, i + 1)
                if i >= 2:
                    pe.wait_ge(s_pt, i - 1)
                for c in range(groups[g]["n"] // P):
                    m = nc.tensor.transpose(k.ps[4 + i % 2][:, c * P:(c + 1) * P], pr[:, g % 3, j, c * P:(c + 1) * P], k.ident)
                m.then_inc(s_t, 1)

            def values(i):
                g, j = divmod(i, GROUP)
                pe.wait_ge(s_pt, i + 1)
                if g >= 2:
                    pe.wait_ge(s_out, g - 1)
                nk = groups[g]["n"] // P
                for c in range(nk):
                    m = nc.tensor.matmul(k.ps[6 + g % 2][:, j * VD:(j + 1) * VD], pt[:, i % 2, c * P:(c + 1) * P], groups[g]["v"][j][c],
                                         start=(c == 0), stop=(c == nk - 1))
                m.then_inc(s_pv, 1)

            for g in range(G + 2):
                if g < G:
                    scores(g)
                if g >= 2:
                    first = GROUP * (g - 2)
                    for j in range(GROUP + 1):
                        if j < GROUP:
                            turn(first + j)
                        if j >= 1:
                            values(first + j - 1)

        @blk.scalar
        def _(act):
            st = Steps(act, s_b)
            for g in range(G + 2):
                if g >= 2:
                    n = groups[g - 2]["n"]
                    for i in range(GROUP * (g - 2), GROUP * (g - 1)):
                        act.wait_ge(s_t, i + 1)
                        if i >= 2:
                            act.wait_ge(s_pv, i - 1)
                        nc.scalar.copy(pt[:, i % 2, 0:n], k.ps[4 + i % 2][:, 0:n]).then_inc(s_pt, 1)
                if g < G:
                    h = groups[g]
                    n = h["n"]
                    act.wait_ge(s_mx, g + 1)
                    if g >= 3:
                        act.wait_ge(s_t, GROUP * (g - 2))
                    if h.get("sink") is not None:
                        v = si[:, GROUP * g:GROUP * (g + 1)]
                        nc.scalar.activation(v, v, ACT.Exp).then_inc(s_se, 1)
                    for j in range(GROUP):
                        i = GROUP * g + j
                        src = sc[:, g % 2, j, 0:n] if masked[g] else k.ps[j][:, 0:n]
                        nc.scalar.activation(pr[:, g % 3, j, 0:n], src, ACT.Exp, bias=nb[:, i:i + 1], scale=1.0 if masked[g] else scale,
                                             accum_out=sm[:, i:i + 1]).then_inc(s_e, 1)
                if beside:
                    beside(act, st, g)

        @blk.vector
        def _(dve):
            st = Steps(dve, s_d)

            def maxima(g):
                h = groups[g]
                n = h["n"]
                cols = slice(GROUP * g, GROUP * (g + 1))
                if masked[g] and g >= 2:
                    dve.wait_ge(s_e, GROUP * (g - 1))
                for j in range(GROUP):
                    i = GROUP * g + j
                    dve.wait_ge(s_s, i + 1)
                    if masked[g]:
                        nc.vector.scalar_tensor_tensor(sc[:, g % 2, j, 0:n], k.ps[j][:, 0:n], scale, h["mask"], ALU.mult, ALU.add).then_inc(s_mk, 1)
                    else:
                        st.mark(nc.vector.tensor_reduce(mx[:, i:i + 1], k.ps[j][:, 0:n], AX.X, ALU.max))
                if masked[g]:
                    dve.wait_ge(s_mk, GROUP * sum(masked[:g + 1]))
                    st.mark(nc.vector.tensor_reduce(mx[:, cols], sc[:, g % 2, :, 0:n], AX.X, ALU.max))
                st.wait()
                sl = 1.0 if masked[g] else scale
                if h.get("sink") is not None:
                    st.then(nc.vector.scalar_tensor_tensor(mx[:, cols], mx[:, cols], sl, h["sink"], ALU.mult, ALU.max))
                    st.mark(nc.vector.tensor_tensor(si[:, cols], h["sink"], mx[:, cols], ALU.subtract))
                    sl = 1.0
                nc.vector.tensor_scalar(nb[:, cols], mx[:, cols], -sl, None, ALU.mult).then_inc(s_mx, 1)

            def finish(g):
                h = groups[g]
                cols = slice(GROUP * g, GROUP * (g + 1))
                dve.wait_ge(s_e, GROUP * (g + 1))
                if h.get("sink") is not None:
                    dve.wait_ge(s_se, sum(x.get("sink") is not None for x in groups[:g + 1]))
                    st.then(nc.vector.tensor_tensor(sm[:, cols], sm[:, cols], si[:, cols], ALU.add))
                st.then(nc.vector.reciprocal(rc[:, cols], sm[:, cols]))
                dve.wait_ge(s_pv, GROUP * (g + 1))
                nc.vector.tensor_tensor(h["out"], k.ps[6 + g % 2][:, 0:GROUP * VD].rearrange("p (h n) -> p h n", h=GROUP),
                                        rc[:, cols].rearrange("p (h o) -> p h o", o=1).to_broadcast([P, GROUP, VD]), ALU.mult).then_inc(s_out, 1)

            for g in range(G + 2):
                if g < G:
                    maxima(g)
                if g >= 2:
                    finish(g - 2)


class RetentionTables:

    def __init__(self, k):
        s = k.s
        self.lg = s[:, 9400:9416]
        self.kdec = s[:, 9416:9432].rearrange("p (d h) -> p d h", d=2)
        self.cdec = s[:, 9432:9448]
        self.gn = s[:, 9448:9448 + RW]
        self.S0 = s[0:RD, 9960:9960 + 2 * RW].rearrange("p (d n) -> p d n", d=2)
        hP = k.hP[:].rearrange("p t n -> p (t n)")
        hT = k.hT[:].rearrange("p k n -> p (k n)")
        self.DT = hP[:, 0:2 * RH * P].rearrange("p (d h n) -> p d h n", d=2, h=RH)
        self.qdec = hT[0:RD, 0:2 * RH * P].rearrange("p (d h n) -> p d h n", d=2, h=RH)


def load_retention(k, e):
    def ahead(sp):
        W = RetentionTables(k)
        for d, n in enumerate(("ret_decay_fwd", "ret_decay_bwd")):
            k.load_ahead(sp, 2, W.lg[:, d * RH:(d + 1) * RH], k.io[n][e:e + 1, :].to_broadcast([P, RH]))
        k.load_ahead(sp, 3, W.gn, k.io["ret_gn_g"][e:e + 1, :].to_broadcast([P, RW]))
        for d, n in enumerate(("state_ret_fwd", "state_ret_bwd")):
            k.load_ahead(sp, 3, W.S0[:, d, :].rearrange("p (h n) -> p h n", h=RH), k.io[n][0, e].rearrange("h d n -> d h n"))
    return ahead


def retention_decays(k, act, st, h):
    nc, W = k.nc, RetentionTables(k)
    if h == 0:
        k.arrived(act, 2)
        st.then(nc.scalar.activation(W.lg, W.lg, ACT.Exp, scale=-1.0))
        st.then(nc.scalar.activation(W.lg, W.lg, ACT.Ln, bias=1.0))
        st.then(nc.scalar.mul(W.lg, W.lg, -1.0))
        for d in range(2):
            nc.scalar.activation(W.kdec[:, d, :], W.lg[:, d * RH:(d + 1) * RH], ACT.Exp, scale=k.const[:, C_COL + d:C_COL + d + 1])
            nc.scalar.activation(W.cdec[:, d * RH:(d + 1) * RH], W.lg[:, d * RH:(d + 1) * RH], ACT.Exp, scale=float(P))
    for d in range(2):
        col = W.lg[:, d * RH + h:d * RH + h + 1]
        nc.scalar.activation(W.DT[:, d, h, :], k.c((C_DF, C_DB)[d], P), ACT.Exp, scale=col)
        nc.scalar.activation(W.qdec[:, d, h, :], k.c((C_QF, C_QB)[d], P, RD), ACT.Exp, scale=col[0:RD])


def stage_retention(k, e, ahead):
    nc, io = k.nc, k.io
    z = k.z[:].rearrange("p (t n) -> p t n", t=TILES)
    R = k.ring
    qT = R[0:RD, 0:3072].rearrange("p (t h n) -> p t h n", t=TILES, h=RH)
    kT = R[0:RD, 3072:6144].rearrange("p (t h n) -> p t h n", t=TILES, h=RH)
    qd = R[0:RD, 6144:10240].rearrange("p (d t h n) -> p d t h n", d=2, t=2, h=RH)
    kd = R[:, 10240:12288].rearrange("p (j n) -> p j n", j=4)
    W = RetentionTables(k)
    DT, qdec, S0, gn = W.DT, W.qdec, W.S0, W.gn
    o = 0

    def cut(n, p=P):
        nonlocal o
        o += n
        return k.s[0:p, o - n:o]

    S1 = cut(4 * RW, RD).rearrange("p (j n) -> p j n", j=4)
    AT = cut(4 * P).rearrange("p (b d n) -> p b d n", b=2, d=2)
    raw = cut(2 * RW)
    sq = cut(2 * RW)
    mu, var, half = cut(16), cut(16), cut(16)
    gate = cut(RW)
    assert o <= 9400, o
    STATES = ((0, 0), (1, 0), (0, 1), (1, 2))
    STATE_BANK = (2, 3, 6, 7)
    with Stage(nc) as ctx:
        s_d, s_p, s_pw, s_st, s_sc, s_store, s_ss, s_ssa = sems(
            nc, ctx, "dve_steps rstd_ready var_ready state_ready keys_scaled states_stored states_updated states_copied")
        s_at, s_am, s_o, s_or, s_gt, s_qd, s_gu = sems(
            nc, ctx, "attn_ready attn_masked out_summed out_read gate_exp q_decayed gate_used")
        blk = ctx.enter_context(nc.Block())

        @blk.sync
        def _(sp):
            ahead(sp)
            sp.wait_ge(s_ssa, 2)
            for d, n in enumerate(("new_ret_fwd", "new_ret_bwd")):
                sp.dma_start(io[n][0, e].rearrange("h d n -> d h n"), S1[:, d, :].rearrange("p (h n) -> p h n", h=RH)).then_inc(s_store, 16)
            sp.wait_ge(s_store, 32)

        @blk.scalar
        def _(act):
            nc.scalar.activation(gate, z[:, 0, Z_RG:EVEN_IN], ACT.Exp, scale=-1.0).then_inc(s_gt, 1)
            for j in range(2):
                act.wait_ge(s_st, j + 1)
                nc.scalar.copy(S1[:, j, :], k.ps[STATE_BANK[j]][0:RD, :]).then_inc(s_ssa, 1)
            for t in range(1, TILES):
                act.wait_ge(s_gu, t)
                nc.scalar.activation(gate, z[:, t, Z_RG:EVEN_IN], ACT.Exp, scale=-1.0).then_inc(s_gt, 1)

        @blk.gpsimd
        def _(pool):
            for t in range(TILES):
                pool.wait_ge(s_pw, t + 1)
                nc.gpsimd.tensor_tensor(var, var, half, ALU.pow).then_inc(s_p, 1)

        @blk.tensor
        def _(pe):
            def attend(i):
                t, h = divmod(i, RH)
                if i >= 2:
                    pe.wait_ge(s_am, 2 * (i - 1))
                nc.tensor.matmul(k.ps[i % 2][:, 0:P], kT[:, t, h, :], qT[:, t, h, :], start=True, stop=True).then_inc(s_at, 1)

            def values(j):
                t, h = divmod(j, RH)
                pe.wait_ge(s_am, 2 * (j + 1))
                if h == 0 and t == 1:
                    pe.wait_ge(s_ss, 2)
                    pe.wait_ge(s_qd, 1)
                if h == 0 and t == 2:
                    pe.wait_ge(s_or, 1)
                v = z[:, t, Z_RV + h * RD:Z_RV + (h + 1) * RD]
                for d in range(2):
                    out = k.ps[4 + 2 * (t % 2) + d][:, h * RD:(h + 1) * RD]
                    m = nc.tensor.matmul(out, AT[:, j % 2, d, :], v, start=True, stop=(t == 0))
                    if t:
                        first = (t == 1) == (d == 0)
                        S = S0[:, d, :] if first else S1[:, 2 + d, :]
                        m = nc.tensor.matmul(out, qd[:, d, t - 1, h, :], S[:, h * RD:(h + 1) * RD], start=False, stop=True)
                m.then_inc(s_o, 1)

            def states():
                pe.wait_ge(s_sc, 1)
                for j, (d, t) in enumerate(STATES):
                    for h in range(RH):
                        m = nc.tensor.matmul(k.ps[STATE_BANK[j]][0:RD, h * RD:(h + 1) * RD], kd[:, j, h * RD:(h + 1) * RD],
                                             z[:, t, Z_RV + h * RD:Z_RV + (h + 1) * RD], start=True, stop=True)
                    m.then_inc(s_st, 1)

            for i in range(TILES * RH + 1):
                if i < TILES * RH:
                    attend(i)
                if i >= 1:
                    values(i - 1)
                if i == RH - 2:
                    states()

        @blk.vector
        def _(dve):
            st = Steps(dve, s_d)

            def prepare(part):
                if part < 2:
                    for j in (2 * part, 2 * part + 1):
                        d, t = STATES[j]
                        st.then(nc.vector.tensor_tensor(kd[:, j, :].rearrange("p (h n) -> p h n", h=RH),
                                                        z[:, t, Z_RK:Z_RV].rearrange("p (h n) -> p h n", h=RH),
                                                        W.kdec[:, d, :].rearrange("p (h o) -> p h o", o=1).to_broadcast([P, RH, RD]), ALU.mult))
                elif part == 2:
                    nc.vector.tensor_scalar(kd, kd, RD ** -0.5, None, ALU.mult).then_inc(s_sc, 1)
                elif part < 7:
                    d, t = divmod(part - 3, 2)
                    m = nc.vector.tensor_tensor(qd[:, d, t], qT[:, t + 1], qdec[:, d], ALU.mult)
                    if part == 6:
                        m.then_inc(s_qd, 1)

            def sample_states():
                for j, (d, t) in enumerate(STATES):
                    if t:
                        sv = S1[:, j, :].rearrange("p (h n) -> p h n", h=RH)
                        st.then(nc.vector.tensor_tensor(sv, S0[:, d, :].rearrange("p (h n) -> p h n", h=RH),
                                                        W.cdec[0:RD, d * RH:(d + 1) * RH].rearrange("p (h o) -> p h o", o=1).to_broadcast([RD, RH, RD]), ALU.mult))
                        dve.wait_ge(s_st, j + 1)
                        nc.vector.tensor_tensor(S1[:, j, :], S1[:, j, :], k.ps[STATE_BANK[j]][0:RD, :], ALU.add).then_inc(s_ss, 1)

            heads2 = lambda v: v.rearrange("p (h n) -> p h n", n=RD)
            bc2 = lambda v: v.rearrange("p (h o) -> p h o", o=1).to_broadcast([P, 2 * RH, RD])

            def norm(t, part):
                if part == 0:
                    dve.wait_ge(s_o, RH * (t + 1))
                    for d in range(2):
                        m = nc.vector.tensor_copy(raw[:, d * RW:(d + 1) * RW], k.ps[4 + 2 * (t % 2) + d][:])
                    m.then_inc(s_or, 1)
                    dve.wait_ge(s_or, t + 1)
                elif part == 1:
                    st.then(nc.vector.tensor_reduce(mu, heads2(raw), AX.X, ALU.add))
                    st.then(nc.vector.tensor_scalar(mu, mu, 1.0 / RD, None, ALU.mult))
                elif part == 2:
                    st.then(nc.vector.tensor_tensor(heads2(raw), heads2(raw), bc2(mu), ALU.subtract))
                elif part == 3:
                    st.then(nc.vector.tensor_tensor(sq, raw, raw, ALU.mult))
                elif part == 4:
                    st.then(nc.vector.tensor_reduce(var, heads2(sq), AX.X, ALU.add))
                    nc.vector.tensor_scalar(var, var, 1.0 / RD, LN_EPS, ALU.mult, ALU.add).then_inc(s_pw, 1)
                elif part == 5:
                    dve.wait_ge(s_p, t + 1)
                    st.then(nc.vector.tensor_tensor(heads2(raw), heads2(raw), bc2(var), ALU.mult))
                elif part == 6:
                    st.then(nc.vector.tensor_tensor(sq[:, 0:RW], raw[:, 0:RW], raw[:, RW:2 * RW], ALU.add))
                    st.then(nc.vector.tensor_tensor(sq[:, 0:RW], sq[:, 0:RW], gn, ALU.mult))
                else:
                    dve.wait_ge(s_gt, t + 1)
                    st.then(nc.vector.tensor_scalar(gate, gate, 1.0, None, ALU.add))
                    st.then(nc.vector.reciprocal(gate, gate))
                    nc.vector.tensor_tensor(sq[:, 0:RW], sq[:, 0:RW], gate, ALU.mult).then_inc(s_gu, 1)
                    dve.wait_ge(s_gu, t + 1)
                    nc.vector.tensor_tensor(k.cat[:, t, HEADS * VD:D], sq[:, 0:RW], z[:, t, Z_RG:EVEN_IN], ALU.mult)

            st.mark(nc.vector.memset(half, -0.5))
            for d in range(2):
                st.mark(nc.vector.tensor_tensor(DT[:, d], DT[:, d], k.c((C_MF, C_MB)[d], P).rearrange("p (o n) -> p o n", o=1).to_broadcast([P, RH, P]), ALU.mult))
            k.arrived(dve, 3)
            st.wait()
            for i in range(TILES * RH):
                t, h = divmod(i, RH)
                if i == RH:
                    sample_states()
                dve.wait_ge(s_at, i + 1)
                if i >= 2:
                    dve.wait_ge(s_o, i - 1)
                for d in range(2):
                    nc.vector.scalar_tensor_tensor(AT[:, i % 2, d, :], k.ps[i % 2][:, 0:P], RD ** -0.5, DT[:, d, h, :], ALU.mult, ALU.mult).then_inc(s_am, 1)
                if t == 0:
                    prepare(h)
                else:
                    norm(t - 1, h)
            for part in range(8):
                norm(TILES - 1, part)


def retention_jobs(k):
    z = k.z[:].rearrange("p (t n) -> p t n", t=TILES)
    R = k.ring
    jobs = []
    for base, at in ((Z_RQ, 0), (Z_RK, 3072)):
        dst = R[0:RD, at:at + 3072].rearrange("p (t h n) -> p t h n", t=TILES, h=RH)
        for t in range(TILES):
            for g in range(2):
                jobs.append(([z[:, t, base + (4 * g + j) * RD:base + (4 * g + j + 1) * RD] for j in range(4)], [(0, RD, dst[:, t, 4 * g:4 * g + 4, :])]))
    return jobs


def stage_swa_prep(k, o):
    nc, io = k.nc, k.io
    z = k.zo
    tmp = k.s[:, 0:4 * SH * SD // 2]
    with Stage(nc) as ctx:
        s_l, s_d, s_z, s_out = sems(nc, ctx, "context_loaded dve_steps zeroed outputs_stored")
        blk = ctx.enter_context(nc.Block())

        @blk.sync
        def _(sp):
            sp.dma_start(k.kctx, io["cache_swa_k"][0, o].rearrange("s h d -> s (h d)")).then_inc(s_l, 16)
            sp.dma_start(k.vctx, io["cache_swa_v"][0, o].rearrange("s h d -> s (h d)")).then_inc(s_l, 16)
            sp.dma_start(k.sink, io["swa_sink"][o:o + 1, :].to_broadcast([P, SH])).then_inc(s_l, 16)
            sp.dma_start(io["new_swa_k"][0, o].rearrange("s h d -> s (h d)"), z[:, 0, SQ_DIM:SQ_DIM + SKV_DIM]).then_inc(s_out, 16)
            sp.dma_start(io["new_swa_v"][0, o].rearrange("s h d -> s (h d)"), z[:, 0, SQ_DIM + SKV_DIM:ODD_IN]).then_inc(s_out, 16)
            sp.wait_ge(s_l, 48)
            sp.wait_ge(s_out, 32)

        @blk.gpsimd
        def _(pool):
            st = Steps(pool, s_z)
            for v in (k.kpad, *k.key_zeros):
                st.then(nc.gpsimd.memset(v, 0.0))

        @blk.vector
        def _(dve):
            st = Steps(dve, s_d)
            for t in (1, 2):
                for at, hh in ((0, SH), (SQ_DIM, SKV)):
                    x = z[:, t, at:at + hh * SD].rearrange("p (h a b f) -> p h a b f", h=hh, a=2, b=2)
                    rope(nc, st, k, C_ROPE_O, t - 1, x, tmp, hh, SD // 4)


class NormBuffers:

    def __init__(self, k, which):
        self.T = k.z[:, 0:6 * D].rearrange("p (c j n) -> p c j n", c=2, j=3)
        self.tmp = k.z[:, 6 * D:7 * D]
        o = 7 * D
        self.stats = k.z[:, o:o + 12 * TILES].rearrange("p (t j n) -> p t j n", t=TILES, j=2)
        self.mv = k.z[:, o + 48:o + 48 + 2 * TILES].rearrange("p (t n) -> p t n", t=TILES)
        self.half = k.z[:, o + 60:o + 61]
        o = (7168, 8192)[which - 1]
        self.n = k.s[:, o:o + TILES * D].rearrange("p (t n) -> p t n", t=TILES)
        self.gb = k.cat[:, 0:2, :] if which == 1 else k.s[:, 12288:12288 + 2 * D].rearrange("p (j n) -> p j n", j=2)


def load_norm_tables(k, eng, layer, which, s_gate, s_tab):
    M = NormBuffers(k, which)
    for cnd in range(2):
        table_load(k, eng, s_gate, M.T[:, cnd, 0, :], layer, cnd, (2, 5)[which - 1])
    for j, n in enumerate("gb"):
        eng.dma_start(M.gb[:, j, :], k.io[f"ln{which}_{n}"][layer:layer + 1, :].to_broadcast([P, D])).then_inc(s_tab, 16)
    if which == 1 or layer + 1 < DEPTH:
        for cnd in range(2):
            for j in range(2):
                at = (layer, 3 + j) if which == 1 else (layer + 1, j)
                table_load(k, eng, s_tab, M.T[:, cnd, 1 + j, :], at[0], cnd, at[1])


def fold_steps(M, eng, c, bs):
    tt = eng.tensor_tensor
    g, b = M.gb[:, 0, :], M.gb[:, 1, :]
    shift, scale = M.T[:, c, 1, :], M.T[:, c, 2, :]
    return [lambda: tt(shift, shift, b, ALU.add), lambda: tt(bs, b, scale, ALU.mult), lambda: tt(shift, shift, bs, ALU.add),
            lambda: tt(scale, scale, g, ALU.mult), lambda: tt(scale, scale, g, ALU.add)]


def dve_stats(k, M, st, t, halves):
    for j in halves:
        st.then(k.nc.vector.bn_stats(M.stats[:, t, j, :], k.x[:, t, j * 512:(j + 1) * 512]))


def dve_variance(k, M, st, t, s_v):
    st.then(k.nc.vector.bn_aggr(M.mv[:, t, :], M.stats[:, t, :, :]))
    k.nc.vector.tensor_scalar(M.mv[:, t, 1:2], M.mv[:, t, 1:2], LN_EPS, None, ALU.add).then_inc(s_v, 1)


def pool_rstd(k, M, pool, t, s_v, s_p):
    pool.wait_ge(s_v, t + 1)
    k.nc.gpsimd.tensor_tensor(M.mv[:, t, 1:2], M.mv[:, t, 1:2], M.half, ALU.pow).then_inc(s_p, 1)


def dve_norm(k, M, dve, st, t, s_p, s_n, s_h, permuted):
    x, n, c = k.x[:, t, :], M.n[:, t, :], min(t, 1)
    dve.wait_ge(s_p, t + 1)
    k.nc.vector.tensor_scalar(n, x, M.mv[:, t, 0:1], M.mv[:, t, 1:2], ALU.subtract, ALU.mult).then_inc(s_n, 1)
    dve.wait_ge(s_n, t + 1)
    G, B, h = M.T[:, c, 2, :], M.T[:, c, 1, :], k.hP[:, t, :]
    if permuted:
        n, G, B = (v.rearrange("p (q k) -> p k q", k=KT) for v in (n, G, B))
        h = h.rearrange("p (k q) -> p k q", k=KT)
    st.then(k.nc.vector.tensor_tensor(h, n, G, ALU.mult))
    k.nc.vector.tensor_tensor(h, h, B, ALU.add).then_inc(s_h, 1)


def pool_affine(k, M, pool, t, s_n, s_g2):
    pool.wait_ge(s_n, t + 1)
    k.nc.gpsimd.tensor_tensor(k.x[:, t, :], M.n[:, t, :], M.gb[:, 0, :], ALU.mult).then_inc(s_g2, 1)
    pool.wait_ge(s_g2, t + 1)
    k.nc.gpsimd.tensor_tensor(k.x[:, t, :], k.x[:, t, :], M.gb[:, 1, :], ALU.add)


def pe_turn_tile(k, pe, t, banks, s_h, s_tr):
    pe.wait_ge(s_h, t + 1)
    for g in range(2):
        for j in range(4):
            kk = 4 * g + j
            m = k.nc.tensor.transpose(k.ps[banks[g]][:, j * P:(j + 1) * P], k.hP[:, t, kk * P:(kk + 1) * P], k.ident)
        m.then_inc(s_tr, 1)


def copy_turned(k, act, t, banks, s_tr):
    for g in range(2):
        act.wait_ge(s_tr, 2 * t + g + 1)
        k.nc.scalar.copy(k.hT[:, 4 * g:4 * g + 4, t * P:(t + 1) * P], k.ps[banks[g]][:].rearrange("p (j n) -> p j n", j=4))


def stage_project_norm(k, w, layer):
    nc = k.nc
    M = NormBuffers(k, 1)
    NCH = D // 512
    w_slot = (early_slot(k), ring_slot(k, 1))
    turn_banks = ((6, 7), (0, 1), (2, 3))
    with Stage(nc) as ctx:
        s_gate, s_tab, s_fold, s_mm, s_d, s_ev, s_v, s_p, s_n, s_h, s_g2, s_tr, s_out = sems(
            nc, ctx, "gate_loaded tables_loaded tables_folded product_ready dve_steps product_taken var_ready rstd_ready "
                     "normed h_ready x_scaled turned rows_stored")
        blk = ctx.enter_context(nc.Block())

        @blk.sync
        def _(sp):
            k.arrived(sp, 1)
            load_norm_tables(k, sp, layer, 1, s_gate, s_tab)
            load_router(k, layer)(sp)
            for t in range(TILES):
                sp.wait_ge(s_h, t + 1)
                sp.dma_start(k.h_d[t * P:(t + 1) * P, :], k.hP[:, t, :]).then_inc(s_out, 16)
            sp.wait_ge(s_out, 16 * TILES)

        @blk.gpsimd
        def _(pool):
            pool.wait_ge(s_tab, 16 * 6)
            for i, step in enumerate(fold_steps(M, nc.gpsimd, 1, M.n[:, TILES - 1, :])):
                if i:
                    pool.wait_ge(s_fold, i)
                step().then_inc(s_fold, 1)
            pool_rstd(k, M, pool, 0, s_v, s_p)
            for t in range(TILES):
                pool_affine(k, M, pool, t, s_n, s_g2)
                if t + 1 < TILES:
                    pool_rstd(k, M, pool, t + 1, s_v, s_p)

        @blk.tensor
        def _(pe):
            for c in range(NCH):
                k.arrived(pe, c)
                for t in range(TILES):
                    for kk in range(KT):
                        m = nc.tensor.matmul(k.ps[TILES * c + t][:], k.hT[:, kk, t * P:(t + 1) * P], w_slot[c][:, kk, :],
                                             start=(kk == 0), stop=(kk == KT - 1))
                    m.then_inc(s_mm, 1)
            for t in range(TILES):
                if t:
                    pe.wait_ge(s_ev, TILES * (NCH - 1))
                pe_turn_tile(k, pe, t, turn_banks[t], s_h, s_tr)

        @blk.scalar
        def _(act):
            for t in range(TILES):
                act.wait_ge(s_mm, TILES * (NCH - 1) + t + 1)
                copy_turned(k, act, t, turn_banks[t], s_tr)

        @blk.vector
        def _(dve):
            st = Steps(dve, s_d)
            st.then(nc.vector.memset(M.half, -0.5))
            dve.wait_ge(s_gate, 32)
            for c in range(NCH):
                for t in range(TILES):
                    cols = slice(c * 512, (c + 1) * 512)
                    x, y = k.x[:, t, cols], M.tmp[:, cols]
                    dve.wait_ge(s_mm, TILES * c + t + 1)
                    nc.vector.tensor_tensor(y, k.ps[TILES * c + t][:], M.T[:, min(t, 1), 0, cols], ALU.mult).then_inc(s_ev, 1)
                    dve.wait_ge(s_ev, TILES * c + t + 1)
                    st.then(nc.vector.scalar_tensor_tensor(x, x, ALPHA, y, ALU.mult, ALU.add))
                    dve_stats(k, M, st, t, (c,))
                    if c == NCH - 1:
                        dve_variance(k, M, st, t, s_v)
                        if t == 1:
                            dve.wait_ge(s_fold, 5)
                        dve_norm(k, M, dve, st, t, s_p, s_n, s_h, True)
                    if c == NCH - 2 and t == 1:
                        dve.wait_ge(s_tab, 16 * 6)
                        for step in fold_steps(M, nc.vector, 0, M.tmp):
                            st.then(step())


def bc(ap, shape):
    return ap.to_broadcast(shape)


MOE_BIAS = 6656


def load_router(k, layer):
    def ahead(sp):
        k.load_ahead(sp, 4, k.s[:, 0:KT * NE], k.io["moe_router"][layer].rearrange("(p k) n -> p (k n)", k=KT))
        k.load_ahead(sp, 4, k.s[:, MOE_BIAS:MOE_BIAS + NE], k.io["moe_router_bias"][layer:layer + 1, :].to_broadcast([P, NE]))
    return ahead


def stage_route(k, layer):
    nc, io = k.nc, k.io
    o = 0

    def cut(n):
        nonlocal o
        o += n
        return k.z[:, o - n:o]

    E3 = TILES * NE
    scores, sel, mask, W, V, junk, ex = (cut(E3) for _ in range(7))
    g8 = cut(TILES * NG * 8)
    grp, rank, pen = (cut(TILES * NG) for _ in range(3))
    gt, eq = (cut(TILES * NG * NG) for _ in range(2))
    t8 = cut(8 * TILES)
    v8 = cut(8 * TILES)
    wsum = cut(4)
    CB = cut(P)
    bias = k.s[:, MOE_BIAS:MOE_BIAS + NE]
    keys = cut(2 * NE)
    okey = cut(OVER_KEYS + 8)
    yf = cut(NE)
    onesb = cut(4)[:, 0:2].bitcast(BF16)[:, 0:1]
    le = cut(2 * TILES * 512).bitcast(BF16).rearrange("p (b t e n) -> p b t e n", b=2, t=TILES, e=8)
    assert o <= TILES * EVEN_IN, o
    rw = k.s[:, 0:KT * NE].rearrange("p (k n) -> p k n", k=KT)
    sg = k.s[:, 512:512 + 4096]
    sd = k.s[:, 4608:4608 + 2048]
    sgv = sg.rearrange("p (j k n) -> p k j n", j=2, k=KT)
    sdv = sd.rearrange("p (j n) -> p j n", j=2)
    sex = k.s[:, 7000:7000 + FD * TILES].rearrange("p (t n) -> p t n", t=TILES)
    sh = k.s[:, 8000:8000 + FD * TILES].rearrange("p (t j n) -> p t j n", t=TILES, j=2)
    shT = k.s[:, 9000:9000 + FD * TILES].rearrange("p (t n) -> p t n", t=TILES)

    def tile3(v):
        return v.rearrange("p (t e) -> p t e", t=TILES)

    logits = k.ps[3][:, 0:E3]
    turned = k.ps[3][:, 256:512]
    incl_ps, total = k.ps[4][:, 0:E3], k.ps[4][:, E3:E3 + NE]
    totalT, base_ps, token = k.ps[5][0:NE, 0:P], k.ps[5][:, P:P + NE], k.ps[6][:, 0:NE]
    out_banks = ((7, 0), (1, 7), (2, 0))

    def not_beyond(g, t):
        return nc.vector.tensor_tensor(le[:, g % 2, t], bc(k.incl[:, t, 8 * g:8 * g + 8].rearrange("p (e o) -> p e o", o=1), [P, 8, P]),
                                 bc(k.c(C_IOTA, P).rearrange("p (o n) -> p o n", o=1), [P, 8, P]), ALU.is_le)

    with Stage(nc) as ctx:
        s_mm, s_e, s_d, s_m, s_cnt, s_cb, s_base, s_le, s_ix = sems(
            nc, ctx, "logits_ready exp_ready dve_steps mask_ready counts_ready counts_copied bases_ready le_ready "
                     "idx_ready")
        s_gul, s_dl, s_gu, s_se, s_h, s_ht, s_hc, s_dn, s_y = sems(
            nc, ctx, "shared_gate_up_loaded shared_down_loaded gate_up_ready shared_exp h_ready h_turned hT_ready down_ready y_copied")
        blk = ctx.enter_context(nc.Block())

        @blk.sync
        def _(sp):
            sp.dma_start(sg[:, 0:2048], io["shared_w_gate"][layer].rearrange("(p k) n -> p (k n)", k=KT)).then_inc(s_gul, 16)
            sp.dma_start(sg[:, 2048:4096], io["shared_w_up"][layer].rearrange("(p k) n -> p (k n)", k=KT)).then_inc(s_gul, 16)
            sp.dma_start(sd, io["shared_w_down"][layer].rearrange("(p j) n -> p (j n)", j=2)).then_inc(s_dl, 16)
            for e in range(2):
                load_expert(k, sp, layer, e, e, k.s_ahead[1 + e], k.s_ahead[1 + e])
                k.ahead[1 + e] += 48

        @blk.gpsimd
        def _(pool):
            nc.gpsimd.memset(k.hP[:], 0.0)

        @blk.tensor
        def _(pe):
            tri = k.c(C_TRI, P)
            m3 = tile3(mask)

            def gate_up(t, lo=0, hi=KT):
                for kk in range(lo, hi):
                    m = nc.tensor.matmul(k.ps[t][:], k.hT[:, kk, t * P:(t + 1) * P], sgv[:, kk], start=(kk == 0), stop=(kk == KT - 1))
                if hi == KT:
                    m.then_inc(s_gu, 1)

            def down(t):
                pe.wait_ge(s_h, t + 1)
                if t:
                    pe.wait_ge(s_hc, t)
                for j in range(2):
                    m = nc.tensor.transpose(turned[:, j * P:(j + 1) * P], sh[:, t, j, :], k.ident)
                m.then_inc(s_ht, 1)
                pe.wait_ge(s_hc, t + 1)
                if t:
                    pe.wait_ge(s_y, t)
                for c in range(2):
                    for j in range(2):
                        m = nc.tensor.matmul(k.ps[out_banks[t][c]][:], shT[:, t, j * P:(j + 1) * P], sdv[:, j, c * 512:(c + 1) * 512],
                                             start=(j == 0), stop=(j == 1))
                    m.then_inc(s_dn, 1)

            def count_le(g):
                pe.wait_ge(s_le, g + 1)
                for e in range(8):
                    for t in range(TILES):
                        m = nc.tensor.matmul(token[:, 8 * g + e:8 * g + e + 1], le[:, g % 2, t, e, :], onesb, start=(t == 0), stop=(t == TILES - 1))
                m.then_inc(s_ix, 1)

            k.arrived(pe, 4)
            for t in range(TILES):
                for kk in range(KT):
                    m = nc.tensor.matmul(tile3(logits)[:, t, :], k.hT[:, kk, t * P:(t + 1) * P], rw[:, kk, :], start=(kk == 0), stop=(kk == KT - 1))
            m.then_inc(s_mm, 1)
            pe.wait_ge(s_gul, 32)
            gate_up(0)
            gate_up(1, hi=KT // 2)
            pe.wait_ge(s_m, 1)
            for t in range(TILES):
                for u in range(t + 1):
                    nc.tensor.matmul(tile3(incl_ps)[:, t, :], tri if u == t else k.ones[:], m3[:, u, :], start=(u == 0), stop=(u == t))
            for t in range(TILES):
                nc.tensor.matmul(total, k.ones[:], m3[:, t, :], start=(t == 0), stop=(t == TILES - 1))
            for t in range(TILES):
                m = nc.tensor.matmul(totalT, m3[:, t, :], k.ones[:], start=(t == 0), stop=(t == TILES - 1))
            m.then_inc(s_cnt, 1)
            gate_up(1, lo=KT // 2)
            pe.wait_ge(s_cb, 1)
            nc.tensor.matmul(base_ps, CB[0:NE, :], tri[0:NE, 0:NE], start=True, stop=True).then_inc(s_base, 1)
            gate_up(2)
            pe.wait_ge(s_dl, 16)
            down(0)
            count_le(0)
            count_le(1)
            down(1)
            count_le(2)
            count_le(3)
            down(2)
            for g in range(4, NE // 8):
                count_le(g)

        @blk.scalar
        def _(act):
            def shared_exp(t):
                act.wait_ge(s_gu, t + 1)
                nc.scalar.activation(sex[:, t, :], k.ps[t][:, 0:FD], ACT.Exp, scale=-1.0).then_inc(s_se, 1)

            act.wait_ge(s_mm, 1)
            nc.scalar.activation(ex, logits, ACT.Exp, scale=-1.0).then_inc(s_e, 1)
            shared_exp(0)
            act.wait_ge(s_cnt, 1)
            nc.scalar.copy(CB[0:NE, :], totalT).then_inc(s_cb, 1)
            shared_exp(1)
            shared_exp(2)
            for t in range(TILES):
                act.wait_ge(s_ht, t + 1)
                nc.scalar.copy(shT[:, t, :], turned).then_inc(s_hc, 1)
                for c in range(2):
                    act.wait_ge(s_dn, 2 * t + c + 1)
                    nc.scalar.copy(k.cat[:, t, c * 512:(c + 1) * 512], k.ps[out_banks[t][c]][:]).then_inc(s_y, 1)

        @blk.vector
        def _(dve):
            st = Steps(dve, s_d)
            st.mark(nc.vector.memset(onesb, 1.0))
            dve.wait_ge(s_e, 1)
            st.then(nc.vector.tensor_scalar(ex, ex, 1.0, None, ALU.add))
            st.then(nc.vector.reciprocal(scores, ex))
            k.arrived(dve, 4)
            st.then(nc.vector.tensor_tensor(tile3(sel), tile3(scores), bc(bias.rearrange("p (o e) -> p o e", o=1), [P, TILES, NE]), ALU.add))
            for i in range(TILES * NG):
                st.mark(nc.vector.max(g8[:, 8 * i:8 * i + 8], sel[:, 8 * i:8 * i + 8]))
            st.wait()
            g8v = g8.rearrange("p (g n) -> p g n", n=8)
            st.then(nc.vector.tensor_tensor(grp, g8v[:, :, 0], g8v[:, :, 1], ALU.add))
            S4 = [P, TILES, NG, NG]
            gj = bc(grp.rearrange("p (t o j) -> p t o j", t=TILES, o=1), S4)
            gg = bc(grp.rearrange("p (t g o) -> p t g o", t=TILES, o=1), S4)
            v4 = lambda v: v.rearrange("p (t g j) -> p t g j", t=TILES, g=NG)
            st.mark(nc.vector.tensor_tensor(v4(gt), gj, gg, ALU.is_gt))
            st.then(nc.vector.tensor_tensor(v4(eq), gj, gg, ALU.is_equal))
            st.then(nc.vector.tensor_tensor(tile3(eq), tile3(eq), bc(k.c(C_LT8, 64).rearrange("p (o n) -> p o n", o=1), [P, TILES, 64]), ALU.mult))
            st.then(nc.vector.tensor_tensor(gt, gt, eq, ALU.add))
            st.then(nc.vector.tensor_reduce(rank, gt.rearrange("p (g j) -> p g j", j=NG), AX.X, ALU.add))
            st.then(nc.vector.tensor_scalar(pen, rank, TOPG - 0.5, -NEG, ALU.is_lt, ALU.mult))
            st.then(nc.vector.tensor_scalar(pen, pen, NEG, None, ALU.add))
            st.then(nc.vector.tensor_tensor(sel.rearrange("p (g n) -> p g n", n=8), sel.rearrange("p (g n) -> p g n", n=8),
                                            bc(pen.rearrange("p (g o) -> p g o", o=1), [P, TILES * NG, 8]), ALU.add))
            for t in range(TILES):
                st.mark(nc.vector.max(t8[:, 8 * t:8 * t + 8], tile3(sel)[:, t, :]))
            st.wait()
            for t in range(TILES):
                st.mark(nc.vector.match_replace(tile3(junk)[:, t, :], t8[:, 8 * t:8 * t + 8], tile3(sel)[:, t, :], 1e38))
            st.wait()
            nc.vector.tensor_scalar(mask, junk, 5e37, None, ALU.is_ge).then_inc(s_m, 1)
            dve.wait_ge(s_m, 1)
            st.then(nc.vector.tensor_tensor(W, scores, mask, ALU.mult))
            st.then(nc.vector.tensor_reduce(wsum[:, 0:TILES], tile3(W), AX.X, ALU.add))
            st.then(nc.vector.reciprocal(wsum[:, 0:TILES], wsum[:, 0:TILES]))
            for t in range(TILES):
                st.mark(nc.vector.tensor_scalar(tile3(W)[:, t, :], tile3(W)[:, t, :], wsum[:, t:t + 1], ROUTED_SCALE, ALU.mult, ALU.mult))

            def shared_hidden(t):
                dve.wait_ge(s_se, t + 1)
                st.then(nc.vector.tensor_scalar(sex[:, t, :], sex[:, t, :], 1.0, None, ALU.add))
                st.then(nc.vector.reciprocal(sex[:, t, :], sex[:, t, :]))
                st.then(nc.vector.tensor_tensor(sex[:, t, :], sex[:, t, :], k.ps[t][:, 0:FD], ALU.mult))
                nc.vector.tensor_tensor(sh[:, t].rearrange("p j q -> p q j"), sex[:, t, :].rearrange("p (q j) -> p q j", j=2),
                                        k.ps[t][:, FD:2 * FD].rearrange("p (q j) -> p q j", j=2), ALU.mult).then_inc(s_h, 1)

            def tokens_by_count(g):
                if g >= 2:
                    dve.wait_ge(s_ix, g - 1)
                for t in range(TILES):
                    m = not_beyond(g, t)
                m.then_inc(s_le, 1)

            shared_hidden(0)
            dve.wait_ge(s_cnt, 1)
            st.then(nc.vector.tensor_tensor(k.incl[:], tile3(incl_ps), tile3(mask), ALU.add))
            tokens_by_count(0)
            tokens_by_count(1)
            shared_hidden(1)
            tokens_by_count(2)
            tokens_by_count(3)
            shared_hidden(2)
            dve.wait_ge(s_base, 1)
            base, end = k.bases[:, 0, :], k.bases[:, 1, :]
            st.then(nc.vector.tensor_copy(base, base_ps))
            st.then(nc.vector.tensor_tensor(end, base, total, ALU.add))
            st.then(nc.vector.tensor_tensor(tile3(V), k.incl[:], bc(base.rearrange("p (o e) -> p o e", o=1), [P, TILES, NE]), ALU.add))
            st.then(nc.vector.tensor_tensor(V, V, mask, ALU.mult))
            for t in range(TILES):
                st.mark(nc.vector.max(v8[:, 8 * t:8 * t + 8], tile3(V)[:, t, :]))
            st.wait()
            st.mark(nc.vector.tensor_scalar(k.slot_u[:].rearrange("p t n -> p (t n)"), v8, -1.0, None, ALU.add))
            for t in range(TILES):
                for j in range(TOPK):
                    st.then(nc.vector.scalar_tensor_tensor(tile3(junk)[:, t, :], tile3(V)[:, t, :], v8[:, 8 * t + j:8 * t + j + 1], tile3(W)[:, t, :],
                                                           ALU.is_equal, ALU.mult, accum_out=k.w8[:, t, j:j + 1]))
            col = k.const[:, C_COL + 1:C_COL + 2]
            st.then(nc.vector.tensor_scalar(yf, base, col, None, ALU.add))
            st.then(nc.vector.tensor_tensor(junk[:, 0:NE], yf, end, ALU.is_ge))
            st.then(nc.vector.scalar_tensor_tensor(yf, junk[:, 0:NE], FAR, yf, ALU.mult, ALU.add))
            st.mark(nc.vector.tensor_copy(k.y_idx[:], yf))
            for b in range(OVER_BLOCKS):
                st.then(nc.vector.tensor_scalar(keys[:, b * NE:(b + 1) * NE], total, P * (b + 1.0), None, ALU.is_gt))
            st.then(nc.vector.tensor_tensor(keys, keys, k.c(C_KEY, 2 * NE), ALU.mult))
            for i in range(OVER_KEYS // 8):
                st.then(nc.vector.max(okey[:, 8 * i:8 * i + 8], keys))
                st.then(nc.vector.match_replace(keys, okey[:, 8 * i:8 * i + 8], keys, -1.0))
            st.then(nc.vector.tensor_scalar(junk[:, 0:OVER_KEYS], okey[:, 0:OVER_KEYS], 0.5, None, ALU.is_gt))
            st.then(nc.vector.tensor_reduce(okey[:, OVER_KEYS:OVER_KEYS + 1], junk[:, 0:OVER_KEYS], AX.X, ALU.add))
            st.then(nc.vector.tensor_scalar(okey[:, 0:OVER_KEYS], okey[:, 0:OVER_KEYS], -1.0, 0.0, ALU.add, ALU.max))
            st.mark(nc.vector.tensor_copy(k.over[:, 0:OVER_KEYS + 1], okey[:, 0:OVER_KEYS + 1]))
            for g in range(4, NE // 8):
                tokens_by_count(g)
            dve.wait_ge(s_ix, NE // 8)
            st.mark(nc.vector.tensor_copy(k.tok_idx[:], token))


def expert_views(k, b):
    w = k.ring[:, b * 6144:(b + 1) * 6144]
    return (w[:, 0:2048], w[:, 2048:4096], w[:, 4096:6144],
            w[:, 0:4096].rearrange("p (j k n) -> p k j n", j=2, k=KT), w[:, 4096:6144].rearrange("p (j n) -> p j n", j=2))


def load_gate_up(k, eng, layer, e, b, sem):
    for name, v in zip(("moe_w_gate", "moe_w_up"), expert_views(k, b)):
        src = k.io[name][layer, bass.ds(e, 1)].rearrange("o (p k) n -> p (o k n)", k=KT)
        eng.dma_start(v, src).then_inc(sem, 16)


def load_down(k, eng, layer, e, b, sem):
    src = k.io["moe_w_down"][layer, bass.ds(e, 1)].rearrange("o (p j) n -> p (o j n)", j=2)
    eng.dma_start(expert_views(k, b)[2], src).then_inc(sem, 16)


def load_expert(k, eng, layer, e, b, sem_gu, sem_d):
    load_gate_up(k, eng, layer, e, b, sem_gu)
    load_down(k, eng, layer, e, b, sem_d)


class MoeBuffers:

    def __init__(self, k):
        self.xg = k.hP[:, 0:2, :]
        f = k.s
        self.xT = f[:, 0:1024]
        self.ex = [f[:, 1024 + i * FD:1024 + (i + 1) * FD] for i in range(2)]
        self.h = [f[:, 1536 + i * FD:1536 + (i + 1) * FD] for i in range(2)]
        self.hT = f[:, 2048:2048 + FD]
        self.y = [f[:, 2560 + i * D:2560 + (i + 1) * D] for i in range(2)]
        self.gi = f[:, 4700:4701].bitcast(U32)
        self.si = f[:, 4710:4711].bitcast(U32)


def pe_turn_rows(k, B, b):
    for kk in range(KT):
        m = k.nc.tensor.transpose(k.ps[kk // 4][:, (kk % 4) * P:(kk % 4 + 1) * P], B.xg[:, b, kk * P:(kk + 1) * P], k.ident)
    return m


def pe_gate_up(k, B, b, bank):
    for kk in range(KT):
        m = k.nc.tensor.matmul(k.ps[bank][:], B.xT[:, kk * P:(kk + 1) * P], expert_views(k, b)[3][:, kk], start=(kk == 0), stop=(kk == KT - 1))
    return m


def pe_turn_h(k, B, b):
    for j in range(2):
        m = k.nc.tensor.transpose(k.ps[4][:, j * P:(j + 1) * P], B.h[b][:, j * P:(j + 1) * P], k.ident)
    return m


def pe_down(k, B, b):
    for c in range(2):
        for j in range(2):
            m = k.nc.tensor.matmul(k.ps[5 + c][:], B.hT[:, j * P:(j + 1) * P], expert_views(k, b)[4][:, j, c * 512:(c + 1) * 512],
                                   start=(j == 0), stop=(j == 1))
    return m


def dve_hidden(k, B, b, bank, eng, sem, n):
    nc = k.nc
    g, u = k.ps[bank][:, 0:FD], k.ps[bank][:, FD:2 * FD]
    nc.vector.tensor_scalar(B.ex[b], B.ex[b], 1.0, None, ALU.add).then_inc(sem, 1)
    eng.wait_ge(sem, n + 1)
    nc.vector.reciprocal(B.ex[b], B.ex[b]).then_inc(sem, 1)
    eng.wait_ge(sem, n + 2)
    nc.vector.tensor_tensor(B.ex[b], B.ex[b], g, ALU.mult).then_inc(sem, 1)
    eng.wait_ge(sem, n + 3)
    return nc.vector.tensor_tensor(B.h[b].rearrange("p (j q) -> p q j", j=2), B.ex[b].rearrange("p (q j) -> p q j", j=2),
                                   u.rearrange("p (q j) -> p q j", j=2), ALU.mult)


def gather(k, out, table, last, idx):
    return k.nc.gpsimd.indirect_dma_start(out=out, out_offset=None, in_=table, in_offset=bass.IndirectOffsetOnAxis(ap=idx, axis=0),
                                          bounds_check=last, oob_is_err=False)


def scatter(k, table, last, idx, in_):
    return k.nc.gpsimd.indirect_dma_start(out=table, out_offset=bass.IndirectOffsetOnAxis(ap=idx, axis=0), in_=in_, in_offset=None,
                                          bounds_check=last, oob_is_err=False)


def bounds(pool):
    regs = []
    for v in (TOK - 1, ASSIGNED - 1):
        r = pool.alloc_register()
        pool.reg_mov(r, v)
        regs.append(r)
    return regs


def for_experts(eng, step, last):
    for e in range(3):
        step(e, e // 2, e % 2)
    pairs = (last - 2) // 2
    with eng.Fori(0, pairs) as i:
        step(2 * i + 3, i + 1, 1)
        step(2 * i + 4, i + 2, 0)
    for e in range(3 + 2 * pairs, last + 1):
        step(e, e // 2, e % 2)


def ge(eng, sem, v):
    if not isinstance(v, int) or v > 0:
        eng.wait_ge(sem, v)


FOLD_FROM = 8


SPLIT = 2


def stage_experts(k, layer):
    nc = k.nc
    B = MoeBuffers(k)
    last_layer = layer == DEPTH - 1
    with Stage(nc) as ctx:
        w_hi, w_lo = (ctx.enter_context(nc.sbuf_tensor(f"{n}_{layer}", [P, SPLIT, 2, FD], F32R)) for n in ("expert_w_hi", "expert_w_lo"))
        x_hi, x_lo = (ctx.enter_context(nc.sbuf_tensor(f"{n}_{layer}", [P, SPLIT * P], F32R)) for n in ("expert_x_hi", "expert_x_lo"))
        s_wh, s_wl, s_xh = sems(nc, ctx, "weights_rounded weights_rest x_rounded")
        s_xt, s_xa, s_xv, s_gu, s_e, s_hs, s_h, s_ht, s_hc, s_d, s_ya, s_yv = sems(
            nc, ctx, "x_turned xT_copied_act xT_copied_dve gate_up_ready exp_ready h_steps h_ready "
                     "h_turned hT_ready down_ready y_copied_act y_copied_dve")
        s_g, s_sc = k.pool_sems[layer][0:2], k.pool_sems[layer][2]
        s_fold = sems(nc, ctx, "table_folded")[0]
        s_wg = sems(nc, ctx, "gate_up0_loaded gate_up1_loaded")
        s_wd = sems(nc, ctx, "down0_loaded down1_loaded")
        blk = ctx.enter_context(nc.Block())

        @blk.sync
        def _(sp):
            def step(e, half, b):
                sp.wait_ge(s_gu, e + 1)
                load_gate_up(k, sp, layer, e + 2, b, s_wg[b])
                if not isinstance(e, int) or e >= 1:
                    sp.wait_ge(s_d, e)
                    load_down(k, sp, layer, e + 1, 1 - b, s_wd[1 - b])
            load_norm_tables(k, sp, layer, 2, k.s_ahead[3], k.s_ahead[3])
            k.ahead[3] += 16 * (4 if last_layer else 8)
            for_experts(sp, step, NE - 3)
            sp.wait_ge(s_d, NE - 2)
            load_down(k, sp, layer, NE - 1, 1, s_wd[1])

        @blk.gpsimd
        def _(pool):
            last_tok, last_row = bounds(pool)

            def get(e, b):
                ge(pool, s_xt, e - 1)
                gather(k, B.xg[:, b, :], k.h_d, last_tok, k.tok_idx[:, e:e + 1]).then_inc(s_g[b], 16)

            def put(e, b):
                pool.wait_ge(s_ya, e + 1)
                pool.wait_ge(s_yv, e + 1)
                ge(pool, s_sc, 16 * e)
                scatter(k, k.y_d, last_row, k.y_idx[:, e:e + 1], B.y[b]).then_inc(s_sc, 16)

            get(0, 0)
            get(1, 1)
            M = NormBuffers(k, 2)
            folds = [] if last_layer else [f for c in range(2) for f in fold_steps(M, nc.gpsimd, c, M.tmp)]
            for e in range(NE - 2):
                get(e + 2, e % 2)
                if e >= 1:
                    put(e - 1, (e - 1) % 2)
                if e >= FOLD_FROM and (e - FOLD_FROM) % 3 == 0 and (e - FOLD_FROM) // 3 < len(folds):
                    i = (e - FOLD_FROM) // 3
                    if i == 0:
                        k.arrived(pool, 3)
                    else:
                        pool.wait_ge(s_fold, i)
                    folds[i]().then_inc(s_fold, 1)
            for e in range(NE - 3, NE):
                put(e, e % 2)
            pool.wait_ge(s_sc, 16 * NE)

        @blk.tensor
        def _(pe):
            def turn_rows(e, half, b):
                pe.wait_ge(s_g[b], 16 * (half + 1))
                ge(pe, s_xa, e)
                ge(pe, s_xv, e)
                pe_turn_rows(k, B, b).then_inc(s_xt, 1)

            def gate_up(e, half, b):
                pe.wait_ge(s_xa, e + 1)
                pe.wait_ge(s_xv, e + 1)
                if isinstance(e, int) and e < 2:
                    k.arrived(pe, 1 + e)
                else:
                    pe.wait_ge(s_wg[b], 32 * half)
                ge(pe, s_h, e - 1)
                out, w = k.ps[2 + b][:], expert_views(k, b)[3]
                for kk in range(SPLIT, KT):
                    nc.tensor.matmul(out, B.xT[:, kk * P:(kk + 1) * P], w[:, kk], start=(kk == SPLIT), stop=False)
                pe.wait_ge(s_wh, e + 1)
                pe.wait_ge(s_wl, e + 1)
                for kk in range(SPLIT):
                    rows = slice(kk * P, (kk + 1) * P)
                    nc.tensor.matmul(out, x_hi[:, rows], w_hi[:, kk], start=False, stop=False)
                    nc.tensor.matmul(out, x_lo[:, rows], w_hi[:, kk], start=False, stop=False)
                    m = nc.tensor.matmul(out, x_hi[:, rows], w_lo[:, kk], start=False, stop=(kk == SPLIT - 1))
                m.then_inc(s_gu, 1)

            def turn_h(e, half, b):
                pe.wait_ge(s_h, e + 1)
                ge(pe, s_hc, e)
                pe_turn_h(k, B, b).then_inc(s_ht, 1)

            def down(e, half, b):
                pe.wait_ge(s_hc, e + 1)
                if isinstance(e, int) and e < 2:
                    k.arrived(pe, 1 + e)
                else:
                    pe.wait_ge(s_wd[b], 16 * half)
                ge(pe, s_ya, e)
                ge(pe, s_yv, e)
                pe_down(k, B, b).then_inc(s_d, 1)

            def step(e, half, b):
                gate_up(e, half, b)
                if not isinstance(e, int) or e >= 1:
                    turn_h(e - 1, half - 1 + b, 1 - b)
                turn_rows(e + 1, half + b, 1 - b)
                if not isinstance(e, int) or e >= 1:
                    down(e - 1, half - 1 + b, 1 - b)
            turn_rows(0, 0, 0)
            for_experts(pe, step, NE - 2)
            gate_up(NE - 1, NE // 2 - 1, 1)
            for e, b in ((NE - 2, 0), (NE - 1, 1)):
                turn_h(e, NE // 2 - 1, b)
                down(e, NE // 2 - 1, b)

        @blk.scalar
        def _(act):
            def copy_x(e):
                act.wait_ge(s_xt, e + 1)
                ge(act, s_gu, e)
                nc.scalar.copy(x_hi[:], k.ps[0][:, 0:SPLIT * P]).then_inc(s_xh, 1)
                nc.scalar.copy(B.xT[:, SPLIT * P:512], k.ps[0][:, SPLIT * P:512]).then_inc(s_xa, 1)

            def split(e, half, b):
                if isinstance(e, int) and e < 2:
                    k.arrived(act, 1 + e)
                else:
                    act.wait_ge(s_wg[b], 32 * half)
                ge(act, s_gu, e)
                nc.scalar.copy(w_hi[:], expert_views(k, b)[3][:, 0:SPLIT]).then_inc(s_wh, 1)

            def hidden(e, b):
                act.wait_ge(s_gu, e + 1)
                ge(act, s_h, e - 1)
                nc.scalar.activation(B.ex[b], k.ps[2 + b][:, 0:FD], ACT.Exp, scale=-1.0).then_inc(s_e, 1)

            def copy_h(e):
                act.wait_ge(s_ht, e + 1)
                nc.scalar.copy(B.hT, k.ps[4][:, 0:FD]).then_inc(s_hc, 1)

            def finish(e, b):
                act.wait_ge(s_d, e + 1)
                ge(act, s_sc, 16 * (e - 1))
                nc.scalar.copy(B.y[b][:, 0:512], k.ps[5][:]).then_inc(s_ya, 1)

            def step(e, half, b):
                hidden(e, b)
                if not isinstance(e, int) or e >= 1:
                    copy_h(e - 1)
                copy_x(e + 1)
                if not isinstance(e, int) or e >= 1:
                    finish(e - 1, 1 - b)
                split(e + 1, half + b, 1 - b)
            copy_x(0)
            split(0, 0, 0)
            for_experts(act, step, NE - 2)
            hidden(NE - 1, 1)
            for e, b in ((NE - 2, 0), (NE - 1, 1)):
                copy_h(e)
                finish(e, b)

        @blk.vector
        def _(dve):
            def copy_x(e):
                dve.wait_ge(s_xt, e + 1)
                nc.vector.tensor_copy(B.xT[:, 512:1024], k.ps[1][:])
                dve.wait_ge(s_xh, e + 1)
                dve.wait_ge(s_xa, e + 1)
                nc.vector.tensor_tensor(x_lo[:], k.ps[0][:, 0:SPLIT * P], x_hi[:].bitcast(F32), ALU.subtract).then_inc(s_xv, 1)

            def split(e, half, b):
                dve.wait_ge(s_wh, e + 1)
                nc.vector.tensor_tensor(w_lo[:], expert_views(k, b)[3][:, 0:SPLIT], w_hi[:].bitcast(F32), ALU.subtract).then_inc(s_wl, 1)

            def hidden(e, b):
                dve.wait_ge(s_e, e + 1)
                ge(dve, s_ht, e - 1)
                dve_hidden(k, B, b, 2 + b, dve, s_hs, 3 * e).then_inc(s_h, 1)

            def finish(e, b):
                dve.wait_ge(s_d, e + 1)
                ge(dve, s_sc, 16 * (e - 1))
                nc.vector.tensor_copy(B.y[b][:, 512:1024], k.ps[6][:]).then_inc(s_yv, 1)

            def step(e, half, b):
                hidden(e, b)
                copy_x(e + 1)
                if not isinstance(e, int) or e >= 1:
                    finish(e - 1, 1 - b)
                split(e + 1, half + b, 1 - b)
            copy_x(0)
            split(0, 0, 0)
            for_experts(dve, step, NE - 2)
            hidden(NE - 1, 1)
            finish(NE - 2, 0)
            finish(NE - 1, 1)


def stage_overflow(k, layer):
    nc = k.nc
    B = MoeBuffers(k)
    le = k.s[:, 5000:5000 + 3 * 64].bitcast(BF16).rearrange("p (t n) -> p t n", t=TILES)
    onesb = k.s[:, 5200:5202].bitcast(BF16)[:, 0:1]
    row = k.s[:, 5210:5211]
    far = k.s[:, 5212:5213]
    with Stage(nc) as ctx:
        s_w, s_le, s_ix, s_si, s_gi, s_xt, s_x, s_gu, s_e, s_hs, s_h, s_ht, s_hc, s_d, s_y, s_v, s_one, s_free = sems(
            nc, ctx, "ov_loaded ov_le ov_idx ov_rows ov_gidx ov_turned ov_xT ov_gate_up ov_exp ov_hsteps ov_h ov_hturned ov_hT ov_down ov_y "
                     "ov_steps ov_ones ov_free")
        s_g, s_sc = k.pool_sems[layer][3:5]
        blk = ctx.enter_context(nc.Block())

        def items(eng, body):
            n = eng.value_load(k.over[0:1, OVER_KEYS:OVER_KEYS + 1], min_val=0, max_val=OVER_KEYS)
            with eng.If(n > 0):
                with eng.Fori(0, n) as i:
                    body(i)
            with eng.Else():
                pass

        def item(eng, i):
            return eng.value_load(k.over[0:1, bass.ds(i, 1)], min_val=0, max_val=2 * NE - 1)

        @blk.sync
        def _(sp):
            def body(i):
                key = item(sp, i)
                sp.wait_ge(s_free, i + 1)
                load_expert(k, sp, layer, key % NE, 0, s_w, s_w)
            items(sp, body)

        @blk.gpsimd
        def _(pool):
            last_tok, last_row = bounds(pool)

            n = pool.value_load(k.over[0:1, OVER_KEYS:OVER_KEYS + 1], min_val=0, max_val=OVER_KEYS)
            pool.sem_inc(s_free, 1)
            for i in range(OVER_KEYS):
                with pool.If(n > i):
                    pool.wait_ge(s_gi, i + 1)
                    gather(k, B.xg[:, 0, :], k.h_d, last_tok, B.gi).then_inc(s_g, 16)
                    pool.wait_ge(s_si, i + 1)
                    pool.wait_ge(s_y, 2 * i + 2)
                    scatter(k, k.y_d, last_row, B.si, B.y[0]).then_inc(s_sc, 16)
                    pool.wait_ge(s_sc, 16 * i + 16)
                    pool.sem_inc(s_free, 1)
                with pool.Else():
                    pass

        @blk.tensor
        def _(pe):
            def body(i):
                pe.wait_ge(s_le, 3 * i + 3)
                for t in range(TILES):
                    m = nc.tensor.matmul(k.ps[7][:, 0:1], le[:, t, :], onesb, start=(t == 0), stop=(t == TILES - 1))
                m.then_inc(s_ix, 1)
                pe.wait_ge(s_g, 16 * i + 16)
                pe_turn_rows(k, B, 0).then_inc(s_xt, 1)
                pe.wait_ge(s_x, 2 * i + 2)
                pe.wait_ge(s_w, 48 * i + 48)
                pe_gate_up(k, B, 0, 2).then_inc(s_gu, 1)
                pe.wait_ge(s_h, i + 1)
                pe_turn_h(k, B, 0).then_inc(s_ht, 1)
                pe.wait_ge(s_hc, i + 1)
                pe_down(k, B, 0).then_inc(s_d, 1)
            items(pe, body)

        @blk.scalar
        def _(act):
            def body(i):
                act.wait_ge(s_xt, i + 1)
                for j in range(2):
                    nc.scalar.copy(B.xT[:, j * 512:(j + 1) * 512], k.ps[j][:]).then_inc(s_x, 1)
                act.wait_ge(s_gu, i + 1)
                nc.scalar.activation(B.ex[0], k.ps[2][:, 0:FD], ACT.Exp, scale=-1.0).then_inc(s_e, 1)
                act.wait_ge(s_ht, i + 1)
                nc.scalar.copy(B.hT, k.ps[4][:, 0:FD]).then_inc(s_hc, 1)
                act.wait_ge(s_d, i + 1)
                for j in range(2):
                    nc.scalar.copy(B.y[0][:, j * 512:(j + 1) * 512], k.ps[5 + j][:]).then_inc(s_y, 1)
            items(act, body)

        @blk.vector
        def _(dve):
            nc.vector.memset(onesb, 1.0).then_inc(s_one, 1)
            dve.wait_ge(s_one, 1)

            def body(i):
                key = item(dve, i)
                e, blk_no = key % NE, key // NE
                dve.wait_ge(s_free, i + 1)
                for t in range(TILES):
                    nc.vector.tensor_scalar(le[:, t, :], k.const[:, bass.ds(C_IOTA + P + blk_no * P, P)], k.incl[:, t, bass.ds(e, 1)], None,
                                            ALU.is_ge).then_inc(s_le, 1)
                first = k.const[:, bass.ds(C_IOTA + P + blk_no * P, 1)]
                nc.vector.tensor_tensor(row, k.bases[:, 0, bass.ds(e, 1)], first, ALU.add).then_inc(s_v, 1)
                dve.wait_ge(s_v, 4 * i + 1)
                nc.vector.tensor_tensor(row, row, k.const[:, C_COL + 1:C_COL + 2], ALU.add).then_inc(s_v, 1)
                dve.wait_ge(s_v, 4 * i + 2)
                nc.vector.tensor_tensor(far, row, k.bases[:, 1, bass.ds(e, 1)], ALU.is_ge).then_inc(s_v, 1)
                dve.wait_ge(s_v, 4 * i + 3)
                nc.vector.scalar_tensor_tensor(row, far, FAR, row, ALU.mult, ALU.add).then_inc(s_v, 1)
                dve.wait_ge(s_v, 4 * i + 4)
                nc.vector.tensor_copy(B.si, row).then_inc(s_si, 1)
                dve.wait_ge(s_ix, i + 1)
                nc.vector.tensor_copy(B.gi, k.ps[7][:, 0:1]).then_inc(s_gi, 1)
                dve.wait_ge(s_e, i + 1)
                dve_hidden(k, B, 0, 2, dve, s_hs, 3 * i).then_inc(s_h, 1)
            items(dve, body)


def stage_combine_norm(k, layer, ahead=None):
    nc, io = k.nc, k.io
    M = NormBuffers(k, 2)
    last = layer == DEPTH - 1
    NB = 8
    buf = k.s[:, 0:NB * D].rearrange("p (b n) -> p b n", b=NB)
    half = TOPK // 2
    diag = k.ring[:, 0:TILES * half * P].rearrange("p (t j n) -> p t j n", t=TILES, j=half)
    order = [(t, j) for t in range(TILES) for j in range(TOPK)]
    turn_banks = ((6, 7), (0, 1), (2, 3))
    with Stage(nc) as ctx:
        s_dg, s_pacc, s_sum = sems(nc, ctx, "diagonals_ready row_added_pe sums_joined")
        s_acc, s_d, s_v, s_p, s_n, s_h, s_g2, s_tr, s_out = sems(
            nc, ctx, "row_added dve_steps var_ready rstd_ready normed h_ready x_scaled turned outputs_stored")
        s_g = k.pool_sems[layer][5:5 + NB]
        blk = ctx.enter_context(nc.Block())

        @blk.sync
        def _(sp):
            if last:
                for t in range(TILES):
                    sp.wait_ge(s_h, t + 1)
                    dst = io["y_prompt"][0] if t == 0 else io["y_sample"][0, (t - 1) * P:t * P, :]
                    sp.dma_start(dst, k.x[:, t, :]).then_inc(s_out, 16)
                sp.wait_ge(s_out, 16 * TILES)
            else:
                sp.wait_ge(s_pacc, TILES * half)
                ahead(sp)

        @blk.gpsimd
        def _(pool):
            last_tok, last_row = bounds(pool)

            def rows(tile):
                for i, (t, j) in enumerate(order):
                    if t == tile:
                        if i >= NB:
                            pool.wait_ge((s_acc, s_pacc)[j % 2], (t - 1) * half + j // 2 + 1)
                        gather(k, buf[:, i % NB, :], k.y_d, last_row, k.slot_u[:, t, j:j + 1]).then_inc(s_g[i % NB], 16)

            rows(0)
            rows(1)
            pool_rstd(k, M, pool, 0, s_v, s_p)
            rows(2)
            pool_rstd(k, M, pool, 1, s_v, s_p)
            if last:
                pool_rstd(k, M, pool, 2, s_v, s_p)
            else:
                pool_affine(k, M, pool, 0, s_n, s_g2)
                pool_rstd(k, M, pool, 2, s_v, s_p)
                pool_affine(k, M, pool, 1, s_n, s_g2)
                pool_affine(k, M, pool, 2, s_n, s_g2)

        @blk.tensor
        def _(pe):
            for t in range(TILES):
                pe.wait_ge(s_dg, t + 1)
                for j in range(half):
                    i = TOPK * t + 2 * j + 1
                    pe.wait_ge(s_g[i % NB], 16 * (i // NB + 1))
                    for c in range(2):
                        m = nc.tensor.matmul(k.ps[2 * t + c][:], diag[:, t, j, :], buf[:, i % NB, c * 512:(c + 1) * 512],
                                             start=(j == 0), stop=(j == half - 1))
                    m.then_inc(s_pacc, 1)
            for t in range(0 if last else TILES):
                if t:
                    pe.wait_ge(s_sum, t)
                pe_turn_tile(k, pe, t, turn_banks[t], s_h, s_tr)

        @blk.scalar
        def _(act):
            for t in range(TILES):
                for j in range(half):
                    m = nc.scalar.mul(diag[:, t, j, :], k.ident, k.w8[:, t, 2 * j + 1:2 * j + 2])
                m.then_inc(s_dg, 1)
            for t in range(0 if last else TILES):
                copy_turned(k, act, t, turn_banks[t], s_tr)

        @blk.vector
        def _(dve):
            st = Steps(dve, s_d)
            st.mark(nc.vector.memset(M.half, -0.5))

            def add_rows(tile):
                for i, (t, j) in enumerate(order):
                    if t == tile and j % 2 == 0:
                        dve.wait_ge(s_g[i % NB], 16 * (i // NB + 1))
                        ge(dve, s_acc, half * t + j // 2)
                        nc.vector.scalar_tensor_tensor(k.cat[:, t, :], buf[:, i % NB, :], k.w8[:, t, j:j + 1], k.cat[:, t, :],
                                                       ALU.mult, ALU.add).then_inc(s_acc, 1)

            def residual(t):
                x, f = k.x[:, t, :], k.cat[:, t, :]
                if t == 0:
                    k.arrived(dve, 3)
                dve.wait_ge(s_acc, half * (t + 1))
                dve.wait_ge(s_pacc, half * (t + 1))
                for c in range(2):
                    m = nc.vector.tensor_tensor(f[:, c * 512:(c + 1) * 512], f[:, c * 512:(c + 1) * 512], k.ps[2 * t + c][:], ALU.add)
                m.then_inc(s_sum, 1)
                dve.wait_ge(s_sum, t + 1)
                st.then(nc.vector.tensor_tensor(f, f, M.T[:, min(t, 1), 0, :], ALU.mult))
                st.then(nc.vector.scalar_tensor_tensor(x, x, ALPHA, f, ALU.mult, ALU.add))
                dve_stats(k, M, st, t, range(2))
                dve_variance(k, M, st, t, s_v)

            def norm(t):
                if not last:
                    dve_norm(k, M, dve, st, t, s_p, s_n, s_h, False)
                    return
                x = k.x[:, t, :]
                dve.wait_ge(s_p, t + 1)
                st.then(nc.vector.tensor_scalar(x, x, M.mv[:, t, 0:1], M.mv[:, t, 1:2], ALU.subtract, ALU.mult))
                st.then(nc.vector.tensor_tensor(x, x, M.gb[:, 0, :], ALU.mult))
                nc.vector.tensor_tensor(x, x, M.gb[:, 1, :], ALU.add).then_inc(s_h, 1)

            for t in range(TILES):
                add_rows(t)
                if t:
                    norm(t - 1)
                residual(t)
            norm(TILES - 1)


def even_mixer(k, e, ahead):
    z = k.z[:].rearrange("p (t n) -> p t n", t=TILES)
    stage_project(k, k.io["mla_ret_w_in"][e], EVEN_IN, lambda t, c, n: z[:, t, c:c + n])
    R, S = k.ring, k.s
    m = k.mla = {}
    m["kT"] = R[0:QK, 0:4096].rearrange("p (h n) -> p h n", h=HEADS)
    m["v"] = R[:, 4096:6144].rearrange("p (t n) -> p t n", t=4)
    m["qT"] = R[0:QK, 6144:9216].rearrange("p (t h n) -> p t h n", t=TILES, h=HEADS)
    m["q"] = R[:, 9216:11520].rearrange("p (t n) -> p t n", t=TILES)
    m["qn"] = R[:, 11520:12288].rearrange("p (t n) -> p t n", t=TILES)
    o = 3200
    for name, n in (("qnT", 768), ("ckv", 512), ("kpe", 384), ("ckvT", 512), ("kpeT", 512), ("wuq", 1536), ("wuk", 512), ("wuv", 512),
                    ("qg", Q_RANK), ("kvg", KV_RANK), ("junk", Q_RANK), ("ss", 6), ("rstd", 6), ("half", 6)):
        m[name] = S[:, o:o + n]
        o += n + n % 2
    m["qnT"] = m["qnT"].rearrange("p (k n) -> p k n", k=2)
    m["ckv"] = m["ckv"].rearrange("p (t n) -> p t n", t=4)
    m["kpe"] = m["kpe"].rearrange("p (t n) -> p t n", t=4)
    m["wuq"] = m["wuq"].rearrange("p (k n) -> p k n", k=2)
    stage_mla_norm(k, e)
    stage_mla_keys(k, e)
    stage_turn_heads(k, [([m["q"][:, t, (4 * g + j) * QK:(4 * g + j + 1) * QK] for j in range(4)],
                          [(0, QK, m["qT"][:, t, 4 * g:4 * g + 4, :])]) for t in range(TILES) for g in range(2)])
    groups = []
    for t in range(TILES):
        for g in range(HEADS // GROUP):
            hs = range(GROUP * g, GROUP * (g + 1))
            lo, hi = (0, 1) if t == 0 else (1, 4)
            groups.append(dict(n=(hi - lo) * P, q=[m["qT"][:, t, h, :] for h in hs], keys=[m["kT"][:, h, lo * P:hi * P] for h in hs],
                               v=[[m["v"][:, i, h * VD:(h + 1) * VD] for i in range(lo, hi)] for h in hs],
                               out=k.cat[:, t, GROUP * g * VD:GROUP * (g + 1) * VD].rearrange("p (h n) -> p h n", h=GROUP)))
    assert len(groups) + 2 == RH
    stage_attention(k, groups, QK ** -0.5, load_retention(k, e), lambda act, st, i: retention_decays(k, act, st, i))
    stage_turn_heads(k, retention_jobs(k))
    stage_retention(k, e, ahead)


def odd_mixer(k, o, ahead):
    z = k.zo = k.z[:, 0:TILES * ODD_IN].rearrange("p (t n) -> p t n", t=TILES)
    stage_project(k, k.io["swa_w_in"][o], ODD_IN, lambda t, c, n: z[:, t, c:c + n])
    R, S = k.ring, k.s
    o_ = 10240
    k.kpad, k.kctx, k.vctx, k.sink = S[:, o_:o_ + SD], S[:, o_ + 64:o_ + 320], S[:, o_ + 320:o_ + 576], S[:, o_ + 576:o_ + 592]
    qT = R[:, 0:3072].rearrange("p (t h n) -> p t h n", t=TILES, h=SH // 2)
    kT = R[:, 3072:7168].rearrange("p (v h j n) -> p v h j n", v=2, h=SKV, j=4)
    k.key_zeros = (kT[SD:P, 0], kT[0:SD, 1])
    stage_swa_prep(k, o)
    jobs = [([z[:, t, (4 * g + j) * P:(4 * g + j + 1) * P] for j in range(4)], [(0, P, qT[:, t, 4 * g:4 * g + 4, :])])
            for t in range(TILES) for g in range(2)]
    for w in range(-1, SKV):
        a = SQ_DIM + w * SD
        srcs = [z[:, t, a:a + P] for t in range(TILES)] + [S[:, o_ + 64 + w * SD:o_ + 64 + w * SD + P]]
        parts = [(0, SD, kT[0:SD, 0, w])] if w >= 0 else []
        if w + 1 < SKV:
            parts.append((SD, P, kT[SD:P, 1, w + 1]))
        jobs.append((srcs, parts))
    stage_turn_heads(k, jobs)
    groups = []
    for t in range(TILES):
        for g in range(SKV):
            lo, hi = (0, 1) if t == 0 else (1, 4)
            a = SQ_DIM + SKV_DIM + g * SD
            vs = [z[:, i, a:a + SD] for i in range(TILES)] + [k.vctx[:, g * SD:(g + 1) * SD]]
            groups.append(dict(n=(hi - lo) * P, q=[qT[:, t, (GROUP * g + j) // 2, :] for j in range(GROUP)],
                               keys=[kT[:, j % 2, g, lo:hi, :].rearrange("p j n -> p (j n)") for j in range(GROUP)],
                               v=[vs[lo:hi]] * GROUP,
                               out=k.cat[:, t, GROUP * g * SD:GROUP * (g + 1) * SD].rearrange("p (h n) -> p h n", h=GROUP),
                               sink=k.sink[:, GROUP * g:GROUP * (g + 1)], mask=k.c(C_MASK + (t - 1) * TOK, TOK) if t else None))
    stage_attention(k, groups, SD ** -0.5, ahead)


def backbone(nc, io):
    def w_in(layer):
        return io[("mla_ret_w_in", "swa_w_in")[layer % 2]][layer // 2]

    with ExitStack() as ctx:
        k = Kernel(nc, ctx, io)
        stage_setup(k)
        stage_mod(k)
        k.work_memory(ctx)
        for layer in range(DEPTH):
            w_out = io[("even_w_out", "swa_w_out")[layer % 2]][layer // 2]
            if layer == 0:
                stage_modulate(k, layer, first_chunks(k, w_in(0)))
            (even_mixer, odd_mixer)[layer % 2](k, layer // 2, out_chunk(k, w_out, 0))
            stage_transpose(k, k.cat, out_chunk(k, w_out, 1))
            stage_project_norm(k, w_out, layer)
            stage_route(k, layer)
            stage_experts(k, layer)
            stage_overflow(k, layer)
            stage_combine_norm(k, layer, None if layer == DEPTH - 1 else first_chunks(k, w_in(layer + 1)))


_OUTS = [("y_prompt", (1, P, D)), ("y_sample", (1, 2 * P, D)), ("new_mla_ckv", (1, 1, P, KV_RANK)), ("new_mla_kpe", (1, 1, P, ROPE)),
         ("new_ret_fwd", (1, 1, RH, RD, RD)), ("new_ret_bwd", (1, 1, RH, RD, RD)), ("new_swa_k", (1, 1, P, SKV, SD)), ("new_swa_v", (1, 1, P, SKV, SD))]


def kernel(**inputs):
    import numpy as _np
    import concourse.bacc as _bacc
    from concourse import mybir as _mybir
    from concourse.bass_utils import run_bass_kernel_spmd as _run

    nc = _bacc.Bacc("TRN2", target_bir_lowering=False, num_devices=1)
    arrays, io = {}, {}
    for name, value in [*inputs.items(), ("tables", shape_tables())]:
        a = _np.ascontiguousarray(value)
        if name == "c_ctx":
            a = a.reshape(-1)
        arrays[f"in_{name}"] = a
        io[name] = nc.dram_tensor(f"in_{name}", a.shape, _mybir.dt.from_np(a.dtype), kind="ExternalInput").ap()
    for name, shape in _OUTS:
        io[name] = nc.dram_tensor(f"out_{name}", shape, _mybir.dt.float32, kind="ExternalOutput").ap()
    backbone(nc, io)
    r = _run(nc, [arrays], core_ids=[0])
    return tuple(r.results[0][f"out_{name}"] for name, _ in _OUTS)
```
